# Optimizing a Trainium2 kernel written in Bass

```python
import jax, jax.numpy as jnp
from jax import lax
import numpy as np

"""Hybrid streaming-encoder trunk: one post-norm (DeepNorm) layer.

Input  x: (BATCH, SEQ, D_MODEL) float32.  Output: (BATCH, SEQ, D_MODEL).
Entry LayerNorm, then per layer:
  p  = h @ W_in                       single combined projection, columns split
                                      between head group A (RWKV-7) and B (GLA)
  y  = [RWKV7_A(p_A) ; GLA_B(p_B)] @ W_out
  h <- LN(alpha * h + y)
  h <- LN(alpha * h + PEER(h))        product-key single-neuron experts
All mixers are forward-in-time (hence chunk-causal for CHUNK = 64).
"""

D_MODEL = 1024
BATCH = 1
SEQ = 1024
DEPTH = 1

CHUNK = 64
LN_EPS = 1e-5
ALPHA = (2.0 * DEPTH) ** 0.25
BETA = (8.0 * DEPTH) ** -0.25

A_HEAD = 64
A_WIDTH = D_MODEL // 2
A_HEADS = A_WIDTH // A_HEAD
A_DECAY_LORA = 64
A_ICLR_LORA = 64
A_GATE_LORA = 128
A_GN_EPS = 64e-5
A_IN = 3 * A_WIDTH + A_DECAY_LORA + A_ICLR_LORA + A_GATE_LORA
A_SPLITS = (A_WIDTH, 2 * A_WIDTH, 3 * A_WIDTH, 3 * A_WIDTH + A_DECAY_LORA,
            3 * A_WIDTH + A_DECAY_LORA + A_ICLR_LORA)

B_WIDTH = D_MODEL // 2
B_HEADS = 4
B_DV = B_WIDTH // B_HEADS
B_DK = B_DV // 2
B_WIDTH_K = B_HEADS * B_DK
B_GATE_LORA = 16
B_GATE_NORM = 16.0
B_CONV = 4
B_RMS_EPS = 1e-5
B_QKV = 2 * B_WIDTH_K + B_WIDTH
B_IN = B_QKV + B_GATE_LORA + B_WIDTH
B_SPLITS = (B_QKV, B_QKV + B_GATE_LORA)

D_MIX = A_WIDTH + B_WIDTH
IN_COLS = A_IN + B_IN

P_HEADS = 8
P_KEYS = 128
P_EXPERTS = P_KEYS * P_KEYS
P_HALF = 128
P_TOPK = 16
P_TOKEN_BLOCK = 128

kernel_name = "hymba_rwkv7_gla_peer_deepnorm"

def layer_norm(x, g, b):
    xf = x.astype(jnp.float32)
    mu = jnp.mean(xf, axis=-1, keepdims=True)
    var = jnp.mean(jnp.square(xf - mu), axis=-1, keepdims=True)
    return ((xf - mu) * lax.rsqrt(var + LN_EPS) * g + b).astype(x.dtype)

def token_shift(p, mu):
    prev = jnp.pad(p, ((0, 0), (1, 0), (0, 0)))[:, :-1]
    return p + (prev - p) * mu

def causal_conv(p, w):
    T = p.shape[1]
    pad = jnp.pad(p, ((0, 0), (B_CONV - 1, 0), (0, 0)))
    return sum(w[j] * pad[:, j:j + T] for j in range(B_CONV))

def rwkv7_scan(r, decay, k, v, kk, b):
    Bn, _, H, N = r.shape

    def step(S, inp):
        r_t, w_t, k_t, v_t, kk_t, b_t = inp
        sa = jnp.einsum('bhvk,bhk->bhv', S, -kk_t)
        S = S * w_t[:, :, None, :] + sa[..., None] * b_t[:, :, None, :] + v_t[..., None] * k_t[:, :, None, :]
        return S, jnp.einsum('bhvk,bhk->bhv', S, r_t)

    xs = tuple(jnp.moveaxis(t, 1, 0) for t in (r, decay, k, v, kk, b))
    S0 = jnp.zeros((Bn, H, N, N), jnp.float32)
    _, y = lax.scan(step, S0, xs)
    return jnp.moveaxis(y, 0, 1)

def rwkv7_group(p, mu, w0, w2, a0, a2, g2, k_k, k_a, r_k, gn_g, gn_b):
    Bn, T, _ = p.shape
    p = token_shift(p, mu)
    r, k, v, wd, ad, gd = jnp.split(p, A_SPLITS, axis=-1)
    w = -jax.nn.softplus(-(w0 + jnp.tanh(wd) @ w2)) - 0.5
    a = jax.nn.sigmoid(a0 + ad @ a2)
    g = jax.nn.sigmoid(gd) @ g2

    def hd(t):
        return t.astype(jnp.float32).reshape(Bn, T, A_HEADS, A_HEAD)

    kk = hd(k * k_k)
    kk = kk / jnp.maximum(jnp.sqrt(jnp.sum(kk * kk, axis=-1, keepdims=True)), 1e-12)
    a_h = hd(a)
    k_h = hd(k * (1 + (a - 1) * k_a))
    r_h, v_h = hd(r), hd(v)
    decay = jnp.exp(-jnp.exp(hd(w)))
    y = rwkv7_scan(r_h, decay, k_h, v_h, kk, kk * a_h)
    mean = jnp.mean(y, axis=-1, keepdims=True)
    var = jnp.mean(jnp.square(y - mean), axis=-1, keepdims=True)
    y = ((y - mean) * lax.rsqrt(var + A_GN_EPS)).reshape(Bn, T, A_WIDTH) * gn_g + gn_b
    bonus = jnp.sum(r_h * k_h * r_k, axis=-1, keepdims=True) * v_h
    y = y + bonus.reshape(Bn, T, A_WIDTH)
    return (y * g).astype(p.dtype)

def gla_chunked(q, k, v, gk):
    Bn, T, H, DK = q.shape
    n = T // CHUNK

    def to_chunks(t):
        return jnp.moveaxis(t.reshape(Bn, n, CHUNK, H, t.shape[-1]), 1, 0)

    causal = jnp.tril(jnp.ones((CHUNK, CHUNK), bool))[None, :, :, None, None]

    def step(S, inp):
        qc, kc, vc, gc = inp
        G = jnp.cumsum(gc, axis=1)
        o_inter = jnp.einsum('bihd,bhdv->bihv', qc * jnp.exp(G), S)
        diff = G[:, :, None] - G[:, None]
        dec = jnp.exp(jnp.where(causal, diff, -jnp.inf))
        A = jnp.einsum('bihd,bjhd,bijhd->bhij', qc, kc, dec)
        o_intra = jnp.einsum('bhij,bjhv->bihv', A, vc)
        G_last = G[:, -1]
        k_dec = kc * jnp.exp(G_last[:, None] - G)
        S = S * jnp.exp(G_last)[..., None] + jnp.einsum('bjhd,bjhv->bhdv', k_dec, vc)
        return S, o_inter + o_intra

    S0 = jnp.zeros((Bn, H, DK, v.shape[-1]), jnp.float32)
    _, o = lax.scan(step, S0, (to_chunks(q), to_chunks(k), to_chunks(v), to_chunks(gk)))
    return jnp.moveaxis(o, 0, 1).reshape(Bn, T, H, v.shape[-1])

def gla_group(p, conv_w, gk_w2, gk_b, norm_g):
    Bn, T, _ = p.shape
    qkv, gkd, g = jnp.split(p, B_SPLITS, axis=-1)
    qkv = jax.nn.silu(causal_conv(qkv, conv_w))
    q, k, v = jnp.split(qkv, (B_WIDTH_K, 2 * B_WIDTH_K), axis=-1)
    gk = jax.nn.log_sigmoid((gkd @ gk_w2 + gk_b).astype(jnp.float32)) / B_GATE_NORM

    def hd(t, d):
        return t.astype(jnp.float32).reshape(Bn, T, B_HEADS, d)

    o = gla_chunked(hd(q, B_DK) * (B_DK ** -0.5), hd(k, B_DK), hd(v, B_DV), hd(gk, B_DK))
    o = o * lax.rsqrt(jnp.mean(o * o, axis=-1, keepdims=True) + B_RMS_EPS) * norm_g
    o = o * jax.nn.silu(hd(g, B_DV))
    return o.reshape(Bn, T, B_WIDTH).astype(p.dtype)

def peer(h, w_q, sub_keys, u_tab, v_tab):
    Bn, T, D = h.shape
    n_tok = Bn * T
    tok = h.reshape(n_tok, D)
    q = (tok @ w_q).reshape(n_tok, P_HEADS, 2, P_HALF).astype(jnp.float32)
    s = jnp.einsum('nhpc,hpkc->nhpk', q, sub_keys.astype(jnp.float32))
    sv, si = lax.top_k(s, P_TOPK)
    cand = sv[:, :, 0, :, None] + sv[:, :, 1, None, :]
    cv, ci = lax.top_k(cand.reshape(n_tok, P_HEADS, P_TOPK * P_TOPK), P_TOPK)
    e1 = jnp.take_along_axis(si[:, :, 0], ci // P_TOPK, axis=-1)
    e2 = jnp.take_along_axis(si[:, :, 1], ci % P_TOPK, axis=-1)
    ids = (e1 * P_KEYS + e2).reshape(n_tok // P_TOKEN_BLOCK, P_TOKEN_BLOCK, P_HEADS * P_TOPK)
    gates = jax.nn.softmax(cv, axis=-1).reshape(n_tok // P_TOKEN_BLOCK, P_TOKEN_BLOCK, P_HEADS * P_TOPK)
    xb = tok.reshape(n_tok // P_TOKEN_BLOCK, P_TOKEN_BLOCK, D)

    def block(args):
        x_b, id_b, g_b = args
        u = u_tab[id_b]
        act = jax.nn.gelu(jnp.einsum('td,tkd->tk', x_b, u), approximate=False) * g_b
        return jnp.einsum('tk,tkd->td', act, v_tab[id_b]).astype(h.dtype)

    out = lax.map(block, (xb, ids, gates))
    return out.reshape(Bn, T, D)

def setup_inputs(seed: int = 0) -> dict:
    key = jax.random.key(seed)
    ks = iter(jax.random.split(key, 40))
    L = DEPTH

    def nrm(shape, scale):
        return jax.random.normal(next(ks), shape, jnp.float32) * scale

    def gain(shape):
        return 1.0 + nrm(shape, 0.02)

    def uni(shape, lo, hi):
        return jax.random.uniform(next(ks), shape, jnp.float32, lo, hi)

    return {
        'x': nrm((BATCH, SEQ, D_MODEL), 1.0),
        'ln_in_g': gain((D_MODEL,)),
        'ln_in_b': nrm((D_MODEL,), 0.02),
        'w_in': nrm((L, D_MODEL, IN_COLS), D_MODEL ** -0.5),
        'a_mu': uni((L, A_IN), 0.0, 1.0),
        'a_w0': uni((L, A_WIDTH), -5.0, -0.5),
        'a_w2': nrm((L, A_DECAY_LORA, A_WIDTH), 0.5 * A_DECAY_LORA ** -0.5),
        'a_a0': nrm((L, A_WIDTH), 0.1),
        'a_a2': nrm((L, A_ICLR_LORA, A_WIDTH), A_ICLR_LORA ** -0.5),
        'a_g2': nrm((L, A_GATE_LORA, A_WIDTH), A_GATE_LORA ** -0.5),
        'a_k_k': 0.85 + nrm((L, A_WIDTH), 0.02),
        'a_k_a': gain((L, A_WIDTH)),
        'a_r_k': nrm((L, A_HEADS, A_HEAD), 0.1),
        'a_gn_g': gain((L, A_WIDTH)),
        'a_gn_b': nrm((L, A_WIDTH), 0.02),
        'b_conv': nrm((L, B_CONV, B_QKV), B_CONV ** -0.5),
        'b_gk_w2': nrm((L, B_GATE_LORA, B_WIDTH_K), B_GATE_LORA ** -0.5),
        'b_gk_b': nrm((L, B_WIDTH_K), 0.1),
        'b_norm_g': gain((L, B_DV)),
        'w_out': nrm((L, D_MIX, D_MODEL), BETA * D_MIX ** -0.5),
        'ln1_g': gain((L, D_MODEL)),
        'ln1_b': nrm((L, D_MODEL), 0.02),
        'p_wq': nrm((L, D_MODEL, P_HEADS * 2 * P_HALF), D_MODEL ** -0.5),
        'p_keys': nrm((L, P_HEADS, 2, P_KEYS, P_HALF), P_HALF ** -0.5),
        'p_u': nrm((L, P_EXPERTS, D_MODEL), D_MODEL ** -0.5),
        'p_v': nrm((L, P_EXPERTS, D_MODEL), BETA),
        'ln2_g': gain((L, D_MODEL)),
        'ln2_b': nrm((L, D_MODEL), 0.02),
    }

def reference(x, ln_in_g, ln_in_b, w_in, a_mu, a_w0, a_w2, a_a0, a_a2, a_g2, a_k_k, a_k_a,
              a_r_k, a_gn_g, a_gn_b, b_conv, b_gk_w2, b_gk_b, b_norm_g, w_out, ln1_g, ln1_b,
              p_wq, p_keys, p_u, p_v, ln2_g, ln2_b):
    h = layer_norm(x, ln_in_g, ln_in_b)
    for l in range(DEPTH):
        p = h @ w_in[l]
        pa, pb = jnp.split(p, (A_IN,), axis=-1)
        ya = rwkv7_group(pa, a_mu[l], a_w0[l], a_w2[l], a_a0[l], a_a2[l], a_g2[l],
                         a_k_k[l], a_k_a[l], a_r_k[l], a_gn_g[l], a_gn_b[l])
        yb = gla_group(pb, b_conv[l], b_gk_w2[l], b_gk_b[l], b_norm_g[l])
        y = jnp.concatenate([ya, yb], axis=-1) @ w_out[l]
        h = layer_norm(ALPHA * h + y, ln1_g[l], ln1_b[l])
        f = peer(h, p_wq[l], p_keys[l], p_u[l], p_v[l])
        h = layer_norm(ALPHA * h + f, ln2_g[l], ln2_b[l])
    return h


_drawn_inputs = setup_inputs


def setup_inputs(seed=0):
    import zlib

    import numpy as np

    out = dict(_drawn_inputs(seed))
    spreads = {}
    factors = {'a_w2': 2.798,
     'a_k_k': 3.953,
     'a_k_a': 3.241,
     'a_gn_g': 3.455,
     'a_gn_b': 3.475,
     'b_gk_b': 3.258,
     'b_norm_g': 3.452,
     'ln2_g': 2.796,
     'ln2_b': 3.117}
    for name, (base, spread) in spreads.items():
        noise = np.random.default_rng([zlib.crc32(name.encode()), seed]).standard_normal(out[name].shape)
        drawn = base * np.exp(spread * noise) if base else spread * noise
        out[name] = __import__('jax').numpy.asarray(drawn.astype(out[name].dtype))
    for name, factor in factors.items():
        out[name] = (out[name] * factor).astype(out[name].dtype)
    return out
```

```python
from collections import namedtuple
from contextlib import ExitStack

import concourse.bass as bass
from concourse import mybir

F32 = mybir.dt.float32
U32 = mybir.dt.uint32
ALU = mybir.AluOpType
ACT = mybir.ActivationFunctionType
AX = mybir.AxisListType

P = 128
T = 1024
D = 1024
ND = D // P
BT = 128
NBLK = T // BT
C = 64
NC2 = BT // C
HP = 4
GH = 4
NCH = 27
PADC = 3
PW = T + PADC
PRW = BT + PADC
CR, CK, CV, CWA, CGD, CQB, CKB, CVB, CGK, CGB = 0, 4, 8, 12, 13, 14, 16, 18, 22, 23
NA = 14
NQKV = 8
EPS = 1e-5
GN_EPS = 64e-5
ALPHA = 2.0 ** 0.25
E05 = 0.6065306597126334
GMAX = 16.0 * 60.0
PH = 8
TOPK = 16
NKEY = 128
NU = 4
NV = 4
ND4 = 4
NEG = -3.0e38
NINIT = 9
NIDS = 21

VMU, VW0, VA0, VKK, VKA, VRK, VGG, VGB, VCV, VGKB, VNG, NVEC = 0, 14, 18, 22, 26, 30, 34, 38, 42, 74, 76, 77
CID, CBO, CMG, CML, CM0T, CI64, CRS, CIO, NCST = 0, 128, 256, 384, 768, 832, 896, 1408, 1424

SIGNALS = """
x_in par_in keys_in lnin_in zpad_out stat_mv std_ok rstd_ok z_ok zg_ok h_ok htr_ok hev_ok h_out
proj_mm proj_ev p_stored
praw_in hin_in credits
shift_ok conv_ok th_ok sgd_ok z_mm a_mm g_mm sig_ok a_ok g_ok csum_ok egp_ok en_ok
kkr_ok sq_ok ss_mm ssm_ok ssq_ok rk_ok bs_mm bon_ok rkr_ok kbb_ok
gkx_mm xg_ok xa_ok xl_ok gsig_ok silu_ok gsil_ok
vtr_mm v_ev kbt_mm kbt_ev gram_mm gram_ev nt_mm ntl_ok tt_ok t_ok zz_mm zz_ev ttm_mm tm_mm
wmm w_ev umm u_ev y_mm y_ev st_mm sa_ok s_ok
ymean_mm yc_ok ysq_ok yvar_mm ystd_ok yn_ok
gd1_ok gcl_ok gex_ok gq1_ok gqx_ok gq_ok gi_ok gqi_ok gl1_ok gl_ok gkd_ok gec_ok
gvt_mm gvt_ev gkt_mm gkt_ev ga_mm ga_ev go_mm go_ev gs_mm gs_ok
osq_ok orms_mm ostd_ok ymixb_ok
op_mm hy_ok mv1_ok sd1_ok h1_ok h1t_mm h1t_ev
q_mm q_ev sc_mm sc_ev
tk_ok ids_ok ge_ok
cur_ok u_done gelu_ok act_ok diag_ok v_done fy_ok mv2_ok sd2_ok fo_ok out_done mix norm1 norm2 stood
""".split()
MIX = {n: i + 1 for i, n in enumerate("""
dif_ok difm_ok rin_ok kkn_ok kf1_ok kf_ok kb1_ok kx_ok rk1_ok tt0_ok gk_ok cg_ok yrs_ok yn2_ok yn3_ok yn4_ok ors_ok on_ok on2_ok
""".split())}
NMIX = len(MIX)


def w(eng, sem, b, k=1, n=1):
    eng.wait_ge(sem, b * n + k)


def named(**fields):
    return namedtuple("Named", fields)(**fields)


def hybrid_layer(nc, x, w_in, vec, cst, w2a2, g2, gkw2, lnrows, w_out, wq, keys, u_tab, v_tab, out):
    p_dram = nc.dram_tensor("p_dram", [NCH, P, PW], F32, kind="Internal").ap()
    h_dram = nc.dram_tensor("h_dram", [T, D], F32, kind="Internal").ap()
    with ExitStack() as ctx:
        sem = lambda n: ctx.enter_context(nc.semaphore(n))
        sems = lambda n, count: [sem(f"{n}{i}") for i in range(count)]
        s = named(w_in3=sems("w_in3_", 3), p_out3=sems("p_out3_", 3), u_in=sems("u_in", NU), v_in=sems("v_in", NV),
                  wo_b=sem("wo_b"), wq_b=sems("wq_b", 2), **{n: sem(n) for n in SIGNALS})
        psums = [ctx.enter_context(nc.psum_tensor(f"bank{i}", [P, 512], F32)) for i in range(8)]

        def sbin(stack):
            return lambda n, *shape, dt=F32: stack.enter_context(nc.sbuf_tensor(n, list(shape), dt))
        sb = sbin(ctx)
        k = named(vec=sb("vecs", P, NVEC), cst=sb("csts", P, NCST), w2a2=sb("w2a2s", P, 512),
                            g2=sb("g2s", P, 512), gkw2=sb("gkw2s", 16, 256), ln=sb("lns", P, 4, D),
                            keys=sb("keyss", P, 2 * PH, NKEY), omka=sb("omka", P, HP), eps=sb("epss", P, 3),
                            zero=sb("zero3", P, 4), ones=sb("ones", P, P))
        dram = named(x=x, w_in=w_in, vec=vec, cst=cst, w2a2=w2a2, g2=g2, gkw2=gkw2, lnrows=lnrows,
                               w_out=w_out, wq=wq, keys=keys, u=u_tab, v=v_tab, out=out, p=p_dram, h=h_dram)
        with ExitStack() as first:
            entry(nc, first, sbin(first), s, k, dram, psums)
        with ExitStack() as second:
            blocks(nc, second, sbin(second), s, k, dram, psums)


def entry(nc, ctx, sb, s, k, dram, ps):
    NT = T // P
    xs = sb("xs", P, NT, D)
    hT = sb("hT", P, ND, T)
    hs = sb("hs", P, 2, D)
    zs = sb("zs", P, 2, D)
    lni = sb("lni", P, 2, D)
    wb = [sb(f"wb{i}", P, ND, P) for i in range(3)]
    pe_out = [sb(f"pout{i}", P, T) for i in range(3)]
    st = sb("lst", P, 12)
    mv = sb("lmv", P, 2)
    sd = sb("lsd", P, 1)
    rs = sb("lrs", P, 1)
    hb = sb("hbuf", P, D)
    block = ctx.enter_context(nc.Block())

    @block.sync
    def _(sp):
        sp.dma_start(xs[:, :, :], dram.x.rearrange("(n p) d -> p n d", p=P)).then_inc(s.x_in, 16)
        for i in range(2):
            sp.dma_start(lni[:, i, :], dram.lnrows[i:i + 1, :].to_broadcast([P, D])).then_inc(s.lnin_in, 16)
        for dst, src in ((k.vec[:, :], dram.vec), (k.cst[:, :], dram.cst), (k.w2a2[:, :], dram.w2a2),
                         (k.g2[:, :], dram.g2), (k.gkw2[:, :], dram.gkw2)):
            sp.dma_start(dst, src).then_inc(s.par_in, 16)
        for i in range(3):
            sp.dma_start(wb[i][:, :, :], dram.w_in[i]).then_inc(s.w_in3[i], 16)
        with sp.Fori(0, NCH // 3 - 1) as i:
            for j in range(3):
                sp.wait_ge(s.proj_mm, i * 3 + j + 1)
                sp.dma_start(wb[j][:, :, :], dram.w_in[bass.ds(i * 3 + j + 3, 1)].rearrange("o p d c -> (o p) d c")).then_inc(s.w_in3[j], 16)
        sp.dma_start(k.keys[:, :, :], dram.keys).then_inc(s.keys_in, 16)
        for i in range(4):
            sp.dma_start(k.ln[:, i, :], dram.lnrows[i + 2:i + 3, :].to_broadcast([P, D])).then_inc(s.keys_in, 16)

    @block.scalar
    def _(act):
        act.wait_ge(s.credits, 4)
        with nc.allow_non_contiguous_dma(reason="three zero tokens in front of every channel"):
            act.dma_start(dram.p[:, :, 0:PADC].rearrange("c p t -> p c t"), k.zero[:, 0:3].unsqueeze(1).to_broadcast([P, NCH, PADC])).then_inc(s.zpad_out, 16)
        act.wait_ge(s.zpad_out, 16)
        with act.Fori(0, NT) as n:
            act.wait_ge(s.stat_mv, n + 1)
            act.activation(sd[:, :], mv[:, 1:2], ACT.Sqrt, bias=k.eps[:, 0:1]).then_inc(s.std_ok, 1)
            for j in range(2):
                act.wait_ge(s.htr_ok, n * 2 + j + 1)
                act.activation(hT[:, 4 * j:4 * j + 4, bass.ds(n * P, P)], ps[j][:, :].rearrange("p (d t) -> p d t", d=4), ACT.Copy).then_inc(s.hev_ok, 1)
            act.wait_ge(s.h_ok, n + 1)
            act.dma_start(dram.h[bass.ds(n * P, P), :], hb[:, :]).then_inc(s.h_out, 16)
        act.wait_ge(s.h_out, 16 * NT)
        with act.Fori(0, NCH // 3) as i:
            for j in range(3):
                act.wait_ge(s.proj_mm, i * 3 + j + 1)
                act.wait_ge(s.p_out3[j], i * 16)
                act.activation(pe_out[j][:, 0:512], ps[2 * j][:, :], ACT.Copy).then_inc(s.proj_ev, 1)
                act.wait_ge(s.p_stored, i * 3 + j + 1)
                act.wait_ge(s.proj_ev, i * 3 + j + 1)
                act.dma_start(dram.p[bass.ds(i * 3 + j, 1), :, PADC:PW].rearrange("o p t -> (o p) t"), pe_out[j][:, :]).then_inc(s.p_out3[j], 16)
        for j in range(3):
            act.wait_ge(s.p_out3[j], 16 * (NCH // 3))

    @block.vector
    def _(dve):
        dve.memset(k.eps[:, 0:1], EPS).then_inc(s.credits, 1)
        dve.memset(k.eps[:, 1:2], GN_EPS).then_inc(s.credits, 1)
        dve.memset(k.eps[:, 2:3], 0.0).then_inc(s.credits, 1)
        dve.memset(k.zero[:, :], 0.0).then_inc(s.credits, 1)
        dve.wait_ge(s.x_in, 16)
        dve.wait_ge(s.lnin_in, 32)
        with dve.Fori(0, NT) as n:
            for j in range(2):
                dve.bn_stats(st[:, 6 * j:6 * j + 6], xs[:, bass.ds(n, 1), 512 * j:512 * j + 512]).then_inc(s.z_ok, 1)
            dve.wait_ge(s.z_ok, n * 3 + 2)
            dve.sem_inc(s.stood, 1)
            dve.bn_aggr(mv[:, :], st[:, :]).then_inc(s.stat_mv, 1)
            dve.wait_ge(s.std_ok, n + 1)
            dve.reciprocal(rs[:, :], sd[:, :]).then_inc(s.rstd_ok, 1)
            dve.wait_ge(s.rstd_ok, n + 1)
            dve.tensor_scalar(zs[:, 0, :], xs[:, bass.ds(n, 1), :], mv[:, 0:1], rs[:, :], ALU.subtract, ALU.mult).then_inc(s.z_ok, 1)
            dve.wait_ge(s.z_ok, n * 3 + 3)
            dve.tensor_tensor(zs[:, 1, :], zs[:, 0, :], lni[:, 0, :], ALU.mult).then_inc(s.zg_ok, 1)
            dve.wait_ge(s.zg_ok, n + 1)
            dve.wait_ge(s.h_out, n * 16)
            dve.wait_ge(s.htr_ok, n * 2)
            dve.tensor_tensor(hb[:, :], zs[:, 1, :], lni[:, 1, :], ALU.add).then_inc(s.h_ok, 1)
        with dve.Fori(0, NCH // 3) as i:
            for j in range(3):
                dve.wait_ge(s.proj_mm, i * 3 + j + 1)
                dve.wait_ge(s.p_out3[j], i * 16)
                dve.tensor_copy(pe_out[j][:, 512:1024], ps[2 * j + 1][:, :]).then_inc(s.p_stored, 1)

    @block.tensor
    def _(pe):
        pe.wait_ge(s.par_in, 80)
        with pe.Fori(0, NT) as n:
            pe.wait_ge(s.h_ok, n + 1)
            for j in range(2):
                pe.wait_ge(s.hev_ok, n * 2)
                for d in range(4):
                    ins = pe.transpose(ps[j][:, d * P:d * P + P], hb[:, (4 * j + d) * P:(4 * j + d) * P + P], k.cst[:, CID:CID + P])
                ins.then_inc(s.htr_ok, 1)
        pe.wait_ge(s.hev_ok, 2 * NT)
        with pe.Fori(0, NCH // 3) as i:
            for j in range(3):
                pe.wait_ge(s.w_in3[j], i * 16 + 16)
                pe.wait_ge(s.proj_ev, i * 3)
                pe.wait_ge(s.p_stored, i * 3)
                for half in range(2):
                    for d in range(ND):
                        ins = pe.matmul(ps[2 * j + half][:, :], wb[j][:, d, :], hT[:, d, half * 512:half * 512 + 512], start=(d == 0), stop=(d == ND - 1))
                ins.then_inc(s.proj_mm, 1)


def blocks(nc, ctx, sb, s, k, dram, ps):
    cst, vec = k.cst, k.vec
    F = [ps[0], ps[1]]
    A, B, Cb, Db, Eb, Fb = ps[2:8]

    praw = sb("praw", P, NCH, PRW)
    sh = sb("sh", P, NA, BT)
    cv = sb("cv", P, NQKV, BT)
    h1 = sb("h1", P, D)
    h1T = sb("h1T", P, ND, BT)
    wo = sb("wo", P, ND, 256)
    wqb = [sb(f"wqb{i}", P, ND, P) for i in range(2)]
    ymix = sb("ymix", P, 2 * HP, BT)
    RK = sb("RK", P, 2, HP * NC2, 2, C)
    R2 = sb("R2", P, HP * NC2 * 2 * C)
    KB = R2[:, :].rearrange("p (q c s t) -> p q c s t", q=HP, c=NC2, s=2)
    th = sb("th", C, BT)
    sgd = sb("sgd", P, BT)
    sg = sb("sg", P, HP, BT)
    aa = sb("aa", P, HP, BT)
    gg = sb("gg", P, HP, BT)

    egp = sb("egp", P, HP, NC2, C + 1)
    en = sb("en", P, HP, NC2, C)
    kkn = sb("kkn", P, HP, NC2, C)
    kx = sb("kx", P, HP, NC2, C)
    bon = sb("bon", P, HP, BT)
    t1 = sb("t1", P, HP, BT)
    t2 = sb("t2", P, HP, BT)
    NTl = sb("NTl", P, 8, C)
    Ti = sb("Ti", P, 8, C)
    Tt = sb("Tt", P, 8, C)
    Z = sb("Z", P, 8, C)
    W = sb("W", P, 8, C)
    S = sb("S", P, HP, C)
    y = sb("y", P, HP, BT)
    cs = y[:, :, :].rearrange("p q t -> p (q t)")
    R1 = sb("R1", P, 4096)
    GT = R1[:, 0:2048].rearrange("p (c h q t) -> p c h q t", c=2, h=2, q=4)
    KBt = R1[:, 2048:3072].rearrange("p (c q t) -> p c q t", c=2, q=4)
    UV = R1[:, 3072:4096].rearrange("p (c h q t) -> p c h q t", c=2, h=2, q=4)
    gdE = R1[:, 0:1024].rearrange("p (m i t) -> p m i t", m=4, i=4)
    kE = R1[:, 1024:2048].rearrange("p (m i t) -> p m i t", m=4, i=4)
    Vt = R1[:, 2048:2560].rearrange("p (h t) -> p h t", h=4)
    kdt = R1[:, 2560:2816].rearrange("p (h t) -> p h t", h=2)

    o = R1[:, 3072:3584].rearrange("p (h t) -> p h t", h=4)
    o2 = R1[:, 3584:4096].rearrange("p (h t) -> p h t", h=4)
    scor = R1[:, 0:2048].rearrange("p (m t) -> p m t", m=16)
    scw = R1[:, 2048:2176]
    cand = R1[:, 2176:2432].rearrange("p (a b) -> p a b", a=16)
    candw = R1[:, 2432:2688]
    sif = R1[:, 2688:2944].rearrange("p (h q a) -> p h q a", h=8, q=2)
    cf = R1[:, 2944:3200].rearrange("p (q n) -> p q n", q=2)
    ef = R1[:, 3200:3456].rearrange("p (q n) -> p q n", q=2)
    oh = R2[:, :].rearrange("p (n a) -> p n a", a=TOPK)
    gsg = h1T[:, :, :].rearrange("p a b -> p (a b)")
    xg = sb("xg", P, 2 * BT)
    xa = sb("xa", P, 2 * BT)
    cg = sb("cg", P, 2 * BT)
    gq = sb("gq", P, 2 * BT)
    qI = sb("qI", P, 2, 4, C)
    qi = sb("qi", P, 2, 2, BT)
    At = sb("At", P, GH, BT)
    qe = R1[:, 2816:3072].rearrange("p (h t) -> p h t", h=2)
    kd = sb("kd", P, 2, BT)
    egc = sb("egc", P, 4)
    Sg = sb("Sg", P, 2, P)
    stt = sb("stt", P, 12)
    mv1 = sb("mv1", P, 2)
    sd1 = sb("sd1", P, 2)
    stf = sb("stf", P, 12)
    mv2 = sb("mv2", P, 2)
    sd2 = sb("sd2", P, 2)
    sv = sb("sv", P, 2 * PH, TOPK)
    si = sb("si", P, 2 * PH, TOPK, dt=U32)
    cval = sb("cval", P, PH, TOPK)
    ci = sb("ci", P, PH * TOPK, dt=U32)
    ca = sb("ca", P, 2, PH * TOPK, dt=U32)
    ids = sb("ids", P, PH * TOPK, dt=U32)
    gate = sb("gate", P, PH, TOPK)
    gsum = sb("gsum", P, 2, PH)
    h1c = sb("h1c", P, D)
    idc = sb("idc", P, PH * TOPK, dt=U32)
    gatec = sb("gatec", P, PH, TOPK)
    ur = [sb(f"ur{i}", P, D) for i in range(NU)]
    vr = [sb(f"vr{i}", P, D) for i in range(NV)]
    dots = sb("dots", P, 2, TOPK)
    gel = sb("gel", P, 2, TOPK)
    actg = sb("actg", P, 2, TOPK)
    diag = [sb(f"diag{i}", P, P) for i in range(ND4)]

    vb = lambda c: 64 * c
    ub = lambda c: 64 - 64 * c
    half = lambda h: slice(64 * h, 64 * h + 64)
    v4 = lambda col: vec[:, col:col + 4].unsqueeze(2).to_broadcast([P, 4, BT])
    f4 = lambda t: t[:, :].rearrange("p (a b) -> p a b", a=4)
    f8 = lambda t: t[:, :].rearrange("p (a b) -> p a b", a=8)
    m8 = lambda col: cst[:, col:col + C].unsqueeze(1).to_broadcast([P, 8, C])
    r_, k_, v_ = sh[:, CR:CR + 4, :], sh[:, CK:CK + 4, :], sh[:, CV:CV + 4, :]
    kk4 = kkn[:, :, :, :].rearrange("p q c t -> p q (c t)")
    kx4 = kx[:, :, :, :].rearrange("p q c t -> p q (c t)")
    en4 = en[:, :, :, :].rearrange("p q c t -> p q (c t)")
    cgm = cg[:, :].rearrange("p (m t) -> p m t", m=4)
    cg4 = cg[:, :].rearrange("p (m i t) -> p m i t", m=4, i=4)
    gq4 = gq[:, :].rearrange("p (m i t) -> p m i t", m=4, i=4)
    block = ctx.enter_context(nc.Block())

    def alone(eng):
        eng.sem_inc(s.stood, 1)

    def sp_mixer(sp, b):
        w(sp, s.ymixb_ok, b, 0)
        sp.dma_start(praw[:, :, :], dram.p[:, :, bass.ds(b * BT, PRW)].rearrange("c p t -> p c t")).then_inc(s.praw_in, 16)
        w(sp, s.cur_ok, b, 0, 3)
        sp.dma_start(h1[:, :], dram.h[bass.ds(b * BT, BT), :]).then_inc(s.hin_in, 16)
        for q in range(4):
            w(sp, s.op_mm, b, q, 4)
            sp.dma_start(wo[:, :, :], dram.w_out[q]).then_inc(s.wo_b, 16)
        for m in range(2 * PH):
            w(sp, s.q_mm, b, max(m - 1, 0), 16)
            sp.dma_start(wqb[m % 2][:, :, :], dram.wq[m]).then_inc(s.wq_b[m % 2], 16)

    def sp_experts(sp, b):
        w(sp, s.fo_ok, b)
        sp.dma_start(dram.out[bass.ds(b * BT, BT), :], h1c[:, :]).then_inc(s.out_done, 16)

    def dve_gates(dve, b):
        dve.wait_ge(s.praw_in, b * 16 + 16)
        cur, prev = praw[:, 0:NA, PADC:PRW], praw[:, 0:NA, PADC - 1:PRW - 1]
        dve.tensor_tensor(sh[:, :, :], prev, cur, ALU.subtract).then_inc(s.mix, 1)
        for i in range(NQKV):
            ins = dve.tensor_scalar(cv[:, i, :], praw[:, CQB + i, 0:BT], vec[:, VCV + i:VCV + i + 1], None, ALU.mult)
        ins.then_inc(s.conv_ok, 1)
        w(dve, s.mix, b, MIX["dif_ok"], NMIX)
        dve.tensor_tensor(sh[:, :, :], sh[:, :, :], vec[:, VMU:VMU + NA].unsqueeze(2).to_broadcast([P, NA, BT]), ALU.mult).then_inc(s.mix, 1)
        w(dve, s.mix, b, MIX["difm_ok"], NMIX)
        dve.tensor_tensor(sh[:, :, :], sh[:, :, :], cur, ALU.add).then_inc(s.shift_ok, 1)
        for j in range(1, 4):
            w(dve, s.conv_ok, b, j, 4)
            for i in range(NQKV):
                c = VCV + NQKV * j + i
                ins = dve.scalar_tensor_tensor(cv[:, i, :], praw[:, CQB + i, j:j + BT], vec[:, c:c + 1], cv[:, i, :], ALU.mult, ALU.add)
            ins.then_inc(s.conv_ok, 1)
        w(dve, s.shift_ok, b)
        dve.tensor_tensor(t1[:, :, :], k_, v4(VKK), ALU.mult).then_inc(s.kkr_ok, 1)
        w(dve, s.gkx_mm, b)
        dve.tensor_tensor(xg[:, :].rearrange("p (a t) -> p a t", a=2), Db[:, 0:256].rearrange("p (a t) -> p a t", a=2),
                          vec[:, VGKB:VGKB + 2].unsqueeze(2).to_broadcast([P, 2, BT]), ALU.add).then_inc(s.xg_ok, 1)
        w(dve, s.ss_mm, b)
        dve.tensor_scalar(t2[:, :, :], f4(Eb), 1e-24, None, ALU.max).then_inc(s.ssm_ok, 1)
        w(dve, s.ssq_ok, b)
        dve.reciprocal(t2[:, :, :], t2[:, :, :]).then_inc(s.mix, 1)
        w(dve, s.mix, b, MIX["rin_ok"], NMIX)
        dve.tensor_tensor(kk4, t1[:, :, :], t2[:, :, :], ALU.mult).then_inc(s.mix, 1)

    def dve_decays(dve, b):
        w(dve, s.sig_ok, b)
        dve.tensor_tensor_scan(cs, cst[:, CRS:CRS + 512], sg[:, :, :].rearrange("p a b -> p (a b)"), 0.0, ALU.mult, ALU.add).then_inc(s.csum_ok, 1)
        w(dve, s.a_ok, b)
        w(dve, s.mix, b, MIX["kkn_ok"], NMIX)
        dve.tensor_tensor(t2[:, :, :], aa[:, :, :], v4(VKA), ALU.mult).then_inc(s.mix, 1)
        w(dve, s.mix, b, MIX["kf1_ok"], NMIX)
        dve.tensor_tensor(t2[:, :, :], t2[:, :, :], k.omka[:, :].unsqueeze(2).to_broadcast([P, 4, BT]), ALU.add).then_inc(s.mix, 1)
        w(dve, s.mix, b, MIX["kf1_ok"], NMIX)
        dve.tensor_tensor(aa[:, :, :], aa[:, :, :], kk4, ALU.mult).then_inc(s.mix, 1)
        w(dve, s.mix, b, MIX["kf_ok"], NMIX)
        dve.tensor_tensor(kx4, k_, t2[:, :, :], ALU.mult).then_inc(s.mix, 1)
        w(dve, s.mix, b, MIX["kx_ok"], NMIX)
        dve.tensor_tensor(t1[:, :, :], r_, kx4, ALU.mult).then_inc(s.mix, 1)
        w(dve, s.egp_ok, b)

        e8 = egp[:, :, :, :].rearrange("p q c t -> p (q c) t")
        kk8 = kkn[:, :, :, :].rearrange("p q c t -> p (q c) t")
        for h in range(2):
            dve.scalar_tensor_tensor(RK[half(h), h, :, 0, :], kk8[half(h)], -1.0, e8[half(h), :, 0:C], ALU.mult, ALU.mult)
        w(dve, s.mix, b, MIX["rk1_ok"], NMIX)
        dve.tensor_tensor(t1[:, :, :], t1[:, :, :], v4(VRK), ALU.mult).then_inc(s.rk_ok, 1)
        for h in range(2):
            ins = dve.tensor_tensor(RK[half(h), h, :, 1, :], sh[half(h), CR:CR + 4, :].rearrange("p q (c t) -> p (q c) t", c=2), e8[half(h), :, 1:C + 1], ALU.mult)
        ins.then_inc(s.rkr_ok, 1)
        w(dve, s.en_ok, b)
        w(dve, s.mix, b, MIX["kb1_ok"], NMIX)
        a5 = aa[:, :, :].rearrange("p q (c t) -> p q c t", c=2)
        for c in range(NC2):
            dve.tensor_tensor(KB[:, :, c, c, :], kx[:, :, c, :], en[:, :, c, :], ALU.mult)
            ins = dve.tensor_tensor(KB[:, :, c, 1 - c, :], a5[:, :, c, :], en[:, :, c, :], ALU.mult)
        ins.then_inc(s.kbb_ok, 1)
        w(dve, s.bs_mm, b)
        dve.tensor_tensor(bon[:, :, :], f4(Fb), v_, ALU.mult).then_inc(s.bon_ok, 1)
        for c in range(NC2):
            w(dve, s.vtr_mm, b, c + 1, 2)
            src = (A, B)[c][0:64, :].rearrange("p (q h v) -> p h q v", q=4, h=2)
            dve.memset(UV[ub(c):ub(c) + 64, c, :, :, :], 0.0)
            dve.tensor_copy(UV[vb(c):vb(c) + 64, c, :, :, :], src).then_inc(s.v_ev, 1)

    def dve_inverse(dve, b):
        for c in range(NC2):
            for h in range(2):
                i = 2 * c + h
                w(dve, s.gram_mm, b, i + 1, 4)
                dve.tensor_tensor(GT[:, c, h, :, :], f4((Eb, Fb, A, B)[i]), cst[:, CMG:CMG + P].unsqueeze(1).to_broadcast([P, 4, P]), ALU.mult).then_inc(s.gram_ev, 1)
        w(dve, s.gram_ev, b, 4, 4)
        for c in range(NC2):
            u = slice(ub(c), ub(c) + 64)
            ins = dve.tensor_tensor(Tt[u, :, :], GT[u, c, :, :, 0:C].rearrange("p h q t -> p (h q) t"),
                                    cst[u, CM0T:CM0T + C].unsqueeze(1).to_broadcast([64, 8, C]), ALU.mult)
        ins.then_inc(s.mix, 1)
        w(dve, s.nt_mm, b)
        dve.tensor_tensor(NTl[:, :, :], f8(Cb), m8(CML), ALU.mult).then_inc(s.ntl_ok, 1)
        w(dve, s.mix, b, MIX["tt0_ok"], NMIX)
        dve.tensor_tensor(Tt[:, :, :], Tt[:, :, :], m8(CI64), ALU.add).then_inc(s.tt_ok, 1)
        w(dve, s.ntl_ok, b, 1, 6)
        dve.tensor_tensor(Ti[:, :, :], NTl[:, :, :], m8(CI64), ALU.add).then_inc(s.t_ok, 1)
        for l in range(1, 6):
            if l == 1:
                w(dve, s.t_ok, b, 1, 5)
            else:
                w(dve, s.zz_mm, b, l - 1, 5)
            dve.tensor_tensor(NTl[:, :, :], f8(Cb), m8(CML + C * l), ALU.mult).then_inc(s.ntl_ok, 1)
            if l > 1:
                dve_grow(dve, b, l - 1)
        dve_grow(dve, b, 5)

    def dve_grow(dve, b, l):
        w(dve, s.ttm_mm, b, l, 5)
        if l < 5:
            w(dve, s.tm_mm, b, l, 4)
        dve.tensor_tensor(Tt[:, :, :], Tt[:, :, :], f8(Eb), ALU.add).then_inc(s.tt_ok, 1)
        if l < 5:
            dve.tensor_tensor(Ti[:, :, :], Ti[:, :, :], f8(Fb), ALU.add).then_inc(s.t_ok, 1)

    def dve_chunks(dve, b):
        for c in range(NC2):
            u = slice(ub(c), ub(c) + 64)
            w(dve, s.umm, b, c + 1, 2)
            dve.tensor_copy(UV[u, c, :, :, :].rearrange("p h q t -> p (h q) t"), f8(B)[u, :, :]).then_inc(s.u_ev, 1)
            w(dve, s.st_mm, b, c + 1, 2)
            dve.tensor_tensor(S[:, :, :], S[:, :, :], Eb[:, c * 256:c * 256 + 256].rearrange("p (q t) -> p q t", q=4), ALU.add).then_inc(s.sa_ok, 1)
            w(dve, s.sa_ok, b, c + 1, 2)
            dve.tensor_tensor(S[:, :, :], S[:, :, :], egp[:, :, c, C:C + 1].to_broadcast([P, 4, C]), ALU.mult).then_inc(s.s_ok, 1)
        w(dve, s.y_mm, b, 2, 2)
        dve.tensor_copy(y[:, :, :], f4(Db)).then_inc(s.y_ev, 1)
        w(dve, s.ymean_mm, b)
        w(dve, s.y_ev, b)
        dve.scalar_tensor_tensor(y[:, :, :], f4(Fb), -1.0 / C, y[:, :, :], ALU.mult, ALU.add).then_inc(s.yc_ok, 1)

    def dve_gla_parts(dve, b):
        w(dve, s.xl_ok, b)
        dve.scalar_tensor_tensor(xg[:, :], xg[:, :], 0.0, xa[:, :], ALU.min, ALU.subtract).then_inc(s.mix, 1)
        w(dve, s.mix, b, MIX["gk_ok"], NMIX)
        dve.tensor_tensor_scan(cg[:, :], cst[:, CRS:CRS + 256], xg[:, :], 0.0, ALU.mult, ALU.add).then_inc(s.mix, 1)
        w(dve, s.gsig_ok, b)
        dve.tensor_tensor(cv[:, :, :], cv[:, :, :], gsg.rearrange("p (a b) -> p a b", a=8), ALU.mult).then_inc(s.silu_ok, 1)
        w(dve, s.s_ok, b, 2, 2)
        w(dve, s.y_mm, b, 2, 2)
        w(dve, s.mix, b, MIX["cg_ok"], NMIX)
        dve.memset(R1[:, 0:1024], -30000.0).then_inc(s.gd1_ok, 1)
        w(dve, s.gd1_ok, b, 1, 2)
        dve.tensor_scalar(gdE[:, :, 0, 0:16], cgm[:, :, 0:16], -1.0, None, ALU.mult)
        for i in range(1, 4):
            n = 16 * i + 16
            ins = dve.tensor_tensor(gdE[:, :, i, 0:n], cgm[:, :, 16 * i - 1:16 * i].to_broadcast([P, 4, n]), cgm[:, :, 0:n], ALU.subtract)
        ins.then_inc(s.gd1_ok, 1)
        dve.tensor_copy(gq4[:, :, 0, :], cg4[:, :, 0, :])
        dve.tensor_tensor(gq4[:, :, 1:4, :], cg4[:, :, 1:4, :], cg4[:, :, 0:3, 15:16].to_broadcast([P, 4, 3, 16]), ALU.subtract).then_inc(s.gq1_ok, 1)
        dve.tensor_tensor(kd[:, :, :].rearrange("p q (c t) -> p (q c) t", c=2), cgm[:, :, C - 1:C].to_broadcast([P, 4, C]), cgm, ALU.subtract).then_inc(s.gl1_ok, 1)
        w(dve, s.gd1_ok, b, 2, 2)
        dve.tensor_scalar(R1[:, 0:1024], R1[:, 0:1024], GMAX, None, ALU.min).then_inc(s.gcl_ok, 1)
        w(dve, s.silu_ok, b)
        kg = cv[:, 2:4, :].rearrange("p q (c t) -> p (q c) t", c=2)
        w(dve, s.gex_ok, b)
        dve.tensor_tensor(kE, gdE, kg.unsqueeze(2).to_broadcast([P, 4, 4, C]), ALU.mult)
        w(dve, s.gqx_ok, b)
        for h in range(2):
            ins = dve.scalar_tensor_tensor(qI[half(h), h, :, :], cv[half(h), 0:2, :].rearrange("p q (c t) -> p (q c) t", c=2), 0.125, gq[half(h), :].rearrange("p (m t) -> p m t", m=4), ALU.mult, ALU.mult)
        ins.then_inc(s.gq_ok, 1)
        w(dve, s.gi_ok, b)
        for h in range(2):
            ins = dve.scalar_tensor_tensor(qi[half(h), h, :, :], cv[half(h), 0:2, :], 0.125, qe[half(h)], ALU.mult, ALU.mult)
        ins.then_inc(s.gqi_ok, 1)
        w(dve, s.gl_ok, b)
        dve.tensor_tensor(kd[:, :, :], kd[:, :, :], cv[:, 2:4, :], ALU.mult).then_inc(s.gkd_ok, 1)

    def dve_group_norm(dve, b):
        w(dve, s.ystd_ok, b)
        dve.reciprocal(t2[:, :, :], t2[:, :, :]).then_inc(s.mix, 1)
        w(dve, s.mix, b, MIX["yrs_ok"], NMIX)
        dve.tensor_tensor(y[:, :, :], y[:, :, :], t2[:, :, :], ALU.mult).then_inc(s.yn_ok, 1)
        w(dve, s.yn_ok, b)
        dve.tensor_tensor(y[:, :, :], y[:, :, :], v4(VGG), ALU.mult).then_inc(s.mix, 1)
        dve.tensor_tensor(bon[:, :, :], bon[:, :, :], v4(VGB), ALU.add).then_inc(s.mix, 1)
        w(dve, s.mix, b, MIX["yn2_ok"], NMIX)
        w(dve, s.mix, b, MIX["yn3_ok"], NMIX)
        dve.tensor_tensor(y[:, :, :], y[:, :, :], bon[:, :, :], ALU.add).then_inc(s.mix, 1)
        w(dve, s.mix, b, MIX["yn4_ok"], NMIX)
        dve.tensor_tensor(ymix[:, 0:HP, :], y[:, :, :], gg[:, :, :], ALU.mult)

    def dve_gla(dve, b):
        w(dve, s.ga_mm, b)
        for c in range(NC2):
            tc = slice(c * C, c * C + C)
            ins = dve.tensor_tensor(At[tc, :, tc], Fb[tc, 0:256].rearrange("p (h t) -> p h t", h=4), cst[tc, CMG + C:CMG + P].unsqueeze(1).to_broadcast([64, 4, C]), ALU.mult)
        ins.then_inc(s.ga_ev, 1)
        w(dve, s.gec_ok, b)
        for c in range(NC2):
            w(dve, s.gs_mm, b, c + 1, 2)
            for q in range(2):
                ins = dve.scalar_tensor_tensor(Sg[:, q, :], Sg[:, q, :], egc[:, 2 * q + c:2 * q + c + 1], Eb[:, c * 256 + q * P:c * 256 + q * P + P], ALU.mult, ALU.add)
            ins.then_inc(s.gs_ok, 1)
        w(dve, s.go_mm, b, 2, 2)
        dve.tensor_copy(o, f4(Db)).then_inc(s.go_ev, 1)
        w(dve, s.ostd_ok, b)
        dve.reciprocal(t1[:, :, :], t1[:, :, :]).then_inc(s.mix, 1)
        w(dve, s.mix, b, MIX["ors_ok"], NMIX)
        w(dve, s.go_ev, b)
        dve.scalar_tensor_tensor(o, o, vec[:, VNG:VNG + 1], t1[:, :, :], ALU.mult, ALU.mult).then_inc(s.mix, 1)
        w(dve, s.gsil_ok, b)
        dve.tensor_tensor(t2[:, :, :], t2[:, :, :], praw[:, CGB:CGB + 4, PADC:PRW], ALU.mult).then_inc(s.mix, 1)
        w(dve, s.mix, b, MIX["on_ok"], NMIX)
        w(dve, s.mix, b, MIX["on2_ok"], NMIX)
        dve.tensor_tensor(ymix[:, HP:2 * HP, :], o, t2[:, :, :], ALU.mult).then_inc(s.ymixb_ok, 1)

    def dve_norm(dve, b, x, st, mv, sd, gamma, own, mv_ok, sd_ok, o_ok):
        for j in range(2):
            ins = dve.bn_stats(st[:, 6 * j:6 * j + 6], x[:, 512 * j:512 * j + 512])
        ins.then_inc(own, 1)
        w(dve, own, b, 1, 4)
        alone(dve)
        dve.bn_aggr(mv[:, :], st[:, :]).then_inc(mv_ok, 1)
        w(dve, sd_ok, b)
        dve.reciprocal(sd[:, 1:2], sd[:, 0:1]).then_inc(own, 1)
        w(dve, own, b, 2, 4)
        dve.tensor_scalar(x[:, :], x[:, :], mv[:, 0:1], sd[:, 1:2], ALU.subtract, ALU.mult).then_inc(own, 1)
        w(dve, own, b, 3, 4)
        dve.tensor_tensor(x[:, :], x[:, :], k.ln[:, gamma, :], ALU.mult).then_inc(own, 1)
        w(dve, own, b, 4, 4)
        dve.tensor_tensor(x[:, :], x[:, :], k.ln[:, gamma + 1, :], ALU.add).then_inc(o_ok, 1)

    def dve_residual(dve, b):
        dve.wait_ge(s.hin_in, b * 16 + 16)
        for j in range(2):
            w(dve, s.op_mm, b, 2 * j + 2, 4)
            dve.scalar_tensor_tensor(h1[:, 512 * j:512 * j + 512], h1[:, 512 * j:512 * j + 512], ALPHA, (B, Cb)[j][:, :], ALU.mult, ALU.add).then_inc(s.hy_ok, 1)
        w(dve, s.hy_ok, b, 2, 2)
        dve_norm(dve, b, h1, stt, mv1, sd1, 0, s.norm1, s.mv1_ok, s.sd1_ok, s.h1_ok)

    def dve_top(dve, b, h):
        n = [16 * h]

        def step(ins):
            ins.then_inc(s.tk_ok, 1)
            n[0] += 1

        def done():
            w(dve, s.tk_ok, b, n[0], 16 * PH)
            alone(dve)

        def top16(src, work, vals, idx):
            step(dve.max(vals[:, 0:8], src))
            done()
            step(dve.max_index(idx[:, 0:8], vals[:, 0:8], src))
            step(dve.match_replace(work, vals[:, 0:8], src, NEG))
            done()
            step(dve.max(vals[:, 8:16], work))
            done()
            step(dve.max_index(idx[:, 8:16], vals[:, 8:16], work))

        w(dve, s.sc_ev, b, h // 2 + 1, 4)
        alone(dve)
        for p in range(2):
            m = 2 * h + p
            top16(scor[:, m, :], scw, sv[:, m, :], si[:, m, :])
        step(dve.tensor_tensor(cand, sv[:, 2 * h, :].unsqueeze(2).to_broadcast([P, 16, 16]), sv[:, 2 * h + 1, :].unsqueeze(1).to_broadcast([P, 16, 16]), ALU.add))
        done()
        top16(cand.rearrange("p a b -> p (a b)"), candw, cval[:, h, :], ci[:, 16 * h:16 * h + 16])
        assert n[0] == 16 * h + 16

    def dve_ids(dve, b):
        n = [0]

        def step(ins):
            ins.then_inc(s.ids_ok, 1)
            n[0] += 1

        def done():
            w(dve, s.ids_ok, b, n[0], NIDS)

        w(dve, s.tk_ok, b, 16 * PH, 16 * PH)
        step(dve.tensor_tensor(gate[:, :, :], cval[:, :, :], cval[:, :, 0:1].to_broadcast([P, PH, TOPK]), ALU.subtract))
        step(dve.tensor_scalar(ca[:, 0, :], ci[:, :], 4, None, ALU.logical_shift_right))
        step(dve.tensor_scalar(ca[:, 1, :], ci[:, :], 15, None, ALU.bitwise_and))
        step(dve.tensor_copy(sif, si[:, :, :].rearrange("p (h q) a -> p h q a", q=2)))
        done()
        step(dve.tensor_copy(cf, ca[:, :, :]))
        io = cst[:, CIO:CIO + TOPK].unsqueeze(1).to_broadcast([P, P // 2, TOPK])
        oh4 = oh.rearrange("p (h n) a -> p h n a", h=PH // 2)
        for q in range(2):
            for j in range(2):
                hk, hh = slice(64 * j, 64 * j + 64), slice(4 * j, 4 * j + 4)
                done()
                step(dve.tensor_tensor(oh, cf[:, q, hk].unsqueeze(2).to_broadcast([P, P // 2, TOPK]), io, ALU.is_equal))
                done()
                step(dve.tensor_tensor(oh4, oh4, sif[:, hh, q, :].unsqueeze(2).to_broadcast([P, PH // 2, TOPK, TOPK]), ALU.mult))
                done()
                step(dve.tensor_reduce(ef[:, q, hk], oh, AX.X, ALU.add))
        done()
        step(dve.scalar_tensor_tensor(ids[:, :], ef[:, 0, :], float(NKEY), ef[:, 1, :], ALU.mult, ALU.add))
        w(dve, s.ge_ok, b)
        step(dve.tensor_reduce(gsum[:, 0, :], gate[:, :, :], AX.X, ALU.add))
        done()
        step(dve.reciprocal(gsum[:, 1, :], gsum[:, 0, :]))
        done()
        step(dve.tensor_tensor(gate[:, :, :], gate[:, :, :], gsum[:, 1, :].unsqueeze(2).to_broadcast([P, PH, TOPK]), ALU.mult))
        assert n[0] == NIDS

    def dve_take(dve, b):
        w(dve, s.ids_ok, b, NIDS, NIDS)
        dve.wait_ge(s.out_done, b * 16)
        dve.tensor_copy(h1c[:, :], h1[:, :]).then_inc(s.cur_ok, 1)
        dve.tensor_copy(idc[:, :], ids[:, :]).then_inc(s.cur_ok, 1)
        dve.tensor_copy(gatec[:, :, :], gate[:, :, :]).then_inc(s.cur_ok, 1)
        w(dve, s.cur_ok, b, 3, 3)

    def dve_dots(dve, b, h, part):
        for kk in range(4 * part, 4 * part + 4):
            g = h * TOPK + kk
            dve.wait_ge(s.u_in[g % NU], (b * (P // NU) + g // NU + 1) * 16)
            u = ur[g % NU][:, :]
            dve.tensor_tensor_reduce(u, u, h1c[:, :], 1.0, 0.0, ALU.mult, ALU.add, dots[:, h % 2, kk:kk + 1]).then_inc(s.u_done, 1)

    def dve_act(dve, b, h):
        w(dve, s.gelu_ok, b, h + 1, PH)
        dve.tensor_tensor(actg[:, h % 2, :], gel[:, h % 2, :], gatec[:, h, :], ALU.mult).then_inc(s.act_ok, 1)

    def dve_final(dve, b):
        dve.wait_ge(s.v_done, NV + b * P + P)
        for j in range(2):
            ins = dve.scalar_tensor_tensor(h1c[:, 512 * j:512 * j + 512], h1c[:, 512 * j:512 * j + 512], ALPHA, F[j][:, :], ALU.mult, ALU.add)
        ins.then_inc(s.fy_ok, 1)
        w(dve, s.fy_ok, b)
        dve_norm(dve, b, h1c, stf, mv2, sd2, 2, s.norm2, s.mv2_ok, s.sd2_ok, s.fo_ok)

    def act_gates(act, b):
        w(act, s.shift_ok, b)
        act.activation(th[:, :], sh[0:64, CWA, :], ACT.Tanh).then_inc(s.th_ok, 1)
        act.activation(sgd[:, :], sh[:, CGD, :], ACT.Sigmoid).then_inc(s.sgd_ok, 1)
        w(act, s.z_mm, b)
        for i in range(4):
            ins = act.activation(sg[:, i, :], A[:, i * BT:i * BT + BT], ACT.Sigmoid, bias=vec[:, VW0 + i:VW0 + i + 1])
        ins.then_inc(s.sig_ok, 1)
        w(act, s.a_mm, b)
        for i in range(4):
            ins = act.activation(aa[:, i, :], B[:, i * BT:i * BT + BT], ACT.Sigmoid, bias=vec[:, VA0 + i:VA0 + i + 1])
        ins.then_inc(s.a_ok, 1)
        w(act, s.conv_ok, b, 4, 4)
        act.activation(gsg, cv[:, :, :].rearrange("p a b -> p (a b)"), ACT.Sigmoid).then_inc(s.gsig_ok, 1)
        w(act, s.g_mm, b)
        act.activation(gg[:, :, :], f4(Cb), ACT.Copy).then_inc(s.g_ok, 1)
        w(act, s.kkr_ok, b)
        act.activation(kk4, t1[:, :, :], ACT.Square).then_inc(s.sq_ok, 1)
        w(act, s.ssm_ok, b)
        act.activation(t2[:, :, :], t2[:, :, :], ACT.Sqrt, bias=k.eps[:, 2:3]).then_inc(s.ssq_ok, 1)
        w(act, s.csum_ok, b)
        act.activation(egp[:, :, :, 1:C + 1], cs[:, :].rearrange("p (q c t) -> p q c t", q=4, c=2), ACT.Exp, scale=-E05).then_inc(s.egp_ok, 1)
        act.activation(en[:, :, :, :], cs[:, :].rearrange("p (q c t) -> p q c t", q=4, c=2), ACT.Exp, scale=E05).then_inc(s.en_ok, 1)
        w(act, s.xg_ok, b)
        act.activation(xa[:, :], xg[:, :], ACT.Abs).then_inc(s.xa_ok, 1)
        w(act, s.xa_ok, b, 1, 2)
        act.activation(xa[:, :], xa[:, :], ACT.Exp, scale=-1.0).then_inc(s.xa_ok, 1)
        w(act, s.xa_ok, b, 2, 2)
        act.activation(xa[:, :], xa[:, :], ACT.Ln, bias=1.0).then_inc(s.xl_ok, 1)
        for c in range(NC2):
            w(act, s.kbt_mm, b, c + 1, 2)
            act.activation(KBt[:, c, :, :], f4((Cb, Db)[c]), ACT.Copy).then_inc(s.kbt_ev, 1)

    def act_inverse(act, b):
        for l in range(1, 6):
            w(act, s.zz_mm, b, l, 5)
            if l > 1:
                w(act, s.tm_mm, b, l - 1, 4)
            act.activation(Z[:, :, :], f8(Db), ACT.Copy).then_inc(s.zz_ev, 1)

    def act_chunks(act, b):
        for c in range(NC2):
            u = slice(ub(c), ub(c) + 64)
            w(act, s.wmm, b, c + 1, 2)
            act.activation(W[u, :, :], f8(A)[u, :, :], ACT.Copy).then_inc(s.w_ev, 1)
        w(act, s.gcl_ok, b)
        act.activation(R1[:, 0:1024], R1[:, 0:1024], ACT.Exp, scale=1.0 / 16).then_inc(s.gex_ok, 1)
        w(act, s.gq1_ok, b)
        act.activation(gq[:, :], gq[:, :], ACT.Exp, scale=1.0 / 16).then_inc(s.gqx_ok, 1)
        act.activation(qe, cg[:, :].rearrange("p (q t) -> p q t", q=2), ACT.Exp, scale=1.0 / 16).then_inc(s.gi_ok, 1)
        w(act, s.gl1_ok, b)
        act.activation(kd[:, :, :], kd[:, :, :], ACT.Exp, scale=1.0 / 16).then_inc(s.gl_ok, 1)
        act.activation(egc[:, :], cgm[:, :, C - 1], ACT.Exp, scale=1.0 / 16).then_inc(s.gec_ok, 1)
        w(act, s.yc_ok, b)
        act.activation(t1[:, :, :], y[:, :, :], ACT.Square).then_inc(s.ysq_ok, 1)
        w(act, s.yvar_mm, b)
        act.activation(t2[:, :, :], f4(A), ACT.Sqrt, bias=k.eps[:, 1:2], scale=1.0 / C).then_inc(s.ystd_ok, 1)

    def act_gla(act, b):
        w(act, s.gvt_mm, b)
        act.activation(Vt, f4(B), ACT.Copy).then_inc(s.gvt_ev, 1)
        w(act, s.gkt_mm, b)
        act.activation(kdt, Cb[:, 0:256].rearrange("p (q t) -> p q t", q=2), ACT.Copy).then_inc(s.gkt_ev, 1)
        w(act, s.go_ev, b)
        act.activation(o2, o, ACT.Square).then_inc(s.osq_ok, 1)
        w(act, s.orms_mm, b)
        act.activation(t1[:, :, :], f4(A), ACT.Sqrt, bias=k.eps[:, 0:1], scale=1.0 / P).then_inc(s.ostd_ok, 1)
        w(act, s.yn_ok, b)
        act.activation(t2[:, :, :], praw[:, CGB:CGB + 4, PADC:PRW], ACT.Sigmoid).then_inc(s.gsil_ok, 1)

    def act_queries(act, b):
        w(act, s.mv1_ok, b)
        act.activation(sd1[:, 0:1], mv1[:, 1:2], ACT.Sqrt, bias=k.eps[:, 0:1]).then_inc(s.sd1_ok, 1)
        for j in range(2):
            w(act, s.h1t_mm, b, j + 1, 2)
            act.activation(h1T[:, 4 * j:4 * j + 4, :], f4((Db, Eb)[j]), ACT.Copy).then_inc(s.h1t_ev, 1)
        for g in range(4):
            w(act, s.q_mm, b, 4 * g + 4, 16)
            if g >= 2:
                w(act, s.sc_mm, b, g - 1, 4)
            act.activation(qT[g % 2], f4((Fb, A)[g % 2]), ACT.Copy).then_inc(s.q_ev, 1)
            w(act, s.sc_mm, b, g + 1, 4)
            act.activation(scor[:, 4 * g:4 * g + 4, :], f4((B, Cb)[g % 2]), ACT.Copy).then_inc(s.sc_ev, 1)

    qT = [y[:, :, :], bon[:, :, :]]

    def act_softmax(act, b):
        w(act, s.ids_ok, b, 1, NIDS)
        act.activation(gate[:, :, :], gate[:, :, :], ACT.Exp).then_inc(s.ge_ok, 1)

    def act_gelu(act, b, h):
        act.wait_ge(s.u_done, NU + b * P + (h + 1) * TOPK)
        act.activation(gel[:, h % 2, :], dots[:, h % 2, :], ACT.Gelu).then_inc(s.gelu_ok, 1)

    def act_diags(act, b, h, part):
        w(act, s.act_ok, b, h + 1, PH)
        for kk in range(4 * part, 4 * part + 4):
            g = h * TOPK + kk
            act.wait_ge(s.v_done, b * P + g + 1)
            act.activation(diag[g % ND4][:, :], cst[:, CID:CID + P], ACT.Copy, scale=actg[:, h % 2, kk:kk + 1]).then_inc(s.diag_ok, 1)

    def act_final(act, b):
        w(act, s.mv2_ok, b)
        act.activation(sd2[:, 0:1], mv2[:, 1:2], ACT.Sqrt, bias=k.eps[:, 0:1]).then_inc(s.sd2_ok, 1)

    def mm(pe, out, l, r, start=True, stop=True):
        return pe.matmul(out, l, r, start=start, stop=stop)

    def pe_gates(pe, b):
        ident, ones2 = cst[:, CID:CID + P], cst[:, CBO:CBO + P]
        w(pe, s.th_ok, b)
        for i in range(4):
            ins = mm(pe, A[:, i * BT:i * BT + BT], k.w2a2[0:64, i * P:i * P + P], th[:, :])
        ins.then_inc(s.z_mm, 1)
        for i in range(4):
            ins = mm(pe, B[:, i * BT:i * BT + BT], k.w2a2[64:128, i * P:i * P + P], sh[64:128, CWA, :])
        ins.then_inc(s.a_mm, 1)
        w(pe, s.sgd_ok, b)
        for i in range(4):
            ins = mm(pe, Cb[:, i * BT:i * BT + BT], k.g2[:, i * P:i * P + P], sgd[:, :])
        ins.then_inc(s.g_mm, 1)
        for i in range(2):
            ins = mm(pe, Db[:, i * BT:i * BT + BT], k.gkw2[:, i * P:i * P + P], praw[0:16, CGK, PADC:PRW])
        ins.then_inc(s.gkx_mm, 1)
        w(pe, s.sq_ok, b)
        mm(pe, Eb[:, :], ones2, kk4.rearrange("p q t -> p (q t)")).then_inc(s.ss_mm, 1)
        w(pe, s.rk_ok, b)
        mm(pe, Fb[:, :], ones2, t1[:, :, :].rearrange("p q t -> p (q t)")).then_inc(s.bs_mm, 1)
        w(pe, s.a_ok, b)
        alone(pe)
        for c in range(NC2):
            for q in range(4):
                ins = pe.transpose((A, B)[c][0:64, q * P:q * P + P], sh[:, CV + q, c * C:c * C + C], ident)
            ins.then_inc(s.vtr_mm, 1)
        w(pe, s.g_ok, b)
        w(pe, s.xg_ok, b)
        w(pe, s.kbb_ok, b)
        for c in range(NC2):
            for q in range(4):
                ins = pe.transpose((Cb, Db)[c][:, q * P:q * P + P], KB[:, q, c, :, :].rearrange("p s t -> p (s t)"), ident)
            ins.then_inc(s.kbt_mm, 1)
        w(pe, s.rkr_ok, b)
        for c in range(NC2):
            for h in range(2):
                i = 2 * c + h
                if i < 2:
                    w(pe, (s.ssm_ok, s.bon_ok)[i], b)
                else:
                    w(pe, s.v_ev, b, i - 1, 2)
                for q in range(4):
                    ins = mm(pe, (Eb, Fb, A, B)[i][:, q * P:q * P + P], KB[:, q, c, :, :].rearrange("p s t -> p (s t)"),
                             RK[:, h, 2 * q + c, :, :].rearrange("p s t -> p (s t)"))
                ins.then_inc(s.gram_mm, 1)
        w(pe, s.kbt_ev, b, 1, 2)
        alone(pe)
        for c in range(NC2):
            for h in range(2):
                for q in range(4):
                    m = (h * 4 + q) * C
                    ins = mm(pe, Cb[ub(c):ub(c) + 64, m:m + C], RK[:, h, 2 * q + c, 0, :], KB[:, q, c, 1 - c, :])
        ins.then_inc(s.nt_mm, 1)

    def each(fn):
        for c in range(NC2):
            for m in range(8):
                ins = fn(slice(ub(c), ub(c) + 64), m)
        return ins

    def pe_inverse(pe, b):
        for l in range(1, 6):
            w(pe, s.tt_ok, b, l, 6)
            w(pe, s.t_ok, b, l, 5)
            w(pe, s.ntl_ok, b, l + 1, 6)
            if l == 1:
                w(pe, s.kbt_ev, b, 2, 2)
                w(pe, s.gram_ev, b, 4, 4)
            else:
                w(pe, s.zz_ev, b, l - 1, 5)
            alone(pe)
            each(lambda u, m: mm(pe, Db[u, m * C:m * C + C], NTl[u, m, :], Tt[u, m, :])).then_inc(s.zz_mm, 1)
            w(pe, s.zz_ev, b, l, 5)
            alone(pe)
            each(lambda u, m: mm(pe, Eb[u, m * C:m * C + C], Ti[u, m, :], Z[u, m, :])).then_inc(s.ttm_mm, 1)
            if l < 5:
                each(lambda u, m: mm(pe, Fb[u, m * C:m * C + C], Z[u, m, :], Ti[u, m, :])).then_inc(s.tm_mm, 1)

    def pe_chunks(pe, b):
        for c in range(NC2):
            u = slice(ub(c), ub(c) + 64)
            hq = [(h, q) for h in range(2) for q in range(4)]
            w(pe, s.s_ok, b, c, 2)
            w(pe, s.v_ev, b, 2, 2)
            if c:
                w(pe, s.w_ev, b, 1, 2)
            alone(pe)
            for h, q in hq:
                m = (h * 4 + q) * C
                mm(pe, A[u, m:m + C], RK[:, h, 2 * q + c, 0, :], S[:, q, :], stop=False)
                ins = mm(pe, A[u, m:m + C], GT[:, c, h, q, 0:C], UV[:, c, h, q, :], start=False)
            ins.then_inc(s.wmm, 1)
            w(pe, s.w_ev, b, c + 1, 2)
            w(pe, s.tt_ok, b, 6, 6)
            if c:
                w(pe, s.u_ev, b, 1, 2)
            alone(pe)
            for h, q in hq:
                m = h * 4 + q
                ins = mm(pe, B[u, m * C:m * C + C], Tt[u, m, :], W[u, m, :])
            ins.then_inc(s.umm, 1)
            w(pe, s.u_ev, b, c + 1, 2)
            alone(pe)
            for h, q in hq:
                col = q * BT + c * C
                mm(pe, Db[half(h), col:col + C], S[:, q, :], RK[:, h, 2 * q + c, 1, :], stop=False)
                ins = mm(pe, Db[half(h), col:col + C], UV[:, c, h, q, :], GT[:, c, h, q, C:2 * C], start=False)
            ins.then_inc(s.y_mm, 1)
            for h, q in hq:
                col = c * 256 + q * C
                ins = mm(pe, Eb[half(h), col:col + C], KBt[:, c, q, h * C:h * C + C], UV[:, c, h, q, :])
            ins.then_inc(s.st_mm, 1)
        w(pe, s.y_ev, b)
        w(pe, s.t_ok, b, 5, 5)
        mm(pe, Fb[:, :], cst[:, CBO:CBO + P], y[:, :, :].rearrange("p q t -> p (q t)")).then_inc(s.ymean_mm, 1)
        w(pe, s.ysq_ok, b)
        mm(pe, A[:, :], cst[:, CBO:CBO + P], t1[:, :, :].rearrange("p q t -> p (q t)")).then_inc(s.yvar_mm, 1)

    def pe_gla(pe, b):
        ident = cst[:, CID:CID + P]
        w(pe, s.silu_ok, b)
        w(pe, s.u_ev, b, 2, 2)
        for h in range(4):
            ins = pe.transpose(B[:, h * P:h * P + P], cv[:, 4 + h, :], ident)
        ins.then_inc(s.gvt_mm, 1)
        w(pe, s.gkd_ok, b)
        for q in range(2):
            ins = pe.transpose(Cb[:, q * P:q * P + P], kd[:, q, :], ident)
        ins.then_inc(s.gkt_mm, 1)
        w(pe, s.gq_ok, b)
        w(pe, s.yc_ok, b)
        alone(pe)
        for h in range(4):
            for c in range(NC2):
                m = (h // 2) * 2 + c
                for i in range(4):
                    col = h * C + 16 * i
                    ins = mm(pe, Fb[c * C:c * C + C, col:col + 16], kE[:, m, i, :], qI[:, h % 2, m, 16 * i:16 * i + 16])
        ins.then_inc(s.ga_mm, 1)
        w(pe, s.gqi_ok, b)
        w(pe, s.gvt_ev, b)
        w(pe, s.gkt_ev, b)
        w(pe, s.ga_ev, b)
        for c in range(NC2):
            w(pe, s.gs_ok, b, c, 2)
            alone(pe)
            tc = slice(c * C, c * C + C)
            for h in range(4):
                col = h * P + c * C
                mm(pe, Db[:, col:col + C], Sg[:, h // 2, :], qi[:, h % 2, h // 2, tc], stop=False)
                ins = mm(pe, Db[:, col:col + C], Vt[:, h, :], At[:, h, tc], start=False)
            ins.then_inc(s.go_mm, 1)
            for h in range(4):
                col = c * 256 + (h // 2) * P
                ins = mm(pe, Eb[half(h % 2), col:col + P], kdt[tc, h // 2, (h % 2) * C:(h % 2) * C + C], Vt[tc, h, :])
            ins.then_inc(s.gs_mm, 1)
        w(pe, s.osq_ok, b)
        w(pe, s.ystd_ok, b)
        mm(pe, A[:, :], k.ones[:, :], o2.rearrange("p q t -> p (q t)")).then_inc(s.orms_mm, 1)

    def pe_out(pe, b):
        w(pe, s.ymixb_ok, b)
        for q in range(4):
            pe.wait_ge(s.wo_b, (b * 4 + q + 1) * 16)
            for c in range(ND):
                ins = mm(pe, (B, Cb)[q // 2][:, (q % 2) * 256:(q % 2) * 256 + 256], ymix[:, c, :], wo[:, c, :], start=c == 0, stop=c == ND - 1)
            ins.then_inc(s.op_mm, 1)
        w(pe, s.h1_ok, b)
        w(pe, s.gs_ok, b, 2, 2)
        w(pe, s.go_ev, b)
        for j in range(2):
            for d in range(4):
                ins = pe.transpose((Db, Eb)[j][:, d * P:d * P + P], h1[:, (4 * j + d) * P:(4 * j + d) * P + P], cst[:, CID:CID + P])
            ins.then_inc(s.h1t_mm, 1)

    def pe_queries(pe, b):
        def queries(g):
            if g == 0:
                w(pe, s.h1t_ev, b, 2, 2)
                w(pe, s.ga_ev, b)
            if g == 1:
                w(pe, s.ostd_ok, b)
            if g >= 2:
                w(pe, s.q_ev, b, g - 1, 4)
            for i in range(4):
                m = 4 * g + i
                pe.wait_ge(s.wq_b[m % 2], (b * 8 + m // 2 + 1) * 16)
                for d in range(ND):
                    ins = mm(pe, (Fb, A)[g % 2][:, i * P:i * P + P], wqb[m % 2][:, d, :], h1T[:, d, :], start=d == 0, stop=d == ND - 1)
                ins.then_inc(s.q_mm, 1)

        def scores(g):
            w(pe, s.q_ev, b, g + 1, 4)
            if g < 2:
                w(pe, s.hy_ok, b, 2, 2)
            else:
                w(pe, s.sc_ev, b, g - 1, 4)
            for i in range(4):
                ins = mm(pe, (B, Cb)[g % 2][:, i * P:i * P + P], qT[g % 2][:, i, :], k.keys[:, 4 * g + i, :])
            ins.then_inc(s.sc_mm, 1)
        for g in range(4):
            queries(g)
            scores(g)

    def pe_values(pe, b, h, part):
        for kk in range(4 * part, 4 * part + 4):
            g = h * TOPK + kk
            pe.wait_ge(s.v_in[g % NV], (b * (P // NV) + g // NV + 1) * 16)
            pe.wait_ge(s.diag_ok, b * P + g + 1)
            if g == 0:
                w(pe, s.fy_ok, b, 0)
            for j in range(2):
                ins = mm(pe, F[j][:, :], diag[g % ND4][:, :], vr[g % NV][:, 512 * j:512 * j + 512], start=g == 0, stop=g == P - 1)
            ins.then_inc(s.v_done, 1)

    def gather_u(pool, b, h, kk):
        g = h * TOPK + kk
        pool.wait_ge(s.u_done, b * P + g + 1)
        alone(pool)
        pool.indirect_dma_start(ur[g % NU][:, :], None, dram.u, bass.IndirectOffsetOnAxis(idc[:, g:g + 1], 0)).then_inc(s.u_in[g % NU], 16)

    def gather_v(pool, b, h, kk):
        g = h * TOPK + kk
        pool.wait_ge(s.v_done, b * P + g + 1)
        alone(pool)
        pool.indirect_dma_start(vr[g % NV][:, :], None, dram.v, bass.IndirectOffsetOnAxis(idc[:, g:g + 1], 0)).then_inc(s.v_in[g % NV], 16)

    @block.sync
    def _(sp):
        with sp.Fori(0, NBLK) as b:
            sp_mixer(sp, b)
            sp_experts(sp, b)
        sp.wait_ge(s.out_done, 16 * NBLK)

    @block.scalar
    def _(act):
        w(act, s.credits, 0, NINIT)
        with act.Fori(0, NBLK) as b:
            act_gates(act, b)
            act_inverse(act, b)
            act_chunks(act, b)
            act_gla(act, b)
            act_queries(act, b)
            act_softmax(act, b)
            for h in range(PH + 1):
                for part in range(4):
                    if h > 0:
                        act_diags(act, b, h - 1, part)
                if h < PH:
                    act_gelu(act, b, h)
            act_final(act, b)

    @block.vector
    def _(dve):
        dve.memset(S[:, :, :], 0.0).then_inc(s.credits, 1)
        dve.memset(Sg[:, :, :], 0.0).then_inc(s.credits, 1)
        dve.memset(RK[:, :, :, :, :], 0.0)
        dve.memset(qI[:, :, :, :], 0.0)
        dve.memset(qi[:, :, :, :], 0.0)
        dve.memset(At[:, :, :], 0.0)
        dve.memset(egp[:, :, :, 0:1], 1.0).then_inc(s.credits, 1)
        dve.memset(k.ones[:, :], 1.0).then_inc(s.credits, 1)
        dve.tensor_scalar(k.omka[:, :], vec[:, VKA:VKA + 4], -1.0, 1.0, ALU.mult, ALU.add).then_inc(s.credits, 1)
        dve.memset(stt[:, 0:1], 0.0).then_inc(s.u_done, NU)
        dve.memset(stt[:, 1:2], 0.0).then_inc(s.v_done, NV)
        w(dve, s.credits, 0, NINIT)
        with dve.Fori(0, NBLK) as b:
            dve_gates(dve, b)
            dve_decays(dve, b)
            dve_inverse(dve, b)
            dve_chunks(dve, b)
            dve_gla_parts(dve, b)
            dve_group_norm(dve, b)
            dve_gla(dve, b)
            dve_residual(dve, b)
            for h in range(PH):
                dve_top(dve, b, h)
            dve_ids(dve, b)
            dve_take(dve, b)
            for h in range(PH + 1):
                for part in range(4):
                    if h < PH:
                        dve_dots(dve, b, h, part)
                    if part == 0 and h > 0:
                        dve_act(dve, b, h - 1)
            dve_final(dve, b)

    @block.tensor
    def _(pe):
        w(pe, s.credits, 0, NINIT)
        with pe.Fori(0, NBLK) as b:
            pe_gates(pe, b)
            pe_inverse(pe, b)
            pe_chunks(pe, b)
            pe_gla(pe, b)
            pe_out(pe, b)
            pe_queries(pe, b)
            for h in range(PH):
                for part in range(4):
                    pe_values(pe, b, h, part)

    @block.gpsimd
    def _(pool):
        with pool.Fori(0, NBLK) as b:
            w(pool, s.cur_ok, b, 3, 3)
            for h in range(PH + 1):
                for kk in range(TOPK):
                    if h < PH:
                        gather_u(pool, b, h, kk)
                    if h > 0:
                        gather_v(pool, b, h - 1, kk)

_INS = ['x', 'w_in', 'vec', 'cst', 'w2a2', 'g2', 'gkw2', 'lnrows', 'w_out', 'wq', 'keys', 'u', 'v']


def _constants():
    import numpy as np
    c = np.zeros((P, NCST), np.float32)
    p = np.arange(P)
    q = p % C
    col = np.arange(C)
    c[:, CID:CID + P] = np.eye(P)
    c[:, CBO:CBO + P] = (p[:, None] // C == p[None, :] // C)
    c[:, CMG:CMG + C] = q[:, None] < col[None, :]
    c[:, CMG + C:CMG + 2 * C] = q[:, None] <= col[None, :]
    for l in range(6):
        s = 1 << l
        t, j = q[:, None], col[None, :]
        m = (t // (2 * s) == j // (2 * s)) & (t % (2 * s) >= s) & (j % (2 * s) < s)
        c[:, CML + l * C:CML + (l + 1) * C] = m
        if l == 0:
            c[:, CM0T:CM0T + C] = (j // 2 == t // 2) & (j % 2 == 1) & (t % 2 == 0)
    c[:, CI64:CI64 + C] = q[:, None] == col[None, :]
    c[:, CRS:CRS + 512] = (np.arange(512) % C != 0)[None, :]
    c[:, CIO:CIO + TOPK] = np.arange(TOPK)[None, :]
    return c


def kernel(**inputs):
    import numpy as np
    import concourse.bacc as bacc
    from concourse.bass_utils import run_bass_kernel_spmd

    a = {n: np.asarray(v) for n, v in inputs.items()}
    cols = lambda v: v.reshape(-1, P).T
    wi = a['w_in'][0]
    gk0 = CGK * P
    wi = np.concatenate([wi[:, :gk0 + P], wi[:, gk0 + 16:]], axis=1)
    vec = np.concatenate([cols(a['a_mu'][0]), cols(a['a_w0'][0]), cols(a['a_a0'][0]), cols(a['a_k_k'][0]), cols(a['a_k_a'][0]),
                          cols(a['a_r_k'][0].reshape(-1)), cols(a['a_gn_g'][0]), cols(a['a_gn_b'][0]),
                          cols(a['b_conv'][0].reshape(-1)), cols(a['b_gk_b'][0]), cols(a['b_norm_g'][0])], axis=1)
    arrays = {
        'x': a['x'][0],
        'w_in': wi.reshape(ND, P, NCH, P).transpose(2, 1, 0, 3),
        'vec': vec,
        'cst': _constants(),
        'w2a2': np.concatenate([a['a_w2'][0], a['a_a2'][0]], axis=0),
        'g2': a['a_g2'][0],
        'gkw2': a['b_gk_w2'][0],
        'lnrows': np.stack([a['ln_in_g'], a['ln_in_b'], a['ln1_g'][0], a['ln1_b'][0], a['ln2_g'][0], a['ln2_b'][0]]),
        'w_out': a['w_out'][0].reshape(ND, P, 4, 256).transpose(2, 1, 0, 3),
        'wq': a['p_wq'][0].reshape(ND, P, 2 * PH, P).transpose(2, 1, 0, 3),
        'keys': a['p_keys'][0].reshape(2 * PH, NKEY, P).transpose(2, 0, 1),
        'u': a['p_u'][0],
        'v': a['p_v'][0],
    }
    nc = bacc.Bacc("TRN2", target_bir_lowering=False, num_devices=1)
    ins, args = {}, []
    for name in _INS:
        arr = np.ascontiguousarray(arrays[name])
        ins[f"in_{name}_dram"] = arr
        args.append(nc.dram_tensor(f"in_{name}_dram", arr.shape, mybir.dt.from_np(arr.dtype), kind="ExternalInput").ap())
    out = nc.dram_tensor("out_0_dram", (T, D), F32, kind="ExternalOutput").ap()
    hybrid_layer(nc, *args, out)
    r = run_bass_kernel_spmd(nc, [ins], core_ids=[0])
    return r.results[0]["out_0_dram"].reshape(1, T, D)
```

```python
from collections import namedtuple
from contextlib import ExitStack

import concourse.bass as bass
from concourse import mybir

F32 = mybir.dt.float32
U32 = mybir.dt.uint32
ALU = mybir.AluOpType
ACT = mybir.ActivationFunctionType
AX = mybir.AxisListType

P = 128
T = 1024
D = 1024
ND = D // P
BT = 128
NBLK = T // BT
C = 64
NC2 = BT // C
HP = 4
GH = 4
NCH = 27
PADC = 3
PW = T + PADC
PRW = BT + PADC
CR, CK, CV, CWA, CGD, CQB, CKB, CVB, CGK, CGB = 0, 4, 8, 12, 13, 14, 16, 18, 22, 23
NA = 14
NQKV = 8
EPS = 1e-5
GN_EPS = 64e-5
ALPHA = 2.0 ** 0.25
E05 = 0.6065306597126334
GMAX = 16.0 * 60.0
PH = 8
TOPK = 16
NKEY = 128
NU = 4
NV = 4
VLAG = 4
PLAG = 7
X0 = TOPK + PLAG
LATE = 2 * TOPK
X_KEEP = 41
NWB = (ND + 2 * PH) // 2
ND4 = 4
NEG = -3.0e38
NINIT = 9
NIDS = 21

VMU, VW0, VA0, VKK, VKA, VRK, VGG, VGB, VCV, VGKB, VNG, NVEC = 0, 14, 18, 22, 26, 30, 34, 38, 42, 74, 76, 77
CID, CBO, CMG, CML, CM0T, CI64, CRS, CIO, NCST = 0, 128, 256, 384, 768, 832, 896, 1408, 1424

SIGNALS = """
x_in par_in keys_in lnin_in zpad_out stat_mv std_ok rstd_ok z_ok zg_ok h_ok htr_ok hev_ok h_out
proj_mm proj_ev p_stored
praw_in hin_in credits
shift_ok conv_ok th_ok sgd_ok z_mm a_mm g_mm sig_ok a_ok g_ok csum_ok egp_ok en_ok
kkr_ok sq_ok ss_mm ssm_ok ssq_ok rk_ok bs_mm bon_ok rkr_ok kbb_ok
gkx_mm xg_ok xa_ok xl_ok gsig_ok silu_ok gsil_ok
vtr_mm v_ev kbt_mm kbt_ev gram_mm gram_ev nt_mm ntl_ok tt_ok t_ok zz_mm zz_ev ttm_mm tm_mm
wmm w_ev umm u_ev y_mm y_ev st_mm sa_ok s_ok
ymean_mm yc_ok ysq_ok yvar_mm ystd_ok yn_ok
gd1_ok gcl_ok gex_ok gq1_ok gqx_ok gq_ok gi_ok gqi_ok gl1_ok gl_ok gkd_ok gec_ok
gvt_mm gvt_ev gkt_mm gkt_ev ga_mm ga_ev go_mm go_ev gs_mm gs_ok
osq_ok orms_mm ostd_ok ymixb_ok
op_mm hy_ok mv1_ok sd1_ok h1_ok h1t_mm h1t_ev
q_mm q_ev sc_mm sc_ev
tk_ok ids_ok ge_ok
cur_ok kept_ok u_done gelu_ok act_ok diag_ok v_done fy_ok stored mv2_ok sd2_ok fo_ok out_done mix norm1 norm2 stood
""".split()
MIX = {n: i + 1 for i, n in enumerate("""
dif_ok difm_ok rin_ok kkn_ok kf1_ok kf_ok kb1_ok kx_ok rk1_ok tt0_ok gk_ok cg_ok yrs_ok yn2_ok yn3_ok yn4_ok ors_ok on_ok on2_ok
""".split())}
NMIX = len(MIX)


def w(eng, sem, b, k=1, n=1):
    eng.wait_ge(sem, b * n + k)


def rounds(eng, n, body):
    body(0)
    with eng.Fori(1, n) as i:
        body(i)


def named(**fields):
    return namedtuple("Named", fields)(**fields)


def hybrid_layer(nc, x, w_in, vec, cst, w2a2, g2, gkw2, lnrows, w_out, wq, keys, u_tab, v_tab, out):
    p_dram = nc.dram_tensor("p_dram", [NCH, P, PW], F32, kind="Internal").ap()
    h_dram = nc.dram_tensor("h_dram", [T, D], F32, kind="Internal").ap()
    with ExitStack() as ctx:
        sem = lambda n: ctx.enter_context(nc.semaphore(n))
        sems = lambda n, count: [sem(f"{n}{i}") for i in range(count)]
        s = named(w_in3=sems("w_in3_", 3), p_out3=sems("p_out3_", 3), u_in=sems("u_in", NU), v_in=sems("v_in", NV),
                  wq_b=sems("wq_b", 2), **{n: sem(n) for n in SIGNALS})
        psums = [ctx.enter_context(nc.psum_tensor(f"bank{i}", [P, 512], F32)) for i in range(8)]

        def sbin(stack):
            return lambda n, *shape, dt=F32: stack.enter_context(nc.sbuf_tensor(n, list(shape), dt))
        sb = sbin(ctx)
        k = named(vec=sb("vecs", P, NVEC), cst=sb("csts", P, NCST), w2a2=sb("w2a2s", P, 512),
                            g2=sb("g2s", P, 512), gkw2=sb("gkw2s", 16, 256), ln=sb("lns", P, 4, D),
                            keys=sb("keyss", P, 2 * PH, NKEY), omka=sb("omka", P, HP), eps=sb("epss", P, 3),
                            zero=sb("zero3", P, 4), ones=sb("ones", P, P))
        dram = named(x=x, w_in=w_in, vec=vec, cst=cst, w2a2=w2a2, g2=g2, gkw2=gkw2, lnrows=lnrows,
                               w_out=w_out, wq=wq, keys=keys, u=u_tab, v=v_tab, out=out, p=p_dram, h=h_dram)
        with ExitStack() as first:
            entry(nc, first, sbin(first), s, k, dram, psums)
        with ExitStack() as second:
            blocks(nc, second, sbin(second), s, k, dram, psums)


def entry(nc, ctx, sb, s, k, dram, ps):
    NT = T // P
    xs = sb("xs", P, NT, D)
    hT = sb("hT", P, ND, T)
    hs = sb("hs", P, 2, D)
    zs = sb("zs", P, 2, D)
    lni = sb("lni", P, 2, D)
    wb = [sb(f"wb{i}", P, ND, P) for i in range(3)]
    pe_out = [sb(f"pout{i}", P, T) for i in range(3)]
    st = sb("lst", P, 12)
    mv = sb("lmv", P, 2)
    sd = sb("lsd", P, 1)
    rs = sb("lrs", P, 1)
    hb = sb("hbuf", P, D)
    block = ctx.enter_context(nc.Block())

    @block.sync
    def _(sp):
        sp.dma_start(xs[:, :, :], dram.x.rearrange("(n p) d -> p n d", p=P)).then_inc(s.x_in, 16)
        for i in range(2):
            sp.dma_start(lni[:, i, :], dram.lnrows[i:i + 1, :].to_broadcast([P, D])).then_inc(s.lnin_in, 16)
        for dst, src in ((k.vec[:, :], dram.vec), (k.cst[:, :], dram.cst), (k.w2a2[:, :], dram.w2a2),
                         (k.g2[:, :], dram.g2), (k.gkw2[:, :], dram.gkw2)):
            sp.dma_start(dst, src).then_inc(s.par_in, 16)
        for i in range(3):
            sp.dma_start(wb[i][:, :, :], dram.w_in[i]).then_inc(s.w_in3[i], 16)
        def chunks(i):
            for j in range(3):
                sp.wait_ge(s.proj_mm, i * 3 + j + 1)
                sp.dma_start(wb[j][:, :, :], dram.w_in[bass.ds(i * 3 + j + 3, 1)].rearrange("o p d c -> (o p) d c")).then_inc(s.w_in3[j], 16)
        rounds(sp, NCH // 3 - 1, chunks)
        sp.dma_start(k.keys[:, :, :], dram.keys).then_inc(s.keys_in, 16)
        for i in range(4):
            sp.dma_start(k.ln[:, i, :], dram.lnrows[i + 2:i + 3, :].to_broadcast([P, D])).then_inc(s.keys_in, 16)

    @block.scalar
    def _(act):
        act.wait_ge(s.credits, 4)
        with nc.allow_non_contiguous_dma(reason="three zero tokens in front of every channel"):
            act.dma_start(dram.p[:, :, 0:PADC].rearrange("c p t -> p c t"), k.zero[:, 0:3].unsqueeze(1).to_broadcast([P, NCH, PADC])).then_inc(s.zpad_out, 16)
        act.wait_ge(s.zpad_out, 16)
        def tile(n):
            act.wait_ge(s.stat_mv, n + 1)
            act.activation(sd[:, :], mv[:, 1:2], ACT.Sqrt, bias=k.eps[:, 0:1]).then_inc(s.std_ok, 1)
            for j in range(2):
                act.wait_ge(s.htr_ok, n * 2 + j + 1)
                act.activation(hT[:, 4 * j:4 * j + 4, bass.ds(n * P, P)], ps[j][:, :].rearrange("p (d t) -> p d t", d=4), ACT.Copy).then_inc(s.hev_ok, 1)
            act.wait_ge(s.h_ok, n + 1)
            act.dma_start(dram.h[bass.ds(n * P, P), :], hb[:, :]).then_inc(s.h_out, 16)
        rounds(act, NT, tile)
        act.wait_ge(s.h_out, 16 * NT)
        def chunks(i):
            for j in range(3):
                act.wait_ge(s.proj_mm, i * 3 + j + 1)
                act.wait_ge(s.p_out3[j], i * 16)
                act.activation(pe_out[j][:, 0:512], ps[2 * j][:, :], ACT.Copy).then_inc(s.proj_ev, 1)
                act.wait_ge(s.p_stored, i * 3 + j + 1)
                act.wait_ge(s.proj_ev, i * 3 + j + 1)
                act.dma_start(dram.p[bass.ds(i * 3 + j, 1), :, PADC:PW].rearrange("o p t -> (o p) t"), pe_out[j][:, :]).then_inc(s.p_out3[j], 16)
        rounds(act, NCH // 3, chunks)
        for j in range(3):
            act.wait_ge(s.p_out3[j], 16 * (NCH // 3))

    @block.vector
    def _(dve):
        dve.memset(k.eps[:, 0:1], EPS).then_inc(s.credits, 1)
        dve.memset(k.eps[:, 1:2], GN_EPS).then_inc(s.credits, 1)
        dve.memset(k.eps[:, 2:3], 0.0).then_inc(s.credits, 1)
        dve.memset(k.zero[:, :], 0.0).then_inc(s.credits, 1)
        dve.wait_ge(s.x_in, 16)
        dve.wait_ge(s.lnin_in, 32)
        def tile(n):
            for j in range(2):
                dve.bn_stats(st[:, 6 * j:6 * j + 6], xs[:, bass.ds(n, 1), 512 * j:512 * j + 512]).then_inc(s.z_ok, 1)
            dve.wait_ge(s.z_ok, n * 3 + 2)
            dve.sem_inc(s.stood, 1)
            dve.bn_aggr(mv[:, :], st[:, :]).then_inc(s.stat_mv, 1)
            dve.wait_ge(s.std_ok, n + 1)
            dve.reciprocal(rs[:, :], sd[:, :]).then_inc(s.rstd_ok, 1)
            dve.wait_ge(s.rstd_ok, n + 1)
            dve.tensor_scalar(zs[:, 0, :], xs[:, bass.ds(n, 1), :], mv[:, 0:1], rs[:, :], ALU.subtract, ALU.mult).then_inc(s.z_ok, 1)
            dve.wait_ge(s.z_ok, n * 3 + 3)
            dve.tensor_tensor(zs[:, 1, :], zs[:, 0, :], lni[:, 0, :], ALU.mult).then_inc(s.zg_ok, 1)
            dve.wait_ge(s.zg_ok, n + 1)
            dve.wait_ge(s.h_out, n * 16)
            dve.wait_ge(s.htr_ok, n * 2)
            dve.tensor_tensor(hb[:, :], zs[:, 1, :], lni[:, 1, :], ALU.add).then_inc(s.h_ok, 1)
        rounds(dve, NT, tile)
        def chunks(i):
            for j in range(3):
                dve.wait_ge(s.proj_mm, i * 3 + j + 1)
                dve.wait_ge(s.p_out3[j], i * 16)
                dve.tensor_copy(pe_out[j][:, 512:1024], ps[2 * j + 1][:, :]).then_inc(s.p_stored, 1)
        rounds(dve, NCH // 3, chunks)

    @block.tensor
    def _(pe):
        pe.wait_ge(s.par_in, 80)
        def tile(n):
            pe.wait_ge(s.h_ok, n + 1)
            for j in range(2):
                pe.wait_ge(s.hev_ok, n * 2)
                for d in range(4):
                    ins = pe.transpose(ps[j][:, d * P:d * P + P], hb[:, (4 * j + d) * P:(4 * j + d) * P + P], k.cst[:, CID:CID + P])
                ins.then_inc(s.htr_ok, 1)
        rounds(pe, NT, tile)
        pe.wait_ge(s.hev_ok, 2 * NT)
        def chunks(i):
            for j in range(3):
                pe.wait_ge(s.w_in3[j], i * 16 + 16)
                pe.wait_ge(s.proj_ev, i * 3)
                pe.wait_ge(s.p_stored, i * 3)
                for half in range(2):
                    for d in range(ND):
                        ins = pe.matmul(ps[2 * j + half][:, :], wb[j][:, d, :], hT[:, d, half * 512:half * 512 + 512], start=(d == 0), stop=(d == ND - 1))
                ins.then_inc(s.proj_mm, 1)
        rounds(pe, NCH // 3, chunks)


def blocks(nc, ctx, sb, s, k, dram, ps):
    cst, vec = k.cst, k.vec
    F = [ps[0], ps[1]]
    A, B, Cb, Db, Eb, Fb = ps[2:8]

    praw = sb("praw", P, NCH, PRW)
    sh = sb("sh", P, NA, BT)
    cv = sb("cv", P, NQKV, BT)
    h1 = sb("h1", P, D)
    h1T = sb("h1T", P, ND, BT)
    wqb = [sb(f"wqb{i}", P, ND, P) for i in range(2)]
    ymix = sb("ymix", P, 2 * HP, BT)
    RK = sb("RK", P, 2, HP * NC2, 2, C)
    R2 = sb("R2", P, HP * NC2 * 2 * C)
    KB = R2[:, :].rearrange("p (q c s t) -> p q c s t", q=HP, c=NC2, s=2)
    th = sb("th", C, BT)
    sgd = sb("sgd", P, BT)
    sg = sb("sg", P, HP, BT)
    aa = sb("aa", P, HP, BT)
    gg = sb("gg", P, HP, BT)

    egp = sb("egp", P, HP, NC2, C + 1)
    en = sb("en", P, HP, NC2, C)
    kkn = sb("kkn", P, HP, NC2, C)
    kx = sb("kx", P, HP, NC2, C)
    bon = sb("bon", P, HP, BT)
    t1 = sb("t1", P, HP, BT)
    t2 = sb("t2", P, HP, BT)
    NTl = sb("NTl", P, 8, C)
    Ti = sb("Ti", P, 8, C)
    Tt = sb("Tt", P, 8, C)
    Z = sb("Z", P, 8, C)
    W = sb("W", P, 8, C)
    S = sb("S", P, HP, C)
    y = sb("y", P, HP, BT)
    cs = y[:, :, :].rearrange("p q t -> p (q t)")
    R1 = sb("R1", P, 4096)
    GT = R1[:, 0:2048].rearrange("p (c h q t) -> p c h q t", c=2, h=2, q=4)
    KBt = R1[:, 2048:3072].rearrange("p (c q t) -> p c q t", c=2, q=4)
    UV = R1[:, 3072:4096].rearrange("p (c h q t) -> p c h q t", c=2, h=2, q=4)
    gdE = R1[:, 0:1024].rearrange("p (m i t) -> p m i t", m=4, i=4)
    kE = R1[:, 1024:2048].rearrange("p (m i t) -> p m i t", m=4, i=4)
    Vt = R1[:, 2048:2560].rearrange("p (h t) -> p h t", h=4)
    kdt = R1[:, 2560:2816].rearrange("p (h t) -> p h t", h=2)

    o = R1[:, 3072:3584].rearrange("p (h t) -> p h t", h=4)
    o2 = R1[:, 3584:4096].rearrange("p (h t) -> p h t", h=4)
    scor = R1[:, 0:2048].rearrange("p (m t) -> p m t", m=16)
    scw = R1[:, 2048:2176]
    cand = R1[:, 2176:2432].rearrange("p (a b) -> p a b", a=16)
    candw = R1[:, 2432:2688]
    sif = R1[:, 2688:2944].rearrange("p (h q a) -> p h q a", h=8, q=2)
    cf = R1[:, 2944:3200].rearrange("p (q n) -> p q n", q=2)
    ef = R1[:, 3200:3456].rearrange("p (q n) -> p q n", q=2)
    oh = R2[:, :].rearrange("p (n a) -> p n a", a=TOPK)
    gsg = h1T[:, :, :].rearrange("p a b -> p (a b)")
    xg = sb("xg", P, 2 * BT)
    xa = sb("xa", P, 2 * BT)
    cg = sb("cg", P, 2 * BT)
    gq = sb("gq", P, 2 * BT)
    qI = sb("qI", P, 2, 4, C)
    qi = sb("qi", P, 2, 2, BT)
    At = sb("At", P, GH, BT)
    qe = R1[:, 2816:3072].rearrange("p (h t) -> p h t", h=2)
    kd = sb("kd", P, 2, BT)
    egc = sb("egc", P, 4)
    Sg = sb("Sg", P, 2, P)
    stt = sb("stt", P, 12)
    mv1 = sb("mv1", P, 2)
    sd1 = sb("sd1", P, 2)
    stf = sb("stf", P, 12)
    mv2 = sb("mv2", P, 2)
    sd2 = sb("sd2", P, 2)
    sv = sb("sv", P, 2 * PH, TOPK)
    si = sb("si", P, 2 * PH, TOPK, dt=U32)
    cval = sb("cval", P, PH, TOPK)
    ci = sb("ci", P, PH * TOPK, dt=U32)
    ca = sb("ca", P, 2, PH * TOPK, dt=U32)
    ids = sb("ids", P, PH * TOPK, dt=U32)
    gate = sb("gate", P, PH, TOPK)
    gsum = sb("gsum", P, 2, PH)
    h1c = sb("h1c", P, D)
    fin = sb("fin", P, D)
    idl = sb("idl", P, LATE, dt=U32)
    gatel = sb("gatel", P, TOPK)
    idc = sb("idc", P, PH * TOPK, dt=U32)
    gatec = sb("gatec", P, PH, TOPK)
    ur = [sb(f"ur{i}", P, D) for i in range(NU)]
    vr = [sb(f"vr{i}", P, D) for i in range(NV)]
    dots = sb("dots", P, 2, TOPK)
    gel = sb("gel", P, 2, TOPK)
    actg = sb("actg", P, 2, TOPK)
    diag = [sb(f"diag{i}", P, P) for i in range(ND4)]

    vb = lambda c: 64 * c
    ub = lambda c: 64 - 64 * c
    half = lambda h: slice(64 * h, 64 * h + 64)
    v4 = lambda col: vec[:, col:col + 4].unsqueeze(2).to_broadcast([P, 4, BT])
    f4 = lambda t: t[:, :].rearrange("p (a b) -> p a b", a=4)
    f8 = lambda t: t[:, :].rearrange("p (a b) -> p a b", a=8)
    m8 = lambda col: cst[:, col:col + C].unsqueeze(1).to_broadcast([P, 8, C])
    r_, k_, v_ = sh[:, CR:CR + 4, :], sh[:, CK:CK + 4, :], sh[:, CV:CV + 4, :]
    kk4 = kkn[:, :, :, :].rearrange("p q c t -> p q (c t)")
    kx4 = kx[:, :, :, :].rearrange("p q c t -> p q (c t)")
    en4 = en[:, :, :, :].rearrange("p q c t -> p q (c t)")
    cgm = cg[:, :].rearrange("p (m t) -> p m t", m=4)
    cg4 = cg[:, :].rearrange("p (m i t) -> p m i t", m=4, i=4)
    gq4 = gq[:, :].rearrange("p (m i t) -> p m i t", m=4, i=4)
    qT = [y[:, :, :], bon[:, :, :]]
    block = ctx.enter_context(nc.Block())

    def alone(eng):
        eng.sem_inc(s.stood, 1)

    def sp_mixer(sp, b):
        w(sp, s.ymixb_ok, b, 0)
        sp.dma_start(praw[:, :, :], dram.p[:, :, bass.ds(b * BT, PRW)].rearrange("c p t -> p c t")).then_inc(s.praw_in, 16)
        w(sp, s.cur_ok, b, 0, 3)
        sp.dma_start(h1[:, :], dram.h[bass.ds(b * BT, BT), :]).then_inc(s.hin_in, 16)
        for m in range(ND + 2 * PH):
            if m < 2:
                w(sp, s.q_mm, b, 0, 2 * PH)
            elif m < ND + 2:
                w(sp, s.op_mm, b, m - 1, ND)
            else:
                w(sp, s.q_mm, b, m - ND - 1, 2 * PH)
            sp.dma_start(wqb[m % 2][:, :, :], dram.w_out[m] if m < ND else dram.wq[m - ND]).then_inc(s.wq_b[m % 2], 16)

    def sp_experts(sp, b):
        w(sp, s.fo_ok, b)
        sp.dma_start(dram.out[bass.ds(b * BT, BT), :], fin[:, :]).then_inc(s.out_done, 16)

    def dve_gates(dve, b, to):
        to(24)
        dve.wait_ge(s.praw_in, b * 16 + 16)
        cur, prev = praw[:, 0:NA, PADC:PRW], praw[:, 0:NA, PADC - 1:PRW - 1]
        dve.tensor_tensor(sh[:, :, :], prev, cur, ALU.subtract).then_inc(s.mix, 1)
        to(24)
        for i in range(NQKV):
            ins = dve.tensor_scalar(cv[:, i, :], praw[:, CQB + i, 0:BT], vec[:, VCV + i:VCV + i + 1], None, ALU.mult)
        ins.then_inc(s.conv_ok, 1)
        to(25)
        w(dve, s.mix, b, MIX["dif_ok"], NMIX)
        dve.tensor_tensor(sh[:, :, :], sh[:, :, :], vec[:, VMU:VMU + NA].unsqueeze(2).to_broadcast([P, NA, BT]), ALU.mult).then_inc(s.mix, 1)
        to(26)
        w(dve, s.mix, b, MIX["difm_ok"], NMIX)
        dve.tensor_tensor(sh[:, :, :], sh[:, :, :], cur, ALU.add).then_inc(s.shift_ok, 1)
        to(27)
        for j in range(1, 4):
            to(27 + j)
            w(dve, s.conv_ok, b, j, 4)
            for i in range(NQKV):
                c = VCV + NQKV * j + i
                ins = dve.scalar_tensor_tensor(cv[:, i, :], praw[:, CQB + i, j:j + BT], vec[:, c:c + 1], cv[:, i, :], ALU.mult, ALU.add)
            ins.then_inc(s.conv_ok, 1)
        to(31)
        w(dve, s.shift_ok, b)
        dve.tensor_tensor(t1[:, :, :], k_, v4(VKK), ALU.mult).then_inc(s.kkr_ok, 1)
        to(31)
        w(dve, s.gkx_mm, b)
        dve.tensor_tensor(xg[:, :].rearrange("p (a t) -> p a t", a=2), Db[:, 0:256].rearrange("p (a t) -> p a t", a=2),
                          vec[:, VGKB:VGKB + 2].unsqueeze(2).to_broadcast([P, 2, BT]), ALU.add).then_inc(s.xg_ok, 1)
        to(32)
        w(dve, s.ss_mm, b)
        dve.tensor_scalar(t2[:, :, :], f4(Eb), 1e-24, None, ALU.max).then_inc(s.ssm_ok, 1)
        to(32)
        w(dve, s.ssq_ok, b)
        dve.reciprocal(t2[:, :, :], t2[:, :, :]).then_inc(s.mix, 1)
        to(33)
        w(dve, s.mix, b, MIX["rin_ok"], NMIX)
        dve.tensor_tensor(kk4, t1[:, :, :], t2[:, :, :], ALU.mult).then_inc(s.mix, 1)

    def dve_decays(dve, b, to):
        to(33)
        w(dve, s.sig_ok, b)
        dve.tensor_tensor_scan(cs, cst[:, CRS:CRS + 512], sg[:, :, :].rearrange("p a b -> p (a b)"), 0.0, ALU.mult, ALU.add).then_inc(s.csum_ok, 1)
        to(34)
        w(dve, s.a_ok, b)
        w(dve, s.mix, b, MIX["kkn_ok"], NMIX)
        dve.tensor_tensor(t2[:, :, :], aa[:, :, :], v4(VKA), ALU.mult).then_inc(s.mix, 1)
        to(34)
        w(dve, s.mix, b, MIX["kf1_ok"], NMIX)
        dve.tensor_tensor(t2[:, :, :], t2[:, :, :], k.omka[:, :].unsqueeze(2).to_broadcast([P, 4, BT]), ALU.add).then_inc(s.mix, 1)
        w(dve, s.mix, b, MIX["kf1_ok"], NMIX)
        to(35)
        dve.tensor_tensor(aa[:, :, :], aa[:, :, :], kk4, ALU.mult).then_inc(s.mix, 1)
        to(35)
        w(dve, s.mix, b, MIX["kf_ok"], NMIX)
        dve.tensor_tensor(kx4, k_, t2[:, :, :], ALU.mult).then_inc(s.mix, 1)
        to(35)
        w(dve, s.mix, b, MIX["kx_ok"], NMIX)
        dve.tensor_tensor(t1[:, :, :], r_, kx4, ALU.mult).then_inc(s.mix, 1)
        to(36)
        w(dve, s.egp_ok, b)

        e8 = egp[:, :, :, :].rearrange("p q c t -> p (q c) t")
        kk8 = kkn[:, :, :, :].rearrange("p q c t -> p (q c) t")
        for h in range(2):
            dve.scalar_tensor_tensor(RK[half(h), h, :, 0, :], kk8[half(h)], -1.0, e8[half(h), :, 0:C], ALU.mult, ALU.mult)
        to(36)
        w(dve, s.mix, b, MIX["rk1_ok"], NMIX)
        dve.tensor_tensor(t1[:, :, :], t1[:, :, :], v4(VRK), ALU.mult).then_inc(s.rk_ok, 1)
        to(36)
        for h in range(2):
            ins = dve.tensor_tensor(RK[half(h), h, :, 1, :], sh[half(h), CR:CR + 4, :].rearrange("p q (c t) -> p (q c) t", c=2), e8[half(h), :, 1:C + 1], ALU.mult)
        ins.then_inc(s.rkr_ok, 1)
        to(37)
        w(dve, s.en_ok, b)
        w(dve, s.mix, b, MIX["kb1_ok"], NMIX)
        a5 = aa[:, :, :].rearrange("p q (c t) -> p q c t", c=2)
        for c in range(NC2):
            dve.tensor_tensor(KB[:, :, c, c, :], kx[:, :, c, :], en[:, :, c, :], ALU.mult)
            ins = dve.tensor_tensor(KB[:, :, c, 1 - c, :], a5[:, :, c, :], en[:, :, c, :], ALU.mult)
        ins.then_inc(s.kbb_ok, 1)
        to(37)
        w(dve, s.bs_mm, b)
        dve.tensor_tensor(bon[:, :, :], f4(Fb), v_, ALU.mult).then_inc(s.bon_ok, 1)
        to(38)
        for c in range(NC2):
            to(38 + c)
            w(dve, s.vtr_mm, b, c + 1, 2)
            src = (A, B)[c][0:64, :].rearrange("p (q h v) -> p h q v", q=4, h=2)
            dve.memset(UV[ub(c):ub(c) + 64, c, :, :, :], 0.0)
            dve.tensor_copy(UV[vb(c):vb(c) + 64, c, :, :, :], src).then_inc(s.v_ev, 1)

    def dve_inverse(dve, b, to):
        for c in range(NC2):
            for h in range(2):
                i = 2 * c + h
                to(39 + i // 2)
                w(dve, s.gram_mm, b, i + 1, 4)
                dve.tensor_tensor(GT[:, c, h, :, :], f4((Eb, Fb, A, B)[i]), cst[:, CMG:CMG + P].unsqueeze(1).to_broadcast([P, 4, P]), ALU.mult).then_inc(s.gram_ev, 1)
        to(41)
        w(dve, s.gram_ev, b, 4, 4)
        for c in range(NC2):
            u = slice(ub(c), ub(c) + 64)
            ins = dve.tensor_tensor(Tt[u, :, :], GT[u, c, :, :, 0:C].rearrange("p h q t -> p (h q) t"),
                                    cst[u, CM0T:CM0T + C].unsqueeze(1).to_broadcast([64, 8, C]), ALU.mult)
        ins.then_inc(s.mix, 1)
        to(41)
        w(dve, s.nt_mm, b)
        dve.tensor_tensor(NTl[:, :, :], f8(Cb), m8(CML), ALU.mult).then_inc(s.ntl_ok, 1)
        to(42)
        w(dve, s.mix, b, MIX["tt0_ok"], NMIX)
        dve.tensor_tensor(Tt[:, :, :], Tt[:, :, :], m8(CI64), ALU.add).then_inc(s.tt_ok, 1)
        to(42)
        w(dve, s.ntl_ok, b, 1, 6)
        dve.tensor_tensor(Ti[:, :, :], NTl[:, :, :], m8(CI64), ALU.add).then_inc(s.t_ok, 1)
        for l in range(1, 6):
            to(38 + 5 * l)
            if l == 1:
                w(dve, s.t_ok, b, 1, 5)
            else:
                w(dve, s.zz_mm, b, l - 1, 5)
            dve.tensor_tensor(NTl[:, :, :], f8(Cb), m8(CML + C * l), ALU.mult).then_inc(s.ntl_ok, 1)
            if l > 1:
                dve_grow(dve, b, l - 1, to)
        dve_grow(dve, b, 5, to)

    def dve_grow(dve, b, l, to):
        to(42 + 5 * l)
        w(dve, s.ttm_mm, b, l, 5)
        if l < 5:
            w(dve, s.tm_mm, b, l, 4)
        dve.tensor_tensor(Tt[:, :, :], Tt[:, :, :], f8(Eb), ALU.add).then_inc(s.tt_ok, 1)
        if l < 5:
            dve.tensor_tensor(Ti[:, :, :], Ti[:, :, :], f8(Fb), ALU.add).then_inc(s.t_ok, 1)

    def dve_chunks(dve, b, to):
        for c in range(NC2):
            u = slice(ub(c), ub(c) + 64)
            to(68 + 5 * c)
            w(dve, s.umm, b, c + 1, 2)
            dve.tensor_copy(UV[u, c, :, :, :].rearrange("p h q t -> p (h q) t"), f8(B)[u, :, :]).then_inc(s.u_ev, 1)
            to(71 + 5 * c)
            w(dve, s.st_mm, b, c + 1, 2)
            dve.tensor_tensor(S[:, :, :], S[:, :, :], Eb[:, c * 256:c * 256 + 256].rearrange("p (q t) -> p q t", q=4), ALU.add).then_inc(s.sa_ok, 1)
            w(dve, s.sa_ok, b, c + 1, 2)
            dve.tensor_tensor(S[:, :, :], S[:, :, :], egp[:, :, c, C:C + 1].to_broadcast([P, 4, C]), ALU.mult).then_inc(s.s_ok, 1)
        to(77)
        w(dve, s.y_mm, b, 2, 2)
        dve.tensor_copy(y[:, :, :], f4(Db)).then_inc(s.y_ev, 1)
        to(78)
        w(dve, s.ymean_mm, b)
        w(dve, s.y_ev, b)
        dve.scalar_tensor_tensor(y[:, :, :], f4(Fb), -1.0 / C, y[:, :, :], ALU.mult, ALU.add).then_inc(s.yc_ok, 1)

    def dve_gla_parts(dve, b, to):
        to(80)
        w(dve, s.xl_ok, b)
        dve.scalar_tensor_tensor(xg[:, :], xg[:, :], 0.0, xa[:, :], ALU.min, ALU.subtract).then_inc(s.mix, 1)
        to(80)
        w(dve, s.mix, b, MIX["gk_ok"], NMIX)
        dve.tensor_tensor_scan(cg[:, :], cst[:, CRS:CRS + 256], xg[:, :], 0.0, ALU.mult, ALU.add).then_inc(s.mix, 1)
        to(81)
        w(dve, s.gsig_ok, b)
        dve.tensor_tensor(cv[:, :, :], cv[:, :, :], gsg.rearrange("p (a b) -> p a b", a=8), ALU.mult).then_inc(s.silu_ok, 1)
        to(82)
        w(dve, s.s_ok, b, 2, 2)
        w(dve, s.y_mm, b, 2, 2)
        w(dve, s.mix, b, MIX["cg_ok"], NMIX)
        dve.memset(R1[:, 0:1024], -30000.0).then_inc(s.gd1_ok, 1)
        w(dve, s.gd1_ok, b, 1, 2)
        to(82)
        dve.tensor_scalar(gdE[:, :, 0, 0:16], cgm[:, :, 0:16], -1.0, None, ALU.mult)
        for i in range(1, 4):
            n = 16 * i + 16
            ins = dve.tensor_tensor(gdE[:, :, i, 0:n], cgm[:, :, 16 * i - 1:16 * i].to_broadcast([P, 4, n]), cgm[:, :, 0:n], ALU.subtract)
        ins.then_inc(s.gd1_ok, 1)
        to(83)
        dve.tensor_copy(gq4[:, :, 0, :], cg4[:, :, 0, :])
        dve.tensor_tensor(gq4[:, :, 1:4, :], cg4[:, :, 1:4, :], cg4[:, :, 0:3, 15:16].to_broadcast([P, 4, 3, 16]), ALU.subtract).then_inc(s.gq1_ok, 1)
        dve.tensor_tensor(kd[:, :, :].rearrange("p q (c t) -> p (q c) t", c=2), cgm[:, :, C - 1:C].to_broadcast([P, 4, C]), cgm, ALU.subtract).then_inc(s.gl1_ok, 1)
        to(84)
        w(dve, s.gd1_ok, b, 2, 2)
        dve.tensor_scalar(R1[:, 0:1024], R1[:, 0:1024], GMAX, None, ALU.min).then_inc(s.gcl_ok, 1)
        to(84)
        w(dve, s.silu_ok, b)
        kg = cv[:, 2:4, :].rearrange("p q (c t) -> p (q c) t", c=2)
        w(dve, s.gex_ok, b)
        dve.tensor_tensor(kE, gdE, kg.unsqueeze(2).to_broadcast([P, 4, 4, C]), ALU.mult)
        to(85)
        w(dve, s.gqx_ok, b)
        for h in range(2):
            ins = dve.scalar_tensor_tensor(qI[half(h), h, :, :], cv[half(h), 0:2, :].rearrange("p q (c t) -> p (q c) t", c=2), 0.125, gq[half(h), :].rearrange("p (m t) -> p m t", m=4), ALU.mult, ALU.mult)
        ins.then_inc(s.gq_ok, 1)
        to(86)
        w(dve, s.gi_ok, b)
        for h in range(2):
            ins = dve.scalar_tensor_tensor(qi[half(h), h, :, :], cv[half(h), 0:2, :], 0.125, qe[half(h)], ALU.mult, ALU.mult)
        ins.then_inc(s.gqi_ok, 1)
        to(86)
        w(dve, s.gl_ok, b)
        dve.tensor_tensor(kd[:, :, :], kd[:, :, :], cv[:, 2:4, :], ALU.mult).then_inc(s.gkd_ok, 1)

    def dve_group_norm(dve, b, to):
        to(87)
        w(dve, s.ystd_ok, b)
        dve.reciprocal(t2[:, :, :], t2[:, :, :]).then_inc(s.mix, 1)
        w(dve, s.mix, b, MIX["yrs_ok"], NMIX)
        dve.tensor_tensor(y[:, :, :], y[:, :, :], t2[:, :, :], ALU.mult).then_inc(s.yn_ok, 1)
        to(88)
        w(dve, s.yn_ok, b)
        dve.tensor_tensor(y[:, :, :], y[:, :, :], v4(VGG), ALU.mult).then_inc(s.mix, 1)
        dve.tensor_tensor(bon[:, :, :], bon[:, :, :], v4(VGB), ALU.add).then_inc(s.mix, 1)
        to(89)
        w(dve, s.mix, b, MIX["yn2_ok"], NMIX)
        w(dve, s.mix, b, MIX["yn3_ok"], NMIX)
        dve.tensor_tensor(y[:, :, :], y[:, :, :], bon[:, :, :], ALU.add).then_inc(s.mix, 1)
        to(89)
        w(dve, s.mix, b, MIX["yn4_ok"], NMIX)
        dve.tensor_tensor(ymix[:, 0:HP, :], y[:, :, :], gg[:, :, :], ALU.mult)

    def dve_gla(dve, b, to):
        to(90)
        w(dve, s.ga_mm, b)
        for c in range(NC2):
            tc = slice(c * C, c * C + C)
            ins = dve.tensor_tensor(At[tc, :, tc], Fb[tc, 0:256].rearrange("p (h t) -> p h t", h=4), cst[tc, CMG + C:CMG + P].unsqueeze(1).to_broadcast([64, 4, C]), ALU.mult)
        ins.then_inc(s.ga_ev, 1)
        to(91)
        w(dve, s.gec_ok, b)
        for c in range(NC2):
            to(92 + 2 * c)
            w(dve, s.gs_mm, b, c + 1, 2)
            for q in range(2):
                ins = dve.scalar_tensor_tensor(Sg[:, q, :], Sg[:, q, :], egc[:, 2 * q + c:2 * q + c + 1], Eb[:, c * 256 + q * P:c * 256 + q * P + P], ALU.mult, ALU.add)
            ins.then_inc(s.gs_ok, 1)
        to(95)
        w(dve, s.go_mm, b, 2, 2)
        dve.tensor_copy(o, f4(Db)).then_inc(s.go_ev, 1)
        to(96)
        w(dve, s.ostd_ok, b)
        dve.reciprocal(t1[:, :, :], t1[:, :, :]).then_inc(s.mix, 1)
        w(dve, s.mix, b, MIX["ors_ok"], NMIX)
        w(dve, s.go_ev, b)
        dve.scalar_tensor_tensor(o, o, vec[:, VNG:VNG + 1], t1[:, :, :], ALU.mult, ALU.mult).then_inc(s.mix, 1)
        to(97)
        w(dve, s.gsil_ok, b)
        dve.tensor_tensor(t2[:, :, :], t2[:, :, :], praw[:, CGB:CGB + 4, PADC:PRW], ALU.mult).then_inc(s.mix, 1)
        w(dve, s.mix, b, MIX["on_ok"], NMIX)
        to(97)
        w(dve, s.mix, b, MIX["on2_ok"], NMIX)
        dve.tensor_tensor(ymix[:, HP:2 * HP, :], o, t2[:, :, :], ALU.mult).then_inc(s.ymixb_ok, 1)

    def dve_norm(dve, b, x, st, mv, sd, gamma, own, mv_ok, sd_ok, o_ok, to, place):
        for j in range(2):
            ins = dve.bn_stats(st[:, 6 * j:6 * j + 6], x[:, 512 * j:512 * j + 512])
        ins.then_inc(own, 1)
        w(dve, own, b, 1, 4)
        alone(dve)
        dve.bn_aggr(mv[:, :], st[:, :]).then_inc(mv_ok, 1)
        to(place)
        w(dve, sd_ok, b)
        dve.reciprocal(sd[:, 1:2], sd[:, 0:1]).then_inc(own, 1)
        w(dve, own, b, 2, 4)
        dve.tensor_scalar(x[:, :], x[:, :], mv[:, 0:1], sd[:, 1:2], ALU.subtract, ALU.mult).then_inc(own, 1)
        w(dve, own, b, 3, 4)
        dve.tensor_tensor(x[:, :], x[:, :], k.ln[:, gamma, :], ALU.mult).then_inc(own, 1)
        to(place + 1)
        w(dve, own, b, 4, 4)
        dve.tensor_tensor(x[:, :], x[:, :], k.ln[:, gamma + 1, :], ALU.add).then_inc(o_ok, 1)

    def dve_residual(dve, b, to):
        to(100)
        dve.wait_ge(s.hin_in, b * 16 + 16)
        for j in range(2):
            to(100 + j)
            w(dve, s.op_mm, b, 4 * j + 4, ND)
            dve.scalar_tensor_tensor(h1[:, 512 * j:512 * j + 512], h1[:, 512 * j:512 * j + 512], ALPHA, (B, Cb)[j][:, :], ALU.mult, ALU.add).then_inc(s.hy_ok, 1)
        to(102)
        w(dve, s.hy_ok, b, 2, 2)
        dve_norm(dve, b, h1, stt, mv1, sd1, 0, s.norm1, s.mv1_ok, s.sd1_ok, s.h1_ok, to, 103)

    def dve_top(dve, b, h, to):
        n = [16 * h]

        def step(ins):
            ins.then_inc(s.tk_ok, 1)
            n[0] += 1

        def done():
            to(109 + n[0] // 8)
            w(dve, s.tk_ok, b, n[0], 16 * PH)
            alone(dve)

        def top16(src, work, vals, idx):
            step(dve.max(vals[:, 0:8], src))
            done()
            step(dve.max_index(idx[:, 0:8], vals[:, 0:8], src))
            step(dve.match_replace(work, vals[:, 0:8], src, NEG))
            done()
            step(dve.max(vals[:, 8:16], work))
            done()
            step(dve.max_index(idx[:, 8:16], vals[:, 8:16], work))

        to(109 + 2 * h)
        w(dve, s.sc_ev, b, h // 2 + 1, 4)
        alone(dve)
        for p in range(2):
            m = 2 * h + p
            top16(scor[:, m, :], scw, sv[:, m, :], si[:, m, :])
        step(dve.tensor_tensor(cand, sv[:, 2 * h, :].unsqueeze(2).to_broadcast([P, 16, 16]), sv[:, 2 * h + 1, :].unsqueeze(1).to_broadcast([P, 16, 16]), ALU.add))
        done()
        top16(cand.rearrange("p a b -> p (a b)"), candw, cval[:, h, :], ci[:, 16 * h:16 * h + 16])
        assert n[0] == 16 * h + 16

    def dve_ids(dve, b, to):
        n = [0]

        def step(ins):
            ins.then_inc(s.ids_ok, 1)
            n[0] += 1

        def done():
            to(125 + n[0] // 7)
            w(dve, s.ids_ok, b, n[0], NIDS)

        w(dve, s.tk_ok, b, 16 * PH, 16 * PH)
        step(dve.tensor_tensor(gate[:, :, :], cval[:, :, :], cval[:, :, 0:1].to_broadcast([P, PH, TOPK]), ALU.subtract))
        step(dve.tensor_scalar(ca[:, 0, :], ci[:, :], 4, None, ALU.logical_shift_right))
        step(dve.tensor_scalar(ca[:, 1, :], ci[:, :], 15, None, ALU.bitwise_and))
        step(dve.tensor_copy(sif, si[:, :, :].rearrange("p (h q) a -> p h q a", q=2)))
        done()
        step(dve.tensor_copy(cf, ca[:, :, :]))
        io = cst[:, CIO:CIO + TOPK].unsqueeze(1).to_broadcast([P, P // 2, TOPK])
        oh4 = oh.rearrange("p (h n) a -> p h n a", h=PH // 2)
        for q in range(2):
            for j in range(2):
                hk, hh = slice(64 * j, 64 * j + 64), slice(4 * j, 4 * j + 4)
                done()
                step(dve.tensor_tensor(oh, cf[:, q, hk].unsqueeze(2).to_broadcast([P, P // 2, TOPK]), io, ALU.is_equal))
                done()
                step(dve.tensor_tensor(oh4, oh4, sif[:, hh, q, :].unsqueeze(2).to_broadcast([P, PH // 2, TOPK, TOPK]), ALU.mult))
                done()
                step(dve.tensor_reduce(ef[:, q, hk], oh, AX.X, ALU.add))
        done()
        step(dve.scalar_tensor_tensor(ids[:, :], ef[:, 0, :], float(NKEY), ef[:, 1, :], ALU.mult, ALU.add))
        w(dve, s.ge_ok, b)
        step(dve.tensor_reduce(gsum[:, 0, :], gate[:, :, :], AX.X, ALU.add))
        done()
        step(dve.reciprocal(gsum[:, 1, :], gsum[:, 0, :]))
        done()
        step(dve.tensor_tensor(gate[:, :, :], gate[:, :, :], gsum[:, 1, :].unsqueeze(2).to_broadcast([P, PH, TOPK]), ALU.mult))
        assert n[0] == NIDS

    def dve_take(dve, b):
        w(dve, s.ids_ok, b, NIDS, NIDS)
        if type(b) is not int:
            w(dve, s.kept_ok, b, 0, 3)
            dve.wait_ge(s.u_done, NU + b * P)
            dve.wait_ge(s.v_done, NV + b * P - LATE)
        dve.tensor_copy(h1c[:, :], h1[:, :]).then_inc(s.cur_ok, 1)
        dve.tensor_copy(idc[:, :], ids[:, :]).then_inc(s.cur_ok, 1)
        dve.tensor_copy(gatec[:, :, :], gate[:, :, :]).then_inc(s.cur_ok, 1)
        w(dve, s.cur_ok, b, 3, 3)

    def dve_keep(dve, b):
        w(dve, s.stored, b)
        dve.tensor_copy(fin[:, :], h1c[:, :]).then_inc(s.kept_ok, 1)
        dve.tensor_copy(idl[:, :], idc[:, P - LATE:P]).then_inc(s.kept_ok, 1)
        dve.tensor_copy(gatel[:, :], gatec[:, PH - 1, :]).then_inc(s.kept_ok, 1)

    def dve_dot(dve, b, g):
        dve.wait_ge(s.u_in[g % NU], (b * (P // NU) + g // NU + 1) * 16)
        u = ur[g % NU][:, :]
        dve.tensor_tensor_reduce(u, u, h1c[:, :], 1.0, 0.0, ALU.mult, ALU.add, dots[:, (g // TOPK) % 2, g % TOPK:g % TOPK + 1]).then_inc(s.u_done, 1)

    def dve_act(dve, b, h):
        w(dve, s.gelu_ok, b, h + 1, PH)
        dve.tensor_tensor(actg[:, h % 2, :], gel[:, h % 2, :], gatec[:, h, :] if h < PH - 1 else gatel[:, :], ALU.mult).then_inc(s.act_ok, 1)

    def dve_expert(dve, b, x):
        if x == P:
            dve_take(dve, b + 1)
        if x == X_KEEP:
            dve_keep(dve, b)
        if x < P:
            dve_dot(dve, b, x)
        else:
            dve_dot(dve, b + 1, x - P)
        if x % TOPK == 4:
            h = x // TOPK - 1
            if h < PH:
                dve_act(dve, b, h)
            else:
                dve_act(dve, b + 1, h - PH)

    def dve_final(dve, b):
        dve.wait_ge(s.v_done, NV + b * P + P)
        for j in range(2):
            ins = dve.scalar_tensor_tensor(fin[:, 512 * j:512 * j + 512], fin[:, 512 * j:512 * j + 512], ALPHA, F[j][:, :], ALU.mult, ALU.add)
        ins.then_inc(s.fy_ok, 1)
        w(dve, s.fy_ok, b, 2)
        dve_norm(dve, b, fin, stf, mv2, sd2, 2, s.norm2, s.mv2_ok, s.sd2_ok, s.fo_ok, idle, 0)

    def act_gates(act, b, to):
        to(28)
        w(act, s.shift_ok, b)
        act.activation(th[:, :], sh[0:64, CWA, :], ACT.Tanh).then_inc(s.th_ok, 1)
        act.activation(sgd[:, :], sh[:, CGD, :], ACT.Sigmoid).then_inc(s.sgd_ok, 1)
        to(29)
        w(act, s.z_mm, b)
        for i in range(4):
            ins = act.activation(sg[:, i, :], A[:, i * BT:i * BT + BT], ACT.Sigmoid, bias=vec[:, VW0 + i:VW0 + i + 1])
        ins.then_inc(s.sig_ok, 1)
        to(30)
        w(act, s.a_mm, b)
        for i in range(4):
            ins = act.activation(aa[:, i, :], B[:, i * BT:i * BT + BT], ACT.Sigmoid, bias=vec[:, VA0 + i:VA0 + i + 1])
        ins.then_inc(s.a_ok, 1)
        to(31)
        w(act, s.conv_ok, b, 4, 4)
        act.activation(gsg, cv[:, :, :].rearrange("p a b -> p (a b)"), ACT.Sigmoid).then_inc(s.gsig_ok, 1)
        to(31)
        w(act, s.g_mm, b)
        act.activation(gg[:, :, :], f4(Cb), ACT.Copy).then_inc(s.g_ok, 1)
        to(31)
        w(act, s.kkr_ok, b)
        act.activation(kk4, t1[:, :, :], ACT.Square).then_inc(s.sq_ok, 1)
        to(32)
        w(act, s.ssm_ok, b)
        act.activation(t2[:, :, :], t2[:, :, :], ACT.Sqrt, bias=k.eps[:, 2:3]).then_inc(s.ssq_ok, 1)
        to(34)
        w(act, s.csum_ok, b)
        act.activation(egp[:, :, :, 1:C + 1], cs[:, :].rearrange("p (q c t) -> p q c t", q=4, c=2), ACT.Exp, scale=-E05).then_inc(s.egp_ok, 1)
        to(34)
        act.activation(en[:, :, :, :], cs[:, :].rearrange("p (q c t) -> p q c t", q=4, c=2), ACT.Exp, scale=E05).then_inc(s.en_ok, 1)
        to(35)
        w(act, s.xg_ok, b)
        act.activation(xa[:, :], xg[:, :], ACT.Abs).then_inc(s.xa_ok, 1)
        w(act, s.xa_ok, b, 1, 2)
        act.activation(xa[:, :], xa[:, :], ACT.Exp, scale=-1.0).then_inc(s.xa_ok, 1)
        to(36)
        w(act, s.xa_ok, b, 2, 2)
        act.activation(xa[:, :], xa[:, :], ACT.Ln, bias=1.0).then_inc(s.xl_ok, 1)
        for c in range(NC2):
            to(38 + c)
            w(act, s.kbt_mm, b, c + 1, 2)
            act.activation(KBt[:, c, :, :], f4((Cb, Db)[c]), ACT.Copy).then_inc(s.kbt_ev, 1)

    def act_inverse(act, b, to):
        for l in range(1, 6):
            to(39 + 5 * l)
            w(act, s.zz_mm, b, l, 5)
            if l > 1:
                w(act, s.tm_mm, b, l - 1, 4)
            act.activation(Z[:, :, :], f8(Db), ACT.Copy).then_inc(s.zz_ev, 1)

    def act_chunks(act, b, to):
        for c in range(NC2):
            u = slice(ub(c), ub(c) + 64)
            to(67 + 5 * c)
            w(act, s.wmm, b, c + 1, 2)
            act.activation(W[u, :, :], f8(A)[u, :, :], ACT.Copy).then_inc(s.w_ev, 1)
        to(79)
        w(act, s.yc_ok, b)
        act.activation(t1[:, :, :], y[:, :, :], ACT.Square).then_inc(s.ysq_ok, 1)
        to(80)
        w(act, s.yvar_mm, b)
        act.activation(t2[:, :, :], f4(A), ACT.Sqrt, bias=k.eps[:, 1:2], scale=1.0 / C).then_inc(s.ystd_ok, 1)
        to(84)
        w(act, s.gcl_ok, b)
        act.activation(R1[:, 0:1024], R1[:, 0:1024], ACT.Exp, scale=1.0 / 16).then_inc(s.gex_ok, 1)
        to(85)
        w(act, s.gq1_ok, b)
        act.activation(gq[:, :], gq[:, :], ACT.Exp, scale=1.0 / 16).then_inc(s.gqx_ok, 1)
        to(85)
        act.activation(qe, cg[:, :].rearrange("p (q t) -> p q t", q=2), ACT.Exp, scale=1.0 / 16).then_inc(s.gi_ok, 1)
        to(86)
        w(act, s.gl1_ok, b)
        act.activation(kd[:, :, :], kd[:, :, :], ACT.Exp, scale=1.0 / 16).then_inc(s.gl_ok, 1)
        act.activation(egc[:, :], cgm[:, :, C - 1], ACT.Exp, scale=1.0 / 16).then_inc(s.gec_ok, 1)

    def act_gla(act, b, to):
        to(86)
        w(act, s.gvt_mm, b)
        act.activation(Vt, f4(B), ACT.Copy).then_inc(s.gvt_ev, 1)
        to(88)
        w(act, s.gkt_mm, b)
        act.activation(kdt, Cb[:, 0:256].rearrange("p (q t) -> p q t", q=2), ACT.Copy).then_inc(s.gkt_ev, 1)
        to(95)
        w(act, s.go_ev, b)
        act.activation(o2, o, ACT.Square).then_inc(s.osq_ok, 1)
        to(96)
        w(act, s.orms_mm, b)
        act.activation(t1[:, :, :], f4(A), ACT.Sqrt, bias=k.eps[:, 0:1], scale=1.0 / P).then_inc(s.ostd_ok, 1)
        to(97)
        w(act, s.yn_ok, b)
        act.activation(t2[:, :, :], praw[:, CGB:CGB + 4, PADC:PRW], ACT.Sigmoid).then_inc(s.gsil_ok, 1)

    def act_queries(act, b, to):
        to(103)
        w(act, s.mv1_ok, b)
        act.activation(sd1[:, 0:1], mv1[:, 1:2], ACT.Sqrt, bias=k.eps[:, 0:1]).then_inc(s.sd1_ok, 1)
        for j in range(2):
            to(105 + j)
            w(act, s.h1t_mm, b, j + 1, 2)
            act.activation(h1T[:, 4 * j:4 * j + 4, :], f4((Db, Eb)[j]), ACT.Copy).then_inc(s.h1t_ev, 1)
        for g in range(4):
            to(107 + 3 * g)
            w(act, s.q_mm, b, 4 * g + 4, 16)
            if g >= 2:
                w(act, s.sc_mm, b, g - 1, 4)
            act.activation(qT[g % 2], f4((Fb, A)[g % 2]), ACT.Copy).then_inc(s.q_ev, 1)
            to(108 + 3 * g)
            w(act, s.sc_mm, b, g + 1, 4)
            act.activation(scor[:, 4 * g:4 * g + 4, :], f4((B, Cb)[g % 2]), ACT.Copy).then_inc(s.sc_ev, 1)

    def act_softmax(act, b, to):
        to(125)
        w(act, s.ids_ok, b, 1, NIDS)
        act.activation(gate[:, :, :], gate[:, :, :], ACT.Exp).then_inc(s.ge_ok, 1)

    def act_gelu(act, b, h):
        act.wait_ge(s.u_done, NU + b * P + (h + 1) * TOPK)
        act.activation(gel[:, h % 2, :], dots[:, h % 2, :], ACT.Gelu).then_inc(s.gelu_ok, 1)

    def act_diag(act, b, g):
        w(act, s.act_ok, b, g // TOPK + 1, PH)
        act.wait_ge(s.v_done, b * P + g + 1)
        act.activation(diag[g % ND4][:, :], cst[:, CID:CID + P], ACT.Copy, scale=actg[:, (g // TOPK) % 2, g % TOPK:g % TOPK + 1]).then_inc(s.diag_ok, 1)

    def act_expert(act, b, x, last=False):
        act_diag(act, b, x - X0)
        if x % TOPK == 2:
            h = x // TOPK - 1
            if h < PH:
                act_gelu(act, b, h)
            elif not last:
                act_gelu(act, b + 1, h - PH)

    def act_final(act, b):
        w(act, s.mv2_ok, b)
        act.activation(sd2[:, 0:1], mv2[:, 1:2], ACT.Sqrt, bias=k.eps[:, 0:1]).then_inc(s.sd2_ok, 1)

    def mm(pe, out, l, r, start=True, stop=True):
        return pe.matmul(out, l, r, start=start, stop=stop)

    def pe_gates(pe, b, to):
        ident, ones2 = cst[:, CID:CID + P], cst[:, CBO:CBO + P]
        to(28)
        w(pe, s.th_ok, b)
        to(28)
        for i in range(4):
            ins = mm(pe, A[:, i * BT:i * BT + BT], k.w2a2[0:64, i * P:i * P + P], th[:, :])
        ins.then_inc(s.z_mm, 1)
        for i in range(4):
            ins = mm(pe, B[:, i * BT:i * BT + BT], k.w2a2[64:128, i * P:i * P + P], sh[64:128, CWA, :])
        ins.then_inc(s.a_mm, 1)
        to(30)
        w(pe, s.sgd_ok, b)
        for i in range(4):
            ins = mm(pe, Cb[:, i * BT:i * BT + BT], k.g2[:, i * P:i * P + P], sgd[:, :])
        ins.then_inc(s.g_mm, 1)
        for i in range(2):
            ins = mm(pe, Db[:, i * BT:i * BT + BT], k.gkw2[:, i * P:i * P + P], praw[0:16, CGK, PADC:PRW])
        ins.then_inc(s.gkx_mm, 1)
        to(31)
        w(pe, s.sq_ok, b)
        mm(pe, Eb[:, :], ones2, kk4.rearrange("p q t -> p (q t)")).then_inc(s.ss_mm, 1)
        to(36)
        w(pe, s.rk_ok, b)
        mm(pe, Fb[:, :], ones2, t1[:, :, :].rearrange("p q t -> p (q t)")).then_inc(s.bs_mm, 1)
        to(37)
        w(pe, s.a_ok, b)
        alone(pe)
        for c in range(NC2):
            for q in range(4):
                ins = pe.transpose((A, B)[c][0:64, q * P:q * P + P], sh[:, CV + q, c * C:c * C + C], ident)
            ins.then_inc(s.vtr_mm, 1)
        to(37)
        w(pe, s.g_ok, b)
        w(pe, s.xg_ok, b)
        w(pe, s.kbb_ok, b)
        for c in range(NC2):
            for q in range(4):
                ins = pe.transpose((Cb, Db)[c][:, q * P:q * P + P], KB[:, q, c, :, :].rearrange("p s t -> p (s t)"), ident)
            ins.then_inc(s.kbt_mm, 1)
        to(39)
        w(pe, s.rkr_ok, b)
        for c in range(NC2):
            for h in range(2):
                i = 2 * c + h
                to(39 + c)
                if i < 2:
                    w(pe, (s.ssm_ok, s.bon_ok)[i], b)
                else:
                    w(pe, s.v_ev, b, i - 1, 2)
                for q in range(4):
                    ins = mm(pe, (Eb, Fb, A, B)[i][:, q * P:q * P + P], KB[:, q, c, :, :].rearrange("p s t -> p (s t)"),
                             RK[:, h, 2 * q + c, :, :].rearrange("p s t -> p (s t)"))
                ins.then_inc(s.gram_mm, 1)
        to(41)
        w(pe, s.kbt_ev, b, 1, 2)
        alone(pe)
        for c in range(NC2):
            for h in range(2):
                for q in range(4):
                    m = (h * 4 + q) * C
                    ins = mm(pe, Cb[ub(c):ub(c) + 64, m:m + C], RK[:, h, 2 * q + c, 0, :], KB[:, q, c, 1 - c, :])
        ins.then_inc(s.nt_mm, 1)

    def each(fn):
        for c in range(NC2):
            for m in range(8):
                ins = fn(slice(ub(c), ub(c) + 64), m)
        return ins

    def pe_inverse(pe, b, to):
        for l in range(1, 6):
            to(38 + 5 * l)
            w(pe, s.tt_ok, b, l, 6)
            w(pe, s.t_ok, b, l, 5)
            w(pe, s.ntl_ok, b, l + 1, 6)
            if l == 1:
                w(pe, s.kbt_ev, b, 2, 2)
                w(pe, s.gram_ev, b, 4, 4)
            else:
                w(pe, s.zz_ev, b, l - 1, 5)
            alone(pe)
            each(lambda u, m: mm(pe, Db[u, m * C:m * C + C], NTl[u, m, :], Tt[u, m, :])).then_inc(s.zz_mm, 1)
            to(40 + 5 * l)
            w(pe, s.zz_ev, b, l, 5)
            alone(pe)
            each(lambda u, m: mm(pe, Eb[u, m * C:m * C + C], Ti[u, m, :], Z[u, m, :])).then_inc(s.ttm_mm, 1)
            to(41 + 5 * l)
            if l < 5:
                each(lambda u, m: mm(pe, Fb[u, m * C:m * C + C], Z[u, m, :], Ti[u, m, :])).then_inc(s.tm_mm, 1)

    def pe_chunks(pe, b, to):
        for c in range(NC2):
            u = slice(ub(c), ub(c) + 64)
            hq = [(h, q) for h in range(2) for q in range(4)]
            to(66 + 5 * c)
            w(pe, s.s_ok, b, c, 2)
            w(pe, s.v_ev, b, 2, 2)
            if c:
                w(pe, s.w_ev, b, 1, 2)
            alone(pe)
            for h, q in hq:
                m = (h * 4 + q) * C
                mm(pe, A[u, m:m + C], RK[:, h, 2 * q + c, 0, :], S[:, q, :], stop=False)
                ins = mm(pe, A[u, m:m + C], GT[:, c, h, q, 0:C], UV[:, c, h, q, :], start=False)
            ins.then_inc(s.wmm, 1)
            to(67 + 5 * c)
            w(pe, s.w_ev, b, c + 1, 2)
            w(pe, s.tt_ok, b, 6, 6)
            if c:
                w(pe, s.u_ev, b, 1, 2)
            alone(pe)
            for h, q in hq:
                m = h * 4 + q
                ins = mm(pe, B[u, m * C:m * C + C], Tt[u, m, :], W[u, m, :])
            ins.then_inc(s.umm, 1)
            to(69 + 5 * c)
            w(pe, s.u_ev, b, c + 1, 2)
            alone(pe)
            to(70 + 5 * c)
            for h, q in hq:
                col = q * BT + c * C
                mm(pe, Db[half(h), col:col + C], S[:, q, :], RK[:, h, 2 * q + c, 1, :], stop=False)
                ins = mm(pe, Db[half(h), col:col + C], UV[:, c, h, q, :], GT[:, c, h, q, C:2 * C], start=False)
            ins.then_inc(s.y_mm, 1)
            for h, q in hq:
                col = c * 256 + q * C
                ins = mm(pe, Eb[half(h), col:col + C], KBt[:, c, q, h * C:h * C + C], UV[:, c, h, q, :])
            ins.then_inc(s.st_mm, 1)
        to(78)
        w(pe, s.y_ev, b)
        w(pe, s.t_ok, b, 5, 5)
        mm(pe, Fb[:, :], cst[:, CBO:CBO + P], y[:, :, :].rearrange("p q t -> p (q t)")).then_inc(s.ymean_mm, 1)
        to(80)
        w(pe, s.ysq_ok, b)
        mm(pe, A[:, :], cst[:, CBO:CBO + P], t1[:, :, :].rearrange("p q t -> p (q t)")).then_inc(s.yvar_mm, 1)

    def pe_gla(pe, b, to):
        ident = cst[:, CID:CID + P]
        to(83)
        w(pe, s.silu_ok, b)
        w(pe, s.u_ev, b, 2, 2)
        for h in range(4):
            ins = pe.transpose(B[:, h * P:h * P + P], cv[:, 4 + h, :], ident)
        ins.then_inc(s.gvt_mm, 1)
        to(87)
        w(pe, s.gkd_ok, b)
        for q in range(2):
            ins = pe.transpose(Cb[:, q * P:q * P + P], kd[:, q, :], ident)
        ins.then_inc(s.gkt_mm, 1)
        to(88)
        w(pe, s.gq_ok, b)
        w(pe, s.yc_ok, b)
        alone(pe)
        for h in range(4):
            for c in range(NC2):
                m = (h // 2) * 2 + c
                to(88 + h // 2)
                for i in range(4):
                    col = h * C + 16 * i
                    ins = mm(pe, Fb[c * C:c * C + C, col:col + 16], kE[:, m, i, :], qI[:, h % 2, m, 16 * i:16 * i + 16])
        ins.then_inc(s.ga_mm, 1)
        to(90)
        w(pe, s.gqi_ok, b)
        w(pe, s.gvt_ev, b)
        w(pe, s.gkt_ev, b)
        w(pe, s.ga_ev, b)
        for c in range(NC2):
            to(91 + 2 * c)
            w(pe, s.gs_ok, b, c, 2)
            alone(pe)
            tc = slice(c * C, c * C + C)
            for h in range(4):
                col = h * P + c * C
                mm(pe, Db[:, col:col + C], Sg[:, h // 2, :], qi[:, h % 2, h // 2, tc], stop=False)
                ins = mm(pe, Db[:, col:col + C], Vt[:, h, :], At[:, h, tc], start=False)
            ins.then_inc(s.go_mm, 1)
            for h in range(4):
                col = c * 256 + (h // 2) * P
                ins = mm(pe, Eb[half(h % 2), col:col + P], kdt[tc, h // 2, (h % 2) * C:(h % 2) * C + C], Vt[tc, h, :])
            ins.then_inc(s.gs_mm, 1)
        to(95)
        w(pe, s.osq_ok, b)
        w(pe, s.ystd_ok, b)
        mm(pe, A[:, :], k.ones[:, :], o2.rearrange("p q t -> p (q t)")).then_inc(s.orms_mm, 1)

    def pe_out(pe, b, to):
        to(98)
        w(pe, s.ymixb_ok, b)
        for m in range(ND):
            to(98 + m // 3)
            pe.wait_ge(s.wq_b[m % 2], (b * NWB + m // 2 + 1) * 16)
            for c in range(ND):
                ins = mm(pe, (B, Cb)[m // 4][:, (m % 4) * P:(m % 4) * P + P], ymix[:, c, :], wqb[m % 2][:, c, :], start=c == 0, stop=c == ND - 1)
            ins.then_inc(s.op_mm, 1)
        to(105)
        w(pe, s.h1_ok, b)
        w(pe, s.gs_ok, b, 2, 2)
        w(pe, s.go_ev, b)
        for j in range(2):
            to(105 + j)
            for d in range(4):
                ins = pe.transpose((Db, Eb)[j][:, d * P:d * P + P], h1[:, (4 * j + d) * P:(4 * j + d) * P + P], cst[:, CID:CID + P])
            ins.then_inc(s.h1t_mm, 1)

    def pe_queries(pe, b, to):
        def queries(g):
            if g == 0:
                w(pe, s.h1t_ev, b, 2, 2)
                w(pe, s.ga_ev, b)
            if g == 1:
                w(pe, s.ostd_ok, b)
            if g >= 2:
                w(pe, s.q_ev, b, g - 1, 4)
            for i in range(4):
                m = 4 * g + i
                to(106 + 3 * g + i // 2)
                pe.wait_ge(s.wq_b[m % 2], (b * NWB + (ND + m) // 2 + 1) * 16)
                for d in range(ND):
                    ins = mm(pe, (Fb, A)[g % 2][:, i * P:i * P + P], wqb[m % 2][:, d, :], h1T[:, d, :], start=d == 0, stop=d == ND - 1)
                ins.then_inc(s.q_mm, 1)

        def scores(g):
            to(108 + 3 * g)
            w(pe, s.q_ev, b, g + 1, 4)
            if g < 2:
                w(pe, s.hy_ok, b, 2, 2)
            else:
                w(pe, s.sc_ev, b, g - 1, 4)
            for i in range(4):
                ins = mm(pe, (B, Cb)[g % 2][:, i * P:i * P + P], qT[g % 2][:, i, :], k.keys[:, 4 * g + i, :])
            ins.then_inc(s.sc_mm, 1)
        for g in range(4):
            queries(g)
            scores(g)

    def pe_value(pe, b, g):
        pe.wait_ge(s.v_in[g % NV], (b * (P // NV) + g // NV + 1) * 16)
        pe.wait_ge(s.diag_ok, b * P + g + 1)
        if g == 0:
            w(pe, s.fy_ok, b)
        for j in range(2):
            ins = mm(pe, F[j][:, :], diag[g % ND4][:, :], vr[g % NV][:, 512 * j:512 * j + 512], start=g == 0, stop=g == P - 1)
        ins.then_inc(s.v_done, 1)

    def gather_u(pool, b, g):
        pool.wait_ge(s.u_done, b * P + g + 1)
        alone(pool)
        pool.indirect_dma_start(ur[g % NU][:, :], None, dram.u, bass.IndirectOffsetOnAxis(idc[:, g:g + 1], 0)).then_inc(s.u_in[g % NU], 16)

    def gather_v(pool, b, g):
        pool.wait_ge(s.v_done, b * P + g + 1)
        if g == P - LATE:
            w(pool, s.kept_ok, b, 3, 3)
        alone(pool)
        i = idc[:, g:g + 1] if g < P - LATE else idl[:, g - P + LATE:g - P + LATE + 1]
        pool.indirect_dma_start(vr[g % NV][:, :], None, dram.v, bass.IndirectOffsetOnAxis(i, 0)).then_inc(s.v_in[g % NV], 16)

    def idle(x):
        pass

    def stream(first, last, step):
        done = [first]

        def to(x):
            while done[0] < min(x, last):
                step(done[0])
                done[0] += 1
        return to

    def of(fn, eng, b, g):
        if g < P:
            fn(eng, b, g)
        else:
            fn(eng, b + 1, g - P)

    @block.sync
    def _(sp):
        sp.sem_inc(s.stored, 1)
        sp_mixer(sp, 0)
        with sp.Fori(0, NBLK - 1) as b:
            sp_mixer(sp, b + 1)
            sp_experts(sp, b)
            sp.wait_ge(s.out_done, b * 16 + 16)
            sp.sem_inc(s.stored, 1)
        sp_experts(sp, NBLK - 1)
        sp.wait_ge(s.out_done, NBLK * 16)

    @block.scalar
    def _(act):
        def mixer(b, to):
            act_gates(act, b, to)
            act_inverse(act, b, to)
            act_chunks(act, b, to)
            act_gla(act, b, to)
            act_queries(act, b, to)
            act_softmax(act, b, to)

        w(act, s.credits, 0, NINIT)
        mixer(0, idle)
        act_gelu(act, 0, 0)
        with act.Fori(0, NBLK - 1) as b:
            to = stream(X0, X0 + P, lambda x: act_expert(act, b, x))
            mixer(b + 1, to)
            to(X0 + P)
            act_final(act, b)
        to = stream(X0, X0 + P, lambda x: act_expert(act, NBLK - 1, x, True))
        to(X0 + P)
        act_final(act, NBLK - 1)

    @block.vector
    def _(dve):
        def mixer(b, to):
            dve_gates(dve, b, to)
            dve_decays(dve, b, to)
            dve_inverse(dve, b, to)
            dve_chunks(dve, b, to)
            dve_gla_parts(dve, b, to)
            dve_group_norm(dve, b, to)
            dve_gla(dve, b, to)
            dve_residual(dve, b, to)
            for h in range(PH):
                dve_top(dve, b, h, to)
            dve_ids(dve, b, to)

        dve.memset(S[:, :, :], 0.0).then_inc(s.credits, 1)
        dve.memset(Sg[:, :, :], 0.0).then_inc(s.credits, 1)
        dve.memset(RK[:, :, :, :, :], 0.0)
        dve.memset(qI[:, :, :, :], 0.0)
        dve.memset(qi[:, :, :, :], 0.0)
        dve.memset(At[:, :, :], 0.0)
        dve.memset(egp[:, :, :, 0:1], 1.0).then_inc(s.credits, 1)
        dve.memset(k.ones[:, :], 1.0).then_inc(s.credits, 1)
        dve.tensor_scalar(k.omka[:, :], vec[:, VKA:VKA + 4], -1.0, 1.0, ALU.mult, ALU.add).then_inc(s.credits, 1)
        dve.memset(stt[:, 0:1], 0.0).then_inc(s.u_done, NU)
        dve.memset(stt[:, 1:2], 0.0).then_inc(s.v_done, NV)
        dve.memset(stt[:, 2:3], 0.0).then_inc(s.fy_ok, 1)
        w(dve, s.credits, 0, NINIT)
        mixer(0, idle)
        dve_take(dve, 0)
        for g in range(TOPK):
            dve_dot(dve, 0, g)
        for x in range(TOPK, X0):
            dve_expert(dve, 0, x)
        with dve.Fori(0, NBLK - 1) as b:
            to = stream(X0, X0 + P, lambda x: dve_expert(dve, b, x))
            mixer(b + 1, to)
            to(X0 + P)
            dve_final(dve, b)
        to = stream(X0, P, lambda x: dve_expert(dve, NBLK - 1, x))
        to(P)
        dve_act(dve, NBLK - 1, PH - 1)
        dve_final(dve, NBLK - 1)

    @block.tensor
    def _(pe):
        def mixer(b, to):
            pe_gates(pe, b, to)
            pe_inverse(pe, b, to)
            pe_chunks(pe, b, to)
            pe_gla(pe, b, to)
            pe_out(pe, b, to)
            pe_queries(pe, b, to)

        w(pe, s.credits, 0, NINIT)
        mixer(0, idle)
        with pe.Fori(0, NBLK - 1) as b:
            to = stream(X0, X0 + P, lambda x: pe_value(pe, b, x - X0))
            mixer(b + 1, to)
            to(X0 + P)
        for g in range(P):
            pe_value(pe, NBLK - 1, g)

    @block.gpsimd
    def _(pool):
        def step(b, x):
            if x == P:
                w(pool, s.cur_ok, b + 1, 3, 3)
            of(gather_u, pool, b, x)
            if x - VLAG >= TOPK:
                of(gather_v, pool, b, x - VLAG - TOPK)

        w(pool, s.cur_ok, 0, 3, 3)
        for x in range(X0):
            step(0, x)
        with pool.Fori(0, NBLK - 1) as b:
            for x in range(X0, X0 + P):
                step(b, x)
        for x in range(X0, P):
            step(NBLK - 1, x)
        for g in range(P - VLAG - TOPK, P):
            gather_v(pool, NBLK - 1, g)

_INS = ['x', 'w_in', 'vec', 'cst', 'w2a2', 'g2', 'gkw2', 'lnrows', 'w_out', 'wq', 'keys', 'u', 'v']


def _constants():
    import numpy as np
    c = np.zeros((P, NCST), np.float32)
    p = np.arange(P)
    q = p % C
    col = np.arange(C)
    c[:, CID:CID + P] = np.eye(P)
    c[:, CBO:CBO + P] = (p[:, None] // C == p[None, :] // C)
    c[:, CMG:CMG + C] = q[:, None] < col[None, :]
    c[:, CMG + C:CMG + 2 * C] = q[:, None] <= col[None, :]
    for l in range(6):
        s = 1 << l
        t, j = q[:, None], col[None, :]
        m = (t // (2 * s) == j // (2 * s)) & (t % (2 * s) >= s) & (j % (2 * s) < s)
        c[:, CML + l * C:CML + (l + 1) * C] = m
        if l == 0:
            c[:, CM0T:CM0T + C] = (j // 2 == t // 2) & (j % 2 == 1) & (t % 2 == 0)
    c[:, CI64:CI64 + C] = q[:, None] == col[None, :]
    c[:, CRS:CRS + 512] = (np.arange(512) % C != 0)[None, :]
    c[:, CIO:CIO + TOPK] = np.arange(TOPK)[None, :]
    return c


def kernel(**inputs):
    import numpy as np
    import concourse.bacc as bacc
    from concourse.bass_utils import run_bass_kernel_spmd

    a = {n: np.asarray(v) for n, v in inputs.items()}
    cols = lambda v: v.reshape(-1, P).T
    wi = a['w_in'][0]
    gk0 = CGK * P
    wi = np.concatenate([wi[:, :gk0 + P], wi[:, gk0 + 16:]], axis=1)
    vec = np.concatenate([cols(a['a_mu'][0]), cols(a['a_w0'][0]), cols(a['a_a0'][0]), cols(a['a_k_k'][0]), cols(a['a_k_a'][0]),
                          cols(a['a_r_k'][0].reshape(-1)), cols(a['a_gn_g'][0]), cols(a['a_gn_b'][0]),
                          cols(a['b_conv'][0].reshape(-1)), cols(a['b_gk_b'][0]), cols(a['b_norm_g'][0])], axis=1)
    arrays = {
        'x': a['x'][0],
        'w_in': wi.reshape(ND, P, NCH, P).transpose(2, 1, 0, 3),
        'vec': vec,
        'cst': _constants(),
        'w2a2': np.concatenate([a['a_w2'][0], a['a_a2'][0]], axis=0),
        'g2': a['a_g2'][0],
        'gkw2': a['b_gk_w2'][0],
        'lnrows': np.stack([a['ln_in_g'], a['ln_in_b'], a['ln1_g'][0], a['ln1_b'][0], a['ln2_g'][0], a['ln2_b'][0]]),
        'w_out': a['w_out'][0].reshape(ND, P, ND, P).transpose(2, 1, 0, 3),
        'wq': a['p_wq'][0].reshape(ND, P, 2 * PH, P).transpose(2, 1, 0, 3),
        'keys': a['p_keys'][0].reshape(2 * PH, NKEY, P).transpose(2, 0, 1),
        'u': a['p_u'][0],
        'v': a['p_v'][0],
    }
    nc = bacc.Bacc("TRN2", target_bir_lowering=False, num_devices=1)
    ins, args = {}, []
    for name in _INS:
        arr = np.ascontiguousarray(arrays[name])
        ins[f"in_{name}_dram"] = arr
        args.append(nc.dram_tensor(f"in_{name}_dram", arr.shape, mybir.dt.from_np(arr.dtype), kind="ExternalInput").ap())
    out = nc.dram_tensor("out_0_dram", (T, D), F32, kind="ExternalOutput").ap()
    hybrid_layer(nc, *args, out)
    r = run_bass_kernel_spmd(nc, [ins], core_ids=[0])
    return r.results[0]["out_0_dram"].reshape(1, T, D)
```

```python
from collections import namedtuple
from contextlib import ExitStack

import concourse.bass as bass
from concourse import mybir

F32 = mybir.dt.float32
U32 = mybir.dt.uint32
ALU = mybir.AluOpType
ACT = mybir.ActivationFunctionType
AX = mybir.AxisListType

P = 128
T = 1024
D = 1024
ND = D // P
BT = 128
NBLK = T // BT
C = 64
NC2 = BT // C
HP = 4
GH = 4
NCH = 27
PADC = 3
PW = T + PADC
PRW = BT + PADC
CR, CK, CV, CWA, CGD, CQB, CGK, CGB = 0, 4, 8, 12, 13, 14, 22, 23
NA = 14
NQKV = 8
EPS = 1e-5
GN_EPS = 64e-5
ALPHA = 2.0 ** 0.25
E05 = 0.6065306597126334
GMAX = 16.0 * 60.0
PH = 8
TOPK = 16
NKEY = 128
NU = 8
NV = 8
VLAG = 4
PLAG = 7
X0 = TOPK + PLAG
LATE = 2 * TOPK
X_KEEP, X_SUM, X_NORM = 41, X0 + 1, X0 + 3
LAST = NBLK - 1
NWB = (ND + 2 * PH) // 2
ND4 = 4
NEG = -3.0e38
NINIT = 9
NIDS = 21
NT = T // P
NRND = NCH // 3
REST = (T - BT) // 2

VMU, VW0, VA0, VKK, VKA, VRK, VGG, VGB, VCV, VGKB, VNG, NVEC = 0, 14, 18, 22, 26, 30, 34, 38, 42, 74, 76, 77
CID, CBO, CMG, CML, CM0T, CI64, CRS, CIO, NCST = 0, 128, 256, 384, 768, 832, 896, 1408, 1424

SIGNALS = """
x_in par_in keys_in lnin_in zpad_out stat_mv std_ok rstd_ok z_ok zg_ok h_ok htr_ok hev_ok h_out
x0_in x1_in ln_in proj_mm proj_ev
praw_in hin_in consts_ok
shift_ok conv_ok g_ok csum_ok egp_ok en_ok
kkr_ok sq_ok ssm_ok ssq_ok rk_ok bon_ok rkr_ok kbb_ok
xg_ok xa_ok xl_ok gsig_ok silu_ok gsil_ok
vtr_mm v_ev kbt_mm kbt_ev gram_mm gram_ev nt_mm ntl_ok tt_ok t_ok zz_mm zz_ev ttm_mm tm_mm
wmm w_ev umm u_ev y_mm y_ev st_mm sa_ok s_ok
ymean_mm yc_ok ysq_ok yvar_mm ystd_ok yn_ok
gd1_ok gcl_ok gq1_ok gq_ok gqi_ok gl1_ok gkd_ok
gvt_mm gvt_ev gkt_mm gkt_ev ga_mm ga_ev go_mm go_ev gs_mm gs_ok
osq_ok orms_mm ostd_ok ymixb_ok
op_mm hy_ok mv1_ok sd1_ok h1_ok h1t_mm h1t_ev
q_mm q_ev sc_mm sc_ev
tk_ok ids_ok ge_ok
cur_ok kept_ok u_done gelu_ok act_ok diag_ok v_done fy_ok mv2_ok sd2_ok fo_ok out_done
mix rates_ok gates_mm gexp norm1 norm2 stood
""".split()
MIX = {n: i + 1 for i, n in enumerate("""
dif_ok difm_ok rin_ok kkn_ok kf1_ok kf_ok kb1_ok kx_ok rk1_ok tt0_ok gk_ok cg_ok yrs_ok yn2_ok yn3_ok yn4_ok ors_ok on_ok on2_ok
""".split())}
NMIX = len(MIX)
RATES = {n: i + 1 for i, n in enumerate("th_ok sgd_ok sig_ok a_ok".split())}
NRATES = len(RATES)
GATES = {n: i + 1 for i, n in enumerate("z_mm a_mm g_mm gkx_mm ss_mm bs_mm".split())}
NGATES = len(GATES)
GEXP = {n: i + 1 for i, n in enumerate("gex_ok gqx_ok gi_ok gl_ok gec_ok".split())}
NGEXP = len(GEXP)


def w(eng, sem, b, k=1, n=1):
    eng.wait_ge(sem, b * n + k)


def rounds(eng, n, body):
    body(0)
    with eng.Fori(1, n) as i:
        body(i)


def named(**fields):
    return namedtuple("Named", fields)(**fields)


def hybrid_layer(nc, x, w_in, vec, cst, w2a2, g2, gkw2, lnrows, w_out, wq, keys, u_tab, v_tab, out):
    p_dram = nc.dram_tensor("p_dram", [NCH, P, PW], F32, kind="Internal").ap()
    h_dram = nc.dram_tensor("h_dram", [T, D], F32, kind="Internal").ap()
    with ExitStack() as ctx:
        sem = lambda n: ctx.enter_context(nc.semaphore(n))
        sems = lambda n, count: [sem(f"{n}{i}") for i in range(count)]
        s = named(w_in3=sems("w_in3_", 3), p_out3=sems("p_out3_", 3), w_rest=sems("w_rest", 3), p_rest=sems("p_rest", 3), u_in=sems("u_in", NU), v_in=sems("v_in", NV),
                  wq_b=sems("wq_b", 2), **{n: sem(n) for n in SIGNALS})
        psums = [ctx.enter_context(nc.psum_tensor(f"bank{i}", [P, 512], F32)) for i in range(8)]

        def sbin(stack):
            return lambda n, *shape, dt=F32: stack.enter_context(nc.sbuf_tensor(n, list(shape), dt))
        sb = sbin(ctx)
        k = named(vec=sb("vecs", P, NVEC), cst=sb("csts", P, NCST), w2a2=sb("w2a2s", P, 512),
                            g2=sb("g2s", P, 512), gkw2=sb("gkw2s", 16, 256),
                            keys=sb("keyss", P, 2 * PH, NKEY), omka=sb("omka", P, HP), eps=sb("epss", P, 3),
                            zero=sb("zero3", P, 4),
                            ring_u=sb("ring_u", P, NU, D), ones=sb("ones", P, P))
        dram = named(x=x, w_in=w_in, vec=vec, cst=cst, w2a2=w2a2, g2=g2, gkw2=gkw2, lnrows=lnrows,
                               w_out=w_out, wq=wq, keys=keys, u=u_tab, v=v_tab, out=out, p=p_dram, h=h_dram)
        with ExitStack() as first:
            entry(nc, first, sbin(first), s, k, dram, psums)
        with ExitStack() as second:
            blocks(nc, second, sbin(second), s, k, dram, psums)


def entry(nc, ctx, sb, s, k, dram, ps):
    xs = sb("xs", P, NT, D)
    hT = k.ring_u[:, :, :].rearrange("p r e -> p (r e)").rearrange("p (d t) -> p d t", d=ND)
    zs = sb("zs", P, 2, D)
    lni = sb("lni", P, 2, D)
    wb = [sb(f"wb{i}", P, ND, P) for i in range(3)]
    pe_out = [sb(f"pout{i}", P, BT) for i in range(3)]
    st = sb("lst", P, 12)
    mv = sb("lmv", P, 2)
    sd = sb("lsd", P, 1)
    rs = sb("lrs", P, 1)
    hb = sb("hbuf", P, D)
    block = ctx.enter_context(nc.Block())

    @block.sync
    def _(sp):
        xt = dram.x.rearrange("(n p) d -> p n d", p=P)
        sp.dma_start(xs[:, 0, :], xt[:, 0, :]).then_inc(s.x0_in, 16)
        for i in range(2):
            sp.dma_start(lni[:, i, :], dram.lnrows[i:i + 1, :].to_broadcast([P, D])).then_inc(s.lnin_in, 16)
        sp.dma_start(k.cst[:, :], dram.cst).then_inc(s.par_in, 16)
        sp.dma_start(xs[:, 1, :], xt[:, 1, :]).then_inc(s.x1_in, 16)
        for i in range(3):
            sp.dma_start(wb[i][:, :, :], dram.w_in[i]).then_inc(s.w_in3[i], 16)
        sp.dma_start(xs[:, 2:NT, :], xt[:, 2:NT, :]).then_inc(s.x_in, 16)
        for dst, src in ((k.vec[:, :], dram.vec), (k.w2a2[:, :], dram.w2a2), (k.g2[:, :], dram.g2), (k.gkw2[:, :], dram.gkw2)):
            sp.dma_start(dst, src).then_inc(s.keys_in, 16)
        def chunks(i):
            for j in range(3):
                sp.wait_ge(s.proj_mm, i * 3 + j + 1)
                sp.dma_start(wb[j][:, :, :], dram.w_in[bass.ds(i * 3 + j + 3, 1)].rearrange("o p d c -> (o p) d c")).then_inc(s.w_in3[j], 16)
        rounds(sp, NRND - 1, chunks)
        sp.dma_start(k.keys[:, :, :], dram.keys).then_inc(s.keys_in, 16)
        sp.wait_ge(s.keys_in, 16 * 5)

    @block.scalar
    def _(act):
        act.wait_ge(s.consts_ok, 4)
        with nc.allow_non_contiguous_dma(reason="three zero tokens in front of every channel"):
            act.dma_start(dram.p[:, :, 0:PADC].rearrange("c p t -> p c t"), k.zero[:, 0:3].unsqueeze(1).to_broadcast([P, NCH, PADC])).then_inc(s.zpad_out, 16)

        def deviation(n):
            act.wait_ge(s.stat_mv, n + 1)
            act.activation(sd[:, :], mv[:, 1:2], ACT.Sqrt, bias=k.eps[:, 0:1]).then_inc(s.std_ok, 1)

        def tile(n):
            act.wait_ge(s.h_ok, n + 1)
            act.dma_start(dram.h[bass.ds(n * P, P), :], hb[:, :]).then_inc(s.h_out, 16)
            for j in range(2):
                act.wait_ge(s.htr_ok, n * 2 + j + 1)
                act.activation(hT[:, 4 * j:4 * j + 4, bass.ds(n * P, P)], ps[j][:, :].rearrange("p (d t) -> p d t", d=4), ACT.Copy).then_inc(s.hev_ok, 1)

        def chunks(i):
            for j in range(3):
                act.wait_ge(s.proj_mm, i * 3 + j + 1)
                act.wait_ge(s.p_out3[j], i * 16)
                act.activation(pe_out[j][:, :], ps[2 + j][:, 0:BT], ACT.Copy).then_inc(s.proj_ev, 1)
                act.wait_ge(s.proj_ev, i * 3 + j + 1)
                act.dma_start(dram.p[bass.ds(i * 3 + j, 1), :, PADC:PADC + BT].rearrange("o p t -> (o p) t"), pe_out[j][:, :]).then_inc(s.p_out3[j], 16)

        def both(i):
            tile(i)
            deviation(i + 1)
            chunks(i)
        deviation(0)
        rounds(act, NT - 1, both)
        tile(NT - 1)
        chunks(NT - 1)
        chunks(NT)
        act.wait_ge(s.zpad_out, 16)
        act.wait_ge(s.h_out, 16 * NT)
        for j in range(3):
            act.wait_ge(s.p_out3[j], 16 * NRND)

    @block.vector
    def _(dve):
        dve.memset(k.eps[:, 0:1], EPS).then_inc(s.consts_ok, 1)
        dve.memset(k.eps[:, 1:2], GN_EPS).then_inc(s.consts_ok, 1)
        dve.memset(k.eps[:, 2:3], 0.0).then_inc(s.consts_ok, 1)
        dve.memset(k.zero[:, :], 0.0).then_inc(s.consts_ok, 1)
        dve.wait_ge(s.x0_in, 16)

        def tile(n):
            for j in range(2):
                dve.bn_stats(st[:, 6 * j:6 * j + 6], xs[:, bass.ds(n, 1), 512 * j:512 * j + 512]).then_inc(s.z_ok, 1)
            dve.wait_ge(s.z_ok, n * 3 + 2)
            dve.sem_inc(s.stood, 1)
            dve.bn_aggr(mv[:, :], st[:, :]).then_inc(s.stat_mv, 1)
            dve.wait_ge(s.std_ok, n + 1)
            dve.reciprocal(rs[:, :], sd[:, :]).then_inc(s.rstd_ok, 1)
            dve.wait_ge(s.rstd_ok, n + 1)
            dve.tensor_scalar(zs[:, 0, :], xs[:, bass.ds(n, 1), :], mv[:, 0:1], rs[:, :], ALU.subtract, ALU.mult).then_inc(s.z_ok, 1)
            dve.wait_ge(s.z_ok, n * 3 + 3)
            dve.wait_ge(s.lnin_in, 32)
            dve.tensor_tensor(zs[:, 1, :], zs[:, 0, :], lni[:, 0, :], ALU.mult).then_inc(s.zg_ok, 1)
            dve.wait_ge(s.zg_ok, n + 1)
            dve.wait_ge(s.h_out, n * 16)
            dve.wait_ge(s.htr_ok, n * 2)
            dve.tensor_tensor(hb[:, :], zs[:, 1, :], lni[:, 1, :], ALU.add).then_inc(s.h_ok, 1)
        tile(0)
        dve.wait_ge(s.x1_in, 16)
        tile(1)
        dve.wait_ge(s.x_in, 16)
        with dve.Fori(2, NT) as n:
            tile(n)

    @block.tensor
    def _(pe):
        pe.wait_ge(s.par_in, 16)

        def tile(n):
            pe.wait_ge(s.h_ok, n + 1)
            for j in range(2):
                pe.wait_ge(s.hev_ok, n * 2)
                for d in range(4):
                    ins = pe.transpose(ps[j][:, d * P:d * P + P], hb[:, (4 * j + d) * P:(4 * j + d) * P + P], k.cst[:, CID:CID + P])
                ins.then_inc(s.htr_ok, 1)

        def chunks(i):
            for j in range(3):
                pe.wait_ge(s.w_in3[j], i * 16 + 16)
                pe.wait_ge(s.proj_ev, i * 3)
                for d in range(ND):
                    ins = pe.matmul(ps[2 + j][:, 0:BT], wb[j][:, d, :], hT[:, d, 0:BT], start=(d == 0), stop=(d == ND - 1))
                ins.then_inc(s.proj_mm, 1)

        def both(i):
            tile(i)
            chunks(i)
        tile(0)
        pe.wait_ge(s.hev_ok, 2)
        chunks(0)
        with pe.Fori(1, NT) as i:
            both(i)
        chunks(NT)


def blocks(nc, ctx, sb, s, k, dram, ps):
    cst, vec = k.cst, k.vec
    F = [ps[0], ps[1]]
    A, B, Cb, Db, Eb, Fb = ps[2:8]

    praw = sb("praw", P, NCH, PRW)
    sh = sb("sh", P, NA, BT)
    cv = sb("cv", P, NQKV, BT)
    h1 = sb("h1", P, D)
    ln = sb("lns", P, 4, D)
    wqb = [sb(f"wqb{i}", P, ND, P) for i in range(2)]
    RK = sb("RK", P, 2, HP * NC2, 2, C)
    R2 = sb("R2", P, HP * NC2 * 2 * C)
    KB = R2[:, :].rearrange("p (q c s t) -> p q c s t", q=HP, c=NC2, s=2)
    gg = sb("gg", P, HP, BT)

    egp = sb("egp", P, HP, NC2, C + 1)
    bon = sb("bon", P, HP, BT)
    t1 = sb("t1", P, HP, BT)
    t2 = sb("t2", P, HP, BT)
    TZ = sb("TZ", P, 4 * HP * BT)
    NTl, Ti, Z, W = (TZ[:, i * 512:i * 512 + 512].rearrange("p (m t) -> p m t", m=8) for i in range(4))
    sg, aa = (TZ[:, i * 512:i * 512 + 512].rearrange("p (q t) -> p q t", q=HP) for i in (2, 3))
    ymix = TZ[:, 0:1024].rearrange("p (m t) -> p m t", m=2 * HP)
    h1T = TZ[:, 1024:2048].rearrange("p (m t) -> p m t", m=ND)
    gsg = TZ[:, 0:1024]
    TE = sb("TE", P, HP * BT)
    sgd, th = TE[:, 0:BT], TE[0:C, BT:2 * BT]
    Tt = TE[:, :].rearrange("p (m t) -> p m t", m=8)
    en = TE[:, :].rearrange("p (q c t) -> p q c t", q=HP, c=NC2)
    S = sb("S", P, HP, C)
    y = sb("y", P, HP, BT)
    cs = y[:, :, :].rearrange("p q t -> p (q t)")
    R1 = sb("R1", P, 4096)
    kkn, kx = (R1[:, i * 512:i * 512 + 512].rearrange("p (q c t) -> p q c t", q=HP, c=NC2) for i in range(2))
    GT = R1[:, 0:2048].rearrange("p (c h q t) -> p c h q t", c=2, h=2, q=4)
    KBt = R1[:, 2048:3072].rearrange("p (c q t) -> p c q t", c=2, q=4)
    UV = R1[:, 3072:4096].rearrange("p (c h q t) -> p c h q t", c=2, h=2, q=4)
    gdE = R1[:, 0:1024].rearrange("p (m i t) -> p m i t", m=4, i=4)
    kE = R1[:, 1024:2048].rearrange("p (m i t) -> p m i t", m=4, i=4)
    Vt = R1[:, 2048:2560].rearrange("p (h t) -> p h t", h=4)
    kdt = R1[:, 2560:2816].rearrange("p (h t) -> p h t", h=2)

    o = R1[:, 3072:3584].rearrange("p (h t) -> p h t", h=4)
    o2 = R1[:, 3584:4096].rearrange("p (h t) -> p h t", h=4)
    scor = R1[:, 0:2048].rearrange("p (m t) -> p m t", m=16)
    scw = R1[:, 2048:2176]
    cand = R1[:, 2176:2432].rearrange("p (a b) -> p a b", a=16)
    candw = R1[:, 2432:2688]
    hold = R1[:, 0:1024]
    sif = R1[:, 2688:2944].rearrange("p (h q a) -> p h q a", h=8, q=2)
    cf = R1[:, 2944:3200].rearrange("p (q n) -> p q n", q=2)
    ef = R1[:, 3200:3456].rearrange("p (q n) -> p q n", q=2)
    oh = R2[:, :].rearrange("p (n a) -> p n a", a=TOPK)
    xg = sb("xg", P, 2 * BT)
    xa = sb("xa", P, 2 * BT)
    cg, gq = R2[:, 0:2 * BT], R2[:, 2 * BT:4 * BT]
    qI = sb("qI", P, 2, 4, C)
    qi = sb("qi", P, 2, 2, BT)
    At = sb("At", P, GH, BT)
    qe = R1[:, 2816:3072].rearrange("p (h t) -> p h t", h=2)
    kd = R2[:, 4 * BT:6 * BT].rearrange("p (h t) -> p h t", h=2)
    egc = sb("egc", P, 4)
    Sg = sb("Sg", P, 2, P)
    stt = sb("stt", P, 12)
    mv1 = sb("mv1", P, 2)
    sd1 = sb("sd1", P, 2)
    stf = sb("stf", P, 12)
    mv2 = sb("mv2", P, 2)
    sd2 = sb("sd2", P, 2)
    sv = R1[:, 3456:3712].rearrange("p (m a) -> p m a", m=2 * PH)
    si = sb("si", P, 2 * PH, TOPK, dt=U32)
    cval = R1[:, 3712:3840].rearrange("p (h a) -> p h a", h=PH)
    ci = sb("ci", P, PH * TOPK, dt=U32)
    ca = sb("ca", P, 2, PH * TOPK, dt=U32)
    ids = sb("ids", P, PH * TOPK, dt=U32)
    gate = sb("gate", P, PH, TOPK)
    gsum = sb("gsum", P, 2, PH)
    h1c = sb("h1c", P, D)
    idl = sb("idl", P, LATE, dt=U32)
    gatel = sb("gatel", P, TOPK)
    idc = sb("idc", P, PH * TOPK, dt=U32)
    gatec = sb("gatec", P, PH, TOPK)
    ur = [k.ring_u[:, i, :] for i in range(NU)]
    vr = [sb(f"vr{i}", P, D) for i in range(NV)]
    hT = k.ring_u[:, :, :].rearrange("p r e -> p (r e)").rearrange("p (d t) -> p d t", d=ND)
    wip = [vr[i][:, :].rearrange("p (d c) -> p d c", d=ND) for i in range(3)]
    pst = [vr[3 + i][:, 0:REST] for i in range(3)]
    dots = sb("dots", P, 2, TOPK)
    gel = sb("gel", P, 2, TOPK)
    actg = sb("actg", P, 2, TOPK)
    diag = [sb(f"diag{i}", P, P) for i in range(ND4)]

    vb = lambda c: 64 * c
    ub = lambda c: 64 - 64 * c
    half = lambda h: slice(64 * h, 64 * h + 64)
    v4 = lambda col: vec[:, col:col + 4].unsqueeze(2).to_broadcast([P, 4, BT])
    f4 = lambda t: t[:, :].rearrange("p (a b) -> p a b", a=4)
    f8 = lambda t: t[:, :].rearrange("p (a b) -> p a b", a=8)
    m8 = lambda col: cst[:, col:col + C].unsqueeze(1).to_broadcast([P, 8, C])
    r_, k_, v_ = sh[:, CR:CR + 4, :], sh[:, CK:CK + 4, :], sh[:, CV:CV + 4, :]
    kk4 = kkn[:, :, :, :].rearrange("p q c t -> p q (c t)")
    kx4 = kx[:, :, :, :].rearrange("p q c t -> p q (c t)")
    cgm = cg[:, :].rearrange("p (m t) -> p m t", m=4)
    cg4 = cg[:, :].rearrange("p (m i t) -> p m i t", m=4, i=4)
    gq4 = gq[:, :].rearrange("p (m i t) -> p m i t", m=4, i=4)
    qT = [y[:, :, :], bon[:, :, :]]
    block = ctx.enter_context(nc.Block())

    def alone(eng):
        eng.sem_inc(s.stood, 1)

    def sp_projections(sp, b):
        w(sp, s.ymixb_ok, b, 0)
        sp.dma_start(praw[:, :, :], dram.p[:, :, bass.ds(b * BT, PRW)].rearrange("c p t -> p c t")).then_inc(s.praw_in, 16)

    def sp_weights(sp, b):
        w(sp, s.cur_ok, b, 0, 3)
        sp.dma_start(h1[:, :], dram.h[bass.ds(b * BT, BT), :]).then_inc(s.hin_in, 16)
        if type(b) is int and b == 0:
            for i in range(4):
                sp.dma_start(ln[:, i, :], dram.lnrows[i + 2:i + 3, :].to_broadcast([P, D])).then_inc(s.ln_in, 16)
        for m in range(ND + 2 * PH):
            if m < 2:
                w(sp, s.q_mm, b, 0, 2 * PH)
            elif m < ND + 2:
                w(sp, s.op_mm, b, m - 1, ND)
            else:
                w(sp, s.q_mm, b, m - ND - 1, 2 * PH)
            sp.dma_start(wqb[m % 2][:, :, :], dram.w_out[m] if m < ND else dram.wq[m - ND]).then_inc(s.wq_b[m % 2], 16)

    def sp_output(sp, b):
        w(sp, s.fo_ok, b)
        sp.dma_start(dram.out[bass.ds(b * BT, BT), :], h1[:, :]).then_inc(s.out_done, 16)
        w(sp, s.out_done, b, 16, 16)
        alone(sp)

    def dve_gates(dve, b, to):
        to(1)
        dve.wait_ge(s.praw_in, b * 16 + 16)
        cur, prev = praw[:, 0:NA, PADC:PRW], praw[:, 0:NA, PADC - 1:PRW - 1]
        dve.tensor_tensor(sh[:, :, :], prev, cur, ALU.subtract).then_inc(s.mix, 1)
        to(1)
        for i in range(NQKV):
            ins = dve.tensor_scalar(cv[:, i, :], praw[:, CQB + i, 0:BT], vec[:, VCV + i:VCV + i + 1], None, ALU.mult)
        ins.then_inc(s.conv_ok, 1)
        to(2)
        w(dve, s.mix, b, MIX["dif_ok"], NMIX)
        dve.tensor_tensor(sh[:, :, :], sh[:, :, :], vec[:, VMU:VMU + NA].unsqueeze(2).to_broadcast([P, NA, BT]), ALU.mult).then_inc(s.mix, 1)
        to(2)
        w(dve, s.mix, b, MIX["difm_ok"], NMIX)
        dve.tensor_tensor(sh[:, :, :], sh[:, :, :], cur, ALU.add).then_inc(s.shift_ok, 1)
        to(3)
        for j in range(1, 4):
            to(3 + j)
            w(dve, s.conv_ok, b, j, 4)
            for i in range(NQKV):
                c = VCV + NQKV * j + i
                ins = dve.scalar_tensor_tensor(cv[:, i, :], praw[:, CQB + i, j:j + BT], vec[:, c:c + 1], cv[:, i, :], ALU.mult, ALU.add)
            ins.then_inc(s.conv_ok, 1)
        to(6)
        w(dve, s.shift_ok, b)
        dve.tensor_tensor(t1[:, :, :], k_, v4(VKK), ALU.mult).then_inc(s.kkr_ok, 1)
        to(7)
        w(dve, s.gates_mm, b, GATES["gkx_mm"], NGATES)
        dve.tensor_tensor(xg[:, :].rearrange("p (a t) -> p a t", a=2), Db[:, 0:256].rearrange("p (a t) -> p a t", a=2),
                          vec[:, VGKB:VGKB + 2].unsqueeze(2).to_broadcast([P, 2, BT]), ALU.add).then_inc(s.xg_ok, 1)
        to(8)
        w(dve, s.gates_mm, b, GATES["ss_mm"], NGATES)
        dve.tensor_scalar(t2[:, :, :], f4(Eb), 1e-24, None, ALU.max).then_inc(s.ssm_ok, 1)
        to(9)
        w(dve, s.ssq_ok, b)
        dve.reciprocal(t2[:, :, :], t2[:, :, :]).then_inc(s.mix, 1)
        to(9)
        w(dve, s.mix, b, MIX["rin_ok"], NMIX)
        dve.tensor_tensor(kk4, t1[:, :, :], t2[:, :, :], ALU.mult).then_inc(s.mix, 1)

    def dve_decays(dve, b, to):
        to(10)
        w(dve, s.rates_ok, b, RATES["sig_ok"], NRATES)
        dve.tensor_tensor_scan(cs, cst[:, CRS:CRS + 512], sg[:, :, :].rearrange("p a b -> p (a b)"), 0.0, ALU.mult, ALU.add).then_inc(s.csum_ok, 1)
        to(10)
        w(dve, s.rates_ok, b, RATES["a_ok"], NRATES)
        w(dve, s.mix, b, MIX["kkn_ok"], NMIX)
        dve.tensor_tensor(t2[:, :, :], aa[:, :, :], v4(VKA), ALU.mult).then_inc(s.mix, 1)
        to(10)
        w(dve, s.mix, b, MIX["kf1_ok"], NMIX)
        dve.tensor_tensor(t2[:, :, :], t2[:, :, :], k.omka[:, :].unsqueeze(2).to_broadcast([P, 4, BT]), ALU.add).then_inc(s.mix, 1)
        w(dve, s.mix, b, MIX["kf1_ok"], NMIX)
        to(10)
        dve.tensor_tensor(aa[:, :, :], aa[:, :, :], kk4, ALU.mult).then_inc(s.mix, 1)
        to(11)
        w(dve, s.mix, b, MIX["kf_ok"], NMIX)
        dve.tensor_tensor(kx4, k_, t2[:, :, :], ALU.mult).then_inc(s.mix, 1)
        to(11)
        w(dve, s.mix, b, MIX["kx_ok"], NMIX)
        dve.tensor_tensor(t1[:, :, :], r_, kx4, ALU.mult).then_inc(s.mix, 1)
        to(12)
        w(dve, s.egp_ok, b)

        e8 = egp[:, :, :, :].rearrange("p q c t -> p (q c) t")
        kk8 = kkn[:, :, :, :].rearrange("p q c t -> p (q c) t")
        for h in range(2):
            dve.scalar_tensor_tensor(RK[half(h), h, :, 0, :], kk8[half(h)], -1.0, e8[half(h), :, 0:C], ALU.mult, ALU.mult)
        to(12)
        w(dve, s.mix, b, MIX["rk1_ok"], NMIX)
        dve.tensor_tensor(t1[:, :, :], t1[:, :, :], v4(VRK), ALU.mult).then_inc(s.rk_ok, 1)
        to(12)
        for h in range(2):
            ins = dve.tensor_tensor(RK[half(h), h, :, 1, :], sh[half(h), CR:CR + 4, :].rearrange("p q (c t) -> p (q c) t", c=2), e8[half(h), :, 1:C + 1], ALU.mult)
        ins.then_inc(s.rkr_ok, 1)
        to(13)
        w(dve, s.en_ok, b)
        w(dve, s.mix, b, MIX["kb1_ok"], NMIX)
        a5 = aa[:, :, :].rearrange("p q (c t) -> p q c t", c=2)
        for c in range(NC2):
            dve.tensor_tensor(KB[:, :, c, c, :], kx[:, :, c, :], en[:, :, c, :], ALU.mult)
            ins = dve.tensor_tensor(KB[:, :, c, 1 - c, :], a5[:, :, c, :], en[:, :, c, :], ALU.mult)
        ins.then_inc(s.kbb_ok, 1)
        to(13)
        w(dve, s.gsig_ok, b)
        dve.tensor_tensor(cv[:, :, :], cv[:, :, :], gsg.rearrange("p (a b) -> p a b", a=8), ALU.mult).then_inc(s.silu_ok, 1)
        to(14)
        w(dve, s.gates_mm, b, GATES["bs_mm"], NGATES)
        dve.tensor_tensor(bon[:, :, :], f4(Fb), v_, ALU.mult).then_inc(s.bon_ok, 1)
        to(14)
        for c in range(NC2):
            to(15 + c)
            w(dve, s.vtr_mm, b, c + 1, 2)
            src = (A, B)[c][0:64, :].rearrange("p (q h v) -> p h q v", q=4, h=2)
            dve.memset(UV[ub(c):ub(c) + 64, c, :, :, :], 0.0)
            dve.tensor_copy(UV[vb(c):vb(c) + 64, c, :, :, :], src).then_inc(s.v_ev, 1)

    def dve_inverse(dve, b, to):
        for c in range(NC2):
            for h in range(2):
                i = 2 * c + h
                to(17 + i // 2)
                w(dve, s.gram_mm, b, i + 1, 4)
                dve.tensor_tensor(GT[:, c, h, :, :], f4((Eb, Fb, A, B)[i]), cst[:, CMG:CMG + P].unsqueeze(1).to_broadcast([P, 4, P]), ALU.mult).then_inc(s.gram_ev, 1)
        to(19)
        w(dve, s.gram_ev, b, 4, 4)
        for c in range(NC2):
            u = slice(ub(c), ub(c) + 64)
            ins = dve.tensor_tensor(Tt[u, :, :], GT[u, c, :, :, 0:C].rearrange("p h q t -> p (h q) t"),
                                    cst[u, CM0T:CM0T + C].unsqueeze(1).to_broadcast([64, 8, C]), ALU.mult)
        ins.then_inc(s.mix, 1)
        to(19)
        w(dve, s.nt_mm, b)
        w(dve, s.silu_ok, b)
        dve.tensor_tensor(NTl[:, :, :], f8(Cb), m8(CML), ALU.mult).then_inc(s.ntl_ok, 1)
        to(19)
        w(dve, s.mix, b, MIX["tt0_ok"], NMIX)
        dve.tensor_tensor(Tt[:, :, :], Tt[:, :, :], m8(CI64), ALU.add).then_inc(s.tt_ok, 1)
        to(19)
        w(dve, s.ntl_ok, b, 1, 6)
        dve.tensor_tensor(Ti[:, :, :], NTl[:, :, :], m8(CI64), ALU.add).then_inc(s.t_ok, 1)
        for l in range(1, 6):
            to(13 + 5 * l)
            if l == 1:
                w(dve, s.t_ok, b, 1, 5)
            else:
                w(dve, s.zz_mm, b, l - 1, 5)
            dve.tensor_tensor(NTl[:, :, :], f8(Cb), m8(CML + C * l), ALU.mult).then_inc(s.ntl_ok, 1)
            if l > 1:
                dve_grow(dve, b, l - 1, to)
        dve_grow(dve, b, 5, to)

    def dve_grow(dve, b, l, to):
        to(19 + 5 * l)
        w(dve, s.ttm_mm, b, l, 5)
        if l < 5:
            w(dve, s.tm_mm, b, l, 4)
        dve.tensor_tensor(Tt[:, :, :], Tt[:, :, :], f8(Eb), ALU.add).then_inc(s.tt_ok, 1)
        if l < 5:
            dve.tensor_tensor(Ti[:, :, :], Ti[:, :, :], f8(Fb), ALU.add).then_inc(s.t_ok, 1)

    def dve_chunks(dve, b, to):
        for c in range(NC2):
            u = slice(ub(c), ub(c) + 64)
            to(46 + 5 * c)
            w(dve, s.umm, b, c + 1, 2)
            dve.tensor_copy(UV[u, c, :, :, :].rearrange("p h q t -> p (h q) t"), f8(B)[u, :, :]).then_inc(s.u_ev, 1)
            to(49 + 5 * c)
            w(dve, s.st_mm, b, c + 1, 2)
            dve.tensor_tensor(S[:, :, :], S[:, :, :], Eb[:, c * 256:c * 256 + 256].rearrange("p (q t) -> p q t", q=4), ALU.add).then_inc(s.sa_ok, 1)
            w(dve, s.sa_ok, b, c + 1, 2)
            dve.tensor_tensor(S[:, :, :], S[:, :, :], egp[:, :, c, C:C + 1].to_broadcast([P, 4, C]), ALU.mult).then_inc(s.s_ok, 1)
        to(54)
        w(dve, s.y_mm, b, 2, 2)
        dve.tensor_copy(y[:, :, :], f4(Db)).then_inc(s.y_ev, 1)
        to(55)
        w(dve, s.ymean_mm, b)
        w(dve, s.y_ev, b)
        dve.scalar_tensor_tensor(y[:, :, :], f4(Fb), -1.0 / C, y[:, :, :], ALU.mult, ALU.add).then_inc(s.yc_ok, 1)

    def dve_gla_parts(dve, b, to):
        to(56)
        w(dve, s.xl_ok, b)
        dve.scalar_tensor_tensor(xg[:, :], xg[:, :], 0.0, xa[:, :], ALU.min, ALU.subtract).then_inc(s.mix, 1)
        to(56)
        w(dve, s.mix, b, MIX["gk_ok"], NMIX)
        dve.tensor_tensor_scan(cg[:, :], cst[:, CRS:CRS + 256], xg[:, :], 0.0, ALU.mult, ALU.add).then_inc(s.mix, 1)
        to(57)
        w(dve, s.s_ok, b, 2, 2)
        w(dve, s.y_mm, b, 2, 2)
        w(dve, s.mix, b, MIX["cg_ok"], NMIX)
        dve.memset(R1[:, 0:1024], -30000.0).then_inc(s.gd1_ok, 1)
        w(dve, s.gd1_ok, b, 1, 2)
        to(57)
        dve.tensor_scalar(gdE[:, :, 0, 0:16], cgm[:, :, 0:16], -1.0, None, ALU.mult)
        for i in range(1, 4):
            n = 16 * i + 16
            ins = dve.tensor_tensor(gdE[:, :, i, 0:n], cgm[:, :, 16 * i - 1:16 * i].to_broadcast([P, 4, n]), cgm[:, :, 0:n], ALU.subtract)
        ins.then_inc(s.gd1_ok, 1)
        to(58)
        dve.tensor_copy(gq4[:, :, 0, :], cg4[:, :, 0, :])
        dve.tensor_tensor(gq4[:, :, 1:4, :], cg4[:, :, 1:4, :], cg4[:, :, 0:3, 15:16].to_broadcast([P, 4, 3, 16]), ALU.subtract).then_inc(s.gq1_ok, 1)
        dve.tensor_tensor(kd[:, :, :].rearrange("p q (c t) -> p (q c) t", c=2), cgm[:, :, C - 1:C].to_broadcast([P, 4, C]), cgm, ALU.subtract).then_inc(s.gl1_ok, 1)
        to(58)
        w(dve, s.gd1_ok, b, 2, 2)
        dve.tensor_scalar(R1[:, 0:1024], R1[:, 0:1024], GMAX, None, ALU.min).then_inc(s.gcl_ok, 1)
        to(60)
        w(dve, s.silu_ok, b)
        kg = cv[:, 2:4, :].rearrange("p q (c t) -> p (q c) t", c=2)
        w(dve, s.gexp, b, GEXP["gex_ok"], NGEXP)
        dve.tensor_tensor(kE, gdE, kg.unsqueeze(2).to_broadcast([P, 4, 4, C]), ALU.mult)
        to(60)
        w(dve, s.gexp, b, GEXP["gqx_ok"], NGEXP)
        for h in range(2):
            ins = dve.scalar_tensor_tensor(qI[half(h), h, :, :], cv[half(h), 0:2, :].rearrange("p q (c t) -> p (q c) t", c=2), 0.125, gq[half(h), :].rearrange("p (m t) -> p m t", m=4), ALU.mult, ALU.mult)
        ins.then_inc(s.gq_ok, 1)
        to(61)
        w(dve, s.gexp, b, GEXP["gi_ok"], NGEXP)
        for h in range(2):
            ins = dve.scalar_tensor_tensor(qi[half(h), h, :, :], cv[half(h), 0:2, :], 0.125, qe[half(h)], ALU.mult, ALU.mult)
        ins.then_inc(s.gqi_ok, 1)
        to(61)
        w(dve, s.gexp, b, GEXP["gl_ok"], NGEXP)
        dve.tensor_tensor(kd[:, :, :], kd[:, :, :], cv[:, 2:4, :], ALU.mult).then_inc(s.gkd_ok, 1)

    def dve_group_norm(dve, b, to):
        to(62)
        w(dve, s.ystd_ok, b)
        dve.reciprocal(t2[:, :, :], t2[:, :, :]).then_inc(s.mix, 1)
        w(dve, s.mix, b, MIX["yrs_ok"], NMIX)
        dve.tensor_tensor(y[:, :, :], y[:, :, :], t2[:, :, :], ALU.mult).then_inc(s.yn_ok, 1)
        to(62)
        w(dve, s.yn_ok, b)
        dve.tensor_tensor(y[:, :, :], y[:, :, :], v4(VGG), ALU.mult).then_inc(s.mix, 1)
        dve.tensor_tensor(bon[:, :, :], bon[:, :, :], v4(VGB), ALU.add).then_inc(s.mix, 1)
        to(63)
        w(dve, s.mix, b, MIX["yn2_ok"], NMIX)
        w(dve, s.mix, b, MIX["yn3_ok"], NMIX)
        dve.tensor_tensor(y[:, :, :], y[:, :, :], bon[:, :, :], ALU.add).then_inc(s.mix, 1)
        to(63)
        w(dve, s.mix, b, MIX["yn4_ok"], NMIX)
        dve.tensor_tensor(ymix[:, 0:HP, :], y[:, :, :], gg[:, :, :], ALU.mult)

    def dve_gla(dve, b, to):
        to(64)
        w(dve, s.ga_mm, b)
        for c in range(NC2):
            tc = slice(c * C, c * C + C)
            ins = dve.tensor_tensor(At[tc, :, tc], Fb[tc, 0:256].rearrange("p (h t) -> p h t", h=4), cst[tc, CMG + C:CMG + P].unsqueeze(1).to_broadcast([64, 4, C]), ALU.mult)
        ins.then_inc(s.ga_ev, 1)
        to(65)
        w(dve, s.gexp, b, GEXP["gec_ok"], NGEXP)
        for c in range(NC2):
            to(66 + 2 * c)
            w(dve, s.gs_mm, b, c + 1, 2)
            for q in range(2):
                ins = dve.scalar_tensor_tensor(Sg[:, q, :], Sg[:, q, :], egc[:, 2 * q + c:2 * q + c + 1], Eb[:, c * 256 + q * P:c * 256 + q * P + P], ALU.mult, ALU.add)
            ins.then_inc(s.gs_ok, 1)
        to(69)
        w(dve, s.go_mm, b, 2, 2)
        dve.tensor_copy(o, f4(Db)).then_inc(s.go_ev, 1)
        to(71)
        w(dve, s.ostd_ok, b)
        dve.reciprocal(t1[:, :, :], t1[:, :, :]).then_inc(s.mix, 1)
        w(dve, s.mix, b, MIX["ors_ok"], NMIX)
        w(dve, s.go_ev, b)
        dve.scalar_tensor_tensor(o, o, vec[:, VNG:VNG + 1], t1[:, :, :], ALU.mult, ALU.mult).then_inc(s.mix, 1)
        to(72)
        w(dve, s.gsil_ok, b)
        dve.tensor_tensor(t2[:, :, :], t2[:, :, :], praw[:, CGB:CGB + 4, PADC:PRW], ALU.mult).then_inc(s.mix, 1)
        w(dve, s.mix, b, MIX["on_ok"], NMIX)
        to(72)
        w(dve, s.mix, b, MIX["on2_ok"], NMIX)
        dve.tensor_tensor(ymix[:, HP:2 * HP, :], o, t2[:, :, :], ALU.mult).then_inc(s.ymixb_ok, 1)

    def dve_moments(dve, b, x, st, mv, own, mv_ok):
        for j in range(2):
            ins = dve.bn_stats(st[:, 6 * j:6 * j + 6], x[:, 512 * j:512 * j + 512])
        ins.then_inc(own, 1)
        w(dve, own, b, 1, 4)
        alone(dve)
        dve.bn_aggr(mv[:, :], st[:, :]).then_inc(mv_ok, 1)

    def dve_norm(dve, b, x, mv, sd, row, own, sd_ok, o_ok, to, place):
        to(place)
        w(dve, sd_ok, b)
        dve.reciprocal(sd[:, 1:2], sd[:, 0:1]).then_inc(own, 1)
        w(dve, own, b, 2, 4)
        dve.tensor_scalar(x, x, mv[:, 0:1], sd[:, 1:2], ALU.subtract, ALU.mult).then_inc(own, 1)
        w(dve, own, b, 3, 4)
        dve.tensor_tensor(x, x, ln[:, row, :], ALU.mult).then_inc(own, 1)
        to(place + 1)
        w(dve, own, b, 4, 4)
        dve.tensor_tensor(x, x, ln[:, row + 1, :], ALU.add).then_inc(o_ok, 1)

    def dve_residual(dve, b, to):
        to(77)
        dve.wait_ge(s.hin_in, b * 16 + 16)
        if type(b) is int and b == 0:
            dve.wait_ge(s.ln_in, 4 * 16)
        for j in range(2):
            to(77 + 4 * j)
            w(dve, s.op_mm, b, 4 * j + 4, ND)
            dve.scalar_tensor_tensor(h1[:, 512 * j:512 * j + 512], h1[:, 512 * j:512 * j + 512], ALPHA, (B, Cb)[j][:, :], ALU.mult, ALU.add).then_inc(s.hy_ok, 1)
        to(82)
        w(dve, s.hy_ok, b, 2, 2)
        dve_moments(dve, b, h1[:, :], stt, mv1, s.norm1, s.mv1_ok)
        dve_norm(dve, b, h1[:, :], mv1, sd1, 0, s.norm1, s.sd1_ok, s.h1_ok, to, 83)

    def dve_top(dve, b, h, to):
        n = [16 * h]

        def step(ins):
            ins.then_inc(s.tk_ok, 1)
            n[0] += 1

        def done():
            to(93 + 3 * h + (n[0] - 16 * h) // 6)
            w(dve, s.tk_ok, b, n[0], 16 * PH)
            alone(dve)

        def top16(src, work, vals, idx):
            step(dve.max(vals[:, 0:8], src))
            done()
            step(dve.max_index(idx[:, 0:8], vals[:, 0:8], src))
            step(dve.match_replace(work, vals[:, 0:8], src, NEG))
            done()
            step(dve.max(vals[:, 8:16], work))
            done()
            step(dve.max_index(idx[:, 8:16], vals[:, 8:16], work))

        to(93 + 3 * h)
        w(dve, s.sc_ev, b, h // 2 + 1, 4)
        alone(dve)
        for p in range(2):
            m = 2 * h + p
            top16(scor[:, m, :], scw, sv[:, m, :], si[:, m, :])
        step(dve.tensor_tensor(cand, sv[:, 2 * h, :].unsqueeze(2).to_broadcast([P, 16, 16]), sv[:, 2 * h + 1, :].unsqueeze(1).to_broadcast([P, 16, 16]), ALU.add))
        done()
        top16(cand.rearrange("p a b -> p (a b)"), candw, cval[:, h, :], ci[:, 16 * h:16 * h + 16])
        assert n[0] == 16 * h + 16

    def dve_ids(dve, b, to):
        n = [0]

        def step(ins):
            ins.then_inc(s.ids_ok, 1)
            n[0] += 1

        def done():
            to(118 + n[0] * 8 // NIDS)
            w(dve, s.ids_ok, b, n[0], NIDS)

        w(dve, s.tk_ok, b, 16 * PH, 16 * PH)
        step(dve.tensor_tensor(gate[:, :, :], cval[:, :, :], cval[:, :, 0:1].to_broadcast([P, PH, TOPK]), ALU.subtract))
        step(dve.tensor_scalar(ca[:, 0, :], ci[:, :], 4, None, ALU.logical_shift_right))
        step(dve.tensor_scalar(ca[:, 1, :], ci[:, :], 15, None, ALU.bitwise_and))
        step(dve.tensor_copy(sif, si[:, :, :].rearrange("p (h q) a -> p h q a", q=2)))
        done()
        step(dve.tensor_copy(cf, ca[:, :, :]))
        io = cst[:, CIO:CIO + TOPK].unsqueeze(1).to_broadcast([P, P // 2, TOPK])
        oh4 = oh.rearrange("p (h n) a -> p h n a", h=PH // 2)
        for q in range(2):
            for j in range(2):
                hk, hh = slice(64 * j, 64 * j + 64), slice(4 * j, 4 * j + 4)
                done()
                step(dve.tensor_tensor(oh, cf[:, q, hk].unsqueeze(2).to_broadcast([P, P // 2, TOPK]), io, ALU.is_equal))
                done()
                step(dve.tensor_tensor(oh4, oh4, sif[:, hh, q, :].unsqueeze(2).to_broadcast([P, PH // 2, TOPK, TOPK]), ALU.mult))
                done()
                step(dve.tensor_reduce(ef[:, q, hk], oh, AX.X, ALU.add))
        done()
        step(dve.scalar_tensor_tensor(ids[:, :], ef[:, 0, :], float(NKEY), ef[:, 1, :], ALU.mult, ALU.add))
        w(dve, s.ge_ok, b)
        step(dve.tensor_reduce(gsum[:, 0, :], gate[:, :, :], AX.X, ALU.add))
        done()
        step(dve.reciprocal(gsum[:, 1, :], gsum[:, 0, :]))
        done()
        step(dve.tensor_tensor(gate[:, :, :], gate[:, :, :], gsum[:, 1, :].unsqueeze(2).to_broadcast([P, PH, TOPK]), ALU.mult))
        assert n[0] == NIDS

    def dve_take(dve, b, prev):
        w(dve, s.ids_ok, b, NIDS, NIDS)
        if prev:
            dve.tensor_copy(hold, h1c[:, :]).then_inc(s.kept_ok, 1)
            w(dve, s.kept_ok, b - 1, 3, 4)
            dve.wait_ge(s.u_done, NU + b * P)
            dve.wait_ge(s.v_done, NV + b * P - LATE)
        dve.tensor_copy(h1c[:, :], h1[:, :]).then_inc(s.cur_ok, 1)
        dve.tensor_copy(idc[:, :], ids[:, :]).then_inc(s.cur_ok, 1)
        dve.tensor_copy(gatec[:, :, :], gate[:, :, :]).then_inc(s.cur_ok, 1)
        w(dve, s.cur_ok, b, 3, 3)
        if prev:
            dve.tensor_copy(h1[:, :], hold).then_inc(s.kept_ok, 1)

    def dve_keep(dve, b):
        dve.tensor_copy(idl[:, :], idc[:, P - LATE:P]).then_inc(s.kept_ok, 1)
        dve.tensor_copy(gatel[:, :], gatec[:, PH - 1, :]).then_inc(s.kept_ok, 1)

    def dve_dot(dve, b, g):
        dve.wait_ge(s.u_in[g % NU], (b * (P // NU) + g // NU + 1) * 16)
        u = ur[g % NU]
        dve.tensor_tensor_reduce(u, u, h1c[:, :], 1.0, 0.0, ALU.mult, ALU.add, dots[:, (g // TOPK) % 2, g % TOPK:g % TOPK + 1]).then_inc(s.u_done, 1)

    def dve_act(dve, b, h):
        w(dve, s.gelu_ok, b, h + 1, PH)
        dve.tensor_tensor(actg[:, h % 2, :], gel[:, h % 2, :], gatec[:, h, :] if h < PH - 1 else gatel[:, :], ALU.mult).then_inc(s.act_ok, 1)

    def dve_expert(dve, b, x, prev):
        if x == 0:
            dve_take(dve, b, prev)
        if x == X_KEEP:
            dve_keep(dve, b)
        if prev and x == X_SUM:
            dve_sum(dve, b - 1, h1)
        if prev and x == X_NORM:
            dve_last_norm(dve, b - 1)
        dve_dot(dve, b, x)
        if x % TOPK == 4:
            if x > TOPK:
                dve_act(dve, b, x // TOPK - 1)
            elif prev:
                dve_act(dve, b - 1, PH - 1)

    def dve_sum(dve, b, h):
        dve.wait_ge(s.v_done, NV + b * P + P)
        if b is LAST:
            w(dve, s.out_done, b, 0, 16)
        else:
            w(dve, s.kept_ok, b, 4, 4)
        for j in range(2):
            ins = dve.scalar_tensor_tensor(h1[:, 512 * j:512 * j + 512], h[:, 512 * j:512 * j + 512], ALPHA, F[j][:, :], ALU.mult, ALU.add)
        ins.then_inc(s.fy_ok, 1)
        w(dve, s.fy_ok, b)
        dve_moments(dve, b, h1[:, :], stf, mv2, s.norm2, s.mv2_ok)

    def dve_last_norm(dve, b):
        dve_norm(dve, b, h1[:, :], mv2, sd2, 2, s.norm2, s.sd2_ok, s.fo_ok, idle, 0)

    def act_gates(act, b, to):
        to(3)
        w(act, s.shift_ok, b)
        act.activation(th, sh[0:64, CWA, :], ACT.Tanh).then_inc(s.rates_ok, 1)
        act.activation(sgd, sh[:, CGD, :], ACT.Sigmoid).then_inc(s.rates_ok, 1)
        to(4)
        w(act, s.gates_mm, b, GATES["z_mm"], NGATES)
        for i in range(4):
            ins = act.activation(sg[:, i, :], A[:, i * BT:i * BT + BT], ACT.Sigmoid, bias=vec[:, VW0 + i:VW0 + i + 1])
        ins.then_inc(s.rates_ok, 1)
        to(5)
        w(act, s.gates_mm, b, GATES["a_mm"], NGATES)
        for i in range(4):
            ins = act.activation(aa[:, i, :], B[:, i * BT:i * BT + BT], ACT.Sigmoid, bias=vec[:, VA0 + i:VA0 + i + 1])
        ins.then_inc(s.rates_ok, 1)
        to(7)
        w(act, s.conv_ok, b, 4, 4)
        act.activation(gsg, cv[:, :, :].rearrange("p a b -> p (a b)"), ACT.Sigmoid).then_inc(s.gsig_ok, 1)
        to(7)
        w(act, s.gates_mm, b, GATES["g_mm"], NGATES)
        act.activation(gg[:, :, :], f4(Cb), ACT.Copy).then_inc(s.g_ok, 1)
        to(7)
        w(act, s.kkr_ok, b)
        act.activation(kk4, t1[:, :, :], ACT.Square).then_inc(s.sq_ok, 1)
        to(8)
        w(act, s.ssm_ok, b)
        act.activation(t2[:, :, :], t2[:, :, :], ACT.Sqrt, bias=k.eps[:, 2:3]).then_inc(s.ssq_ok, 1)
        to(10)
        w(act, s.csum_ok, b)
        act.activation(egp[:, :, :, 1:C + 1], cs[:, :].rearrange("p (q c t) -> p q c t", q=4, c=2), ACT.Exp, scale=-E05).then_inc(s.egp_ok, 1)
        to(10)
        act.activation(en[:, :, :, :], cs[:, :].rearrange("p (q c t) -> p q c t", q=4, c=2), ACT.Exp, scale=E05).then_inc(s.en_ok, 1)
        to(11)
        w(act, s.xg_ok, b)
        act.activation(xa[:, :], xg[:, :], ACT.Abs).then_inc(s.xa_ok, 1)
        w(act, s.xa_ok, b, 1, 2)
        act.activation(xa[:, :], xa[:, :], ACT.Exp, scale=-1.0).then_inc(s.xa_ok, 1)
        to(11)
        w(act, s.xa_ok, b, 2, 2)
        act.activation(xa[:, :], xa[:, :], ACT.Ln, bias=1.0).then_inc(s.xl_ok, 1)
        for c in range(NC2):
            to(15 + c)
            w(act, s.kbt_mm, b, c + 1, 2)
            act.activation(KBt[:, c, :, :], f4((Cb, Db)[c]), ACT.Copy).then_inc(s.kbt_ev, 1)

    def act_inverse(act, b, to):
        for l in range(1, 6):
            to(16 + 5 * l)
            w(act, s.zz_mm, b, l, 5)
            if l > 1:
                w(act, s.tm_mm, b, l - 1, 4)
            act.activation(Z[:, :, :], f8(Db), ACT.Copy).then_inc(s.zz_ev, 1)

    def act_chunks(act, b, to):
        for c in range(NC2):
            u = slice(ub(c), ub(c) + 64)
            to(45 + 5 * c)
            w(act, s.wmm, b, c + 1, 2)
            act.activation(W[u, :, :], f8(A)[u, :, :], ACT.Copy).then_inc(s.w_ev, 1)
        to(56)
        w(act, s.yc_ok, b)
        act.activation(t1[:, :, :], y[:, :, :], ACT.Square).then_inc(s.ysq_ok, 1)
        to(57)
        w(act, s.yvar_mm, b)
        act.activation(t2[:, :, :], f4(A), ACT.Sqrt, bias=k.eps[:, 1:2], scale=1.0 / C).then_inc(s.ystd_ok, 1)
        to(58)
        w(act, s.gcl_ok, b)
        act.activation(R1[:, 0:1024], R1[:, 0:1024], ACT.Exp, scale=1.0 / 16).then_inc(s.gexp, 1)
        to(59)
        w(act, s.gq1_ok, b)
        act.activation(gq[:, :], gq[:, :], ACT.Exp, scale=1.0 / 16).then_inc(s.gexp, 1)
        to(59)
        act.activation(qe, cg[:, :].rearrange("p (q t) -> p q t", q=2), ACT.Exp, scale=1.0 / 16).then_inc(s.gexp, 1)
        to(60)
        w(act, s.gl1_ok, b)
        act.activation(kd[:, :, :], kd[:, :, :], ACT.Exp, scale=1.0 / 16).then_inc(s.gexp, 1)
        act.activation(egc[:, :], cgm[:, :, C - 1], ACT.Exp, scale=1.0 / 16).then_inc(s.gexp, 1)

    def act_gla(act, b, to):
        to(59)
        w(act, s.gvt_mm, b)
        act.activation(Vt, f4(B), ACT.Copy).then_inc(s.gvt_ev, 1)
        to(62)
        w(act, s.gkt_mm, b)
        act.activation(kdt, Cb[:, 0:256].rearrange("p (q t) -> p q t", q=2), ACT.Copy).then_inc(s.gkt_ev, 1)
        to(69)
        w(act, s.go_ev, b)
        act.activation(o2, o, ACT.Square).then_inc(s.osq_ok, 1)
        to(70)
        w(act, s.orms_mm, b)
        act.activation(t1[:, :, :], f4(A), ACT.Sqrt, bias=k.eps[:, 0:1], scale=1.0 / P).then_inc(s.ostd_ok, 1)
        to(71)
        w(act, s.yn_ok, b)
        act.activation(t2[:, :, :], praw[:, CGB:CGB + 4, PADC:PRW], ACT.Sigmoid).then_inc(s.gsil_ok, 1)

    def act_queries(act, b, to):
        to(83)
        w(act, s.mv1_ok, b)
        act.activation(sd1[:, 0:1], mv1[:, 1:2], ACT.Sqrt, bias=k.eps[:, 0:1]).then_inc(s.sd1_ok, 1)
        for j in range(2):
            to(85 + j)
            w(act, s.h1t_mm, b, j + 1, 2)
            act.activation(h1T[:, 4 * j:4 * j + 4, :], f4((Db, Eb)[j]), ACT.Copy).then_inc(s.h1t_ev, 1)
        for g in range(4):
            to(91 + 6 * g)
            w(act, s.q_mm, b, 4 * g + 4, 16)
            if g >= 2:
                w(act, s.sc_mm, b, g - 1, 4)
            act.activation(qT[g % 2], f4((Fb, A)[g % 2]), ACT.Copy).then_inc(s.q_ev, 1)
            to(92 + 6 * g)
            w(act, s.sc_mm, b, g + 1, 4)
            act.activation(scor[:, 4 * g:4 * g + 4, :], f4((B, Cb)[g % 2]), ACT.Copy).then_inc(s.sc_ev, 1)

    def act_softmax(act, b, to):
        to(119)
        w(act, s.ids_ok, b, 1, NIDS)
        act.activation(gate[:, :, :], gate[:, :, :], ACT.Exp).then_inc(s.ge_ok, 1)

    def act_gelu(act, b, h):
        act.wait_ge(s.u_done, NU + b * P + (h + 1) * TOPK)
        act.activation(gel[:, h % 2, :], dots[:, h % 2, :], ACT.Gelu).then_inc(s.gelu_ok, 1)

    def act_diag(act, b, g):
        w(act, s.act_ok, b, g // TOPK + 1, PH)
        act.wait_ge(s.v_done, NV - ND4 + b * P + g + 1)
        act.activation(diag[g % ND4][:, :], cst[:, CID:CID + P], ACT.Copy, scale=actg[:, (g // TOPK) % 2, g % TOPK:g % TOPK + 1]).then_inc(s.diag_ok, 1)

    def act_expert(act, b, x, prev):
        if x >= X0:
            act_diag(act, b, x - X0)
        elif prev:
            act_diag(act, b - 1, x - X0 + P)
        if x % TOPK == 2:
            if x > TOPK:
                act_gelu(act, b, x // TOPK - 1)
            elif prev:
                act_gelu(act, b - 1, PH - 1)
        if prev and x == X_SUM + 1:
            act_final(act, b - 1)

    def act_final(act, b):
        w(act, s.mv2_ok, b)
        act.activation(sd2[:, 0:1], mv2[:, 1:2], ACT.Sqrt, bias=k.eps[:, 0:1]).then_inc(s.sd2_ok, 1)

    def mm(pe, out, l, r, start=True, stop=True):
        return pe.matmul(out, l, r, start=start, stop=stop)

    def pe_gates(pe, b, to):
        ident, ones2 = cst[:, CID:CID + P], cst[:, CBO:CBO + P]
        to(4)
        w(pe, s.rates_ok, b, RATES["th_ok"], NRATES)
        to(4)
        for i in range(4):
            ins = mm(pe, A[:, i * BT:i * BT + BT], k.w2a2[0:64, i * P:i * P + P], th)
        ins.then_inc(s.gates_mm, 1)
        for i in range(4):
            ins = mm(pe, B[:, i * BT:i * BT + BT], k.w2a2[64:128, i * P:i * P + P], sh[64:128, CWA, :])
        ins.then_inc(s.gates_mm, 1)
        to(5)
        w(pe, s.rates_ok, b, RATES["sgd_ok"], NRATES)
        for i in range(4):
            ins = mm(pe, Cb[:, i * BT:i * BT + BT], k.g2[:, i * P:i * P + P], sgd)
        ins.then_inc(s.gates_mm, 1)
        for i in range(2):
            ins = mm(pe, Db[:, i * BT:i * BT + BT], k.gkw2[:, i * P:i * P + P], praw[0:16, CGK, PADC:PRW])
        ins.then_inc(s.gates_mm, 1)
        to(8)
        w(pe, s.sq_ok, b)
        mm(pe, Eb[:, :], ones2, kk4.rearrange("p q t -> p (q t)")).then_inc(s.gates_mm, 1)
        to(13)
        w(pe, s.rk_ok, b)
        mm(pe, Fb[:, :], ones2, t1[:, :, :].rearrange("p q t -> p (q t)")).then_inc(s.gates_mm, 1)
        to(13)
        w(pe, s.rates_ok, b, RATES["a_ok"], NRATES)
        alone(pe)
        for c in range(NC2):
            for q in range(4):
                ins = pe.transpose((A, B)[c][0:64, q * P:q * P + P], sh[:, CV + q, c * C:c * C + C], ident)
            ins.then_inc(s.vtr_mm, 1)
        to(13)
        w(pe, s.g_ok, b)
        w(pe, s.xg_ok, b)
        w(pe, s.kbb_ok, b)
        for c in range(NC2):
            for q in range(4):
                ins = pe.transpose((Cb, Db)[c][:, q * P:q * P + P], KB[:, q, c, :, :].rearrange("p s t -> p (s t)"), ident)
            ins.then_inc(s.kbt_mm, 1)
        to(15)
        w(pe, s.rkr_ok, b)
        for c in range(NC2):
            for h in range(2):
                i = 2 * c + h
                to(15 + c)
                if i < 2:
                    w(pe, (s.ssm_ok, s.bon_ok)[i], b)
                else:
                    w(pe, s.v_ev, b, i - 1, 2)
                for q in range(4):
                    ins = mm(pe, (Eb, Fb, A, B)[i][:, q * P:q * P + P], KB[:, q, c, :, :].rearrange("p s t -> p (s t)"),
                             RK[:, h, 2 * q + c, :, :].rearrange("p s t -> p (s t)"))
                ins.then_inc(s.gram_mm, 1)
        to(17)
        w(pe, s.kbt_ev, b, 1, 2)
        alone(pe)
        for c in range(NC2):
            for h in range(2):
                for q in range(4):
                    m = (h * 4 + q) * C
                    ins = mm(pe, Cb[ub(c):ub(c) + 64, m:m + C], RK[:, h, 2 * q + c, 0, :], KB[:, q, c, 1 - c, :])
        ins.then_inc(s.nt_mm, 1)

    def each(fn):
        for c in range(NC2):
            for m in range(8):
                ins = fn(slice(ub(c), ub(c) + 64), m)
        return ins

    def pe_inverse(pe, b, to):
        for l in range(1, 6):
            to(15 + 5 * l)
            w(pe, s.tt_ok, b, l, 6)
            w(pe, s.t_ok, b, l, 5)
            w(pe, s.ntl_ok, b, l + 1, 6)
            if l == 1:
                w(pe, s.kbt_ev, b, 2, 2)
                w(pe, s.gram_ev, b, 4, 4)
            else:
                w(pe, s.zz_ev, b, l - 1, 5)
            alone(pe)
            each(lambda u, m: mm(pe, Db[u, m * C:m * C + C], NTl[u, m, :], Tt[u, m, :])).then_inc(s.zz_mm, 1)
            to(17 + 5 * l)
            w(pe, s.zz_ev, b, l, 5)
            alone(pe)
            each(lambda u, m: mm(pe, Eb[u, m * C:m * C + C], Ti[u, m, :], Z[u, m, :])).then_inc(s.ttm_mm, 1)
            to(18 + 5 * l)
            if l < 5:
                each(lambda u, m: mm(pe, Fb[u, m * C:m * C + C], Z[u, m, :], Ti[u, m, :])).then_inc(s.tm_mm, 1)

    def pe_chunks(pe, b, to):
        for c in range(NC2):
            u = slice(ub(c), ub(c) + 64)
            hq = [(h, q) for h in range(2) for q in range(4)]
            to(44 + 5 * c)
            w(pe, s.s_ok, b, c, 2)
            w(pe, s.v_ev, b, 2, 2)
            if c:
                w(pe, s.w_ev, b, 1, 2)
            alone(pe)
            for h, q in hq:
                m = (h * 4 + q) * C
                mm(pe, A[u, m:m + C], RK[:, h, 2 * q + c, 0, :], S[:, q, :], stop=False)
                ins = mm(pe, A[u, m:m + C], GT[:, c, h, q, 0:C], UV[:, c, h, q, :], start=False)
            ins.then_inc(s.wmm, 1)
            to(45 + 5 * c)
            w(pe, s.w_ev, b, c + 1, 2)
            w(pe, s.tt_ok, b, 6, 6)
            if c:
                w(pe, s.u_ev, b, 1, 2)
            alone(pe)
            for h, q in hq:
                m = h * 4 + q
                ins = mm(pe, B[u, m * C:m * C + C], Tt[u, m, :], W[u, m, :])
            ins.then_inc(s.umm, 1)
            to(47 + 5 * c)
            w(pe, s.u_ev, b, c + 1, 2)
            alone(pe)
            to(48 + 5 * c)
            for h, q in hq:
                col = q * BT + c * C
                mm(pe, Db[half(h), col:col + C], S[:, q, :], RK[:, h, 2 * q + c, 1, :], stop=False)
                ins = mm(pe, Db[half(h), col:col + C], UV[:, c, h, q, :], GT[:, c, h, q, C:2 * C], start=False)
            ins.then_inc(s.y_mm, 1)
            for h, q in hq:
                col = c * 256 + q * C
                ins = mm(pe, Eb[half(h), col:col + C], KBt[:, c, q, h * C:h * C + C], UV[:, c, h, q, :])
            ins.then_inc(s.st_mm, 1)
        to(54)
        w(pe, s.y_ev, b)
        w(pe, s.t_ok, b, 5, 5)
        mm(pe, Fb[:, :], cst[:, CBO:CBO + P], y[:, :, :].rearrange("p q t -> p (q t)")).then_inc(s.ymean_mm, 1)
        to(56)
        w(pe, s.ysq_ok, b)
        mm(pe, A[:, :], cst[:, CBO:CBO + P], t1[:, :, :].rearrange("p q t -> p (q t)")).then_inc(s.yvar_mm, 1)

    def pe_gla(pe, b, to):
        ident = cst[:, CID:CID + P]
        to(58)
        w(pe, s.silu_ok, b)
        w(pe, s.u_ev, b, 2, 2)
        for h in range(4):
            ins = pe.transpose(B[:, h * P:h * P + P], cv[:, 4 + h, :], ident)
        ins.then_inc(s.gvt_mm, 1)
        to(61)
        w(pe, s.gkd_ok, b)
        for q in range(2):
            ins = pe.transpose(Cb[:, q * P:q * P + P], kd[:, q, :], ident)
        ins.then_inc(s.gkt_mm, 1)
        to(62)
        w(pe, s.gq_ok, b)
        w(pe, s.yc_ok, b)
        alone(pe)
        for h in range(4):
            for c in range(NC2):
                m = (h // 2) * 2 + c
                to(62 + h // 2)
                for i in range(4):
                    col = h * C + 16 * i
                    ins = mm(pe, Fb[c * C:c * C + C, col:col + 16], kE[:, m, i, :], qI[:, h % 2, m, 16 * i:16 * i + 16])
        ins.then_inc(s.ga_mm, 1)
        to(64)
        w(pe, s.gqi_ok, b)
        w(pe, s.gvt_ev, b)
        w(pe, s.gkt_ev, b)
        w(pe, s.ga_ev, b)
        for c in range(NC2):
            to(65 + 2 * c)
            w(pe, s.gs_ok, b, c, 2)
            alone(pe)
            tc = slice(c * C, c * C + C)
            for h in range(4):
                col = h * P + c * C
                mm(pe, Db[:, col:col + C], Sg[:, h // 2, :], qi[:, h % 2, h // 2, tc], stop=False)
                ins = mm(pe, Db[:, col:col + C], Vt[:, h, :], At[:, h, tc], start=False)
            ins.then_inc(s.go_mm, 1)
            for h in range(4):
                col = c * 256 + (h // 2) * P
                ins = mm(pe, Eb[half(h % 2), col:col + P], kdt[tc, h // 2, (h % 2) * C:(h % 2) * C + C], Vt[tc, h, :])
            ins.then_inc(s.gs_mm, 1)
        to(70)
        w(pe, s.osq_ok, b)
        w(pe, s.ystd_ok, b)
        mm(pe, A[:, :], k.ones[:, :], o2.rearrange("p q t -> p (q t)")).then_inc(s.orms_mm, 1)

    def pe_out(pe, b, to):
        to(73)
        w(pe, s.ymixb_ok, b)
        for m in range(ND):
            to(73 + m)
            pe.wait_ge(s.wq_b[m % 2], (b * NWB + m // 2 + 1) * 16)
            for c in range(ND):
                ins = mm(pe, (B, Cb)[m // 4][:, (m % 4) * P:(m % 4) * P + P], ymix[:, c, :], wqb[m % 2][:, c, :], start=c == 0, stop=c == ND - 1)
            ins.then_inc(s.op_mm, 1)
        to(84)
        w(pe, s.h1_ok, b)
        w(pe, s.gs_ok, b, 2, 2)
        w(pe, s.go_ev, b)
        for j in range(2):
            to(84 + j)
            for d in range(4):
                ins = pe.transpose((Db, Eb)[j][:, d * P:d * P + P], h1[:, (4 * j + d) * P:(4 * j + d) * P + P], cst[:, CID:CID + P])
            ins.then_inc(s.h1t_mm, 1)

    def pe_queries(pe, b, to):
        def queries(g):
            if g == 0:
                w(pe, s.h1t_ev, b, 2, 2)
                w(pe, s.ga_ev, b)
            if g == 1:
                w(pe, s.ostd_ok, b)
            if g >= 2:
                w(pe, s.q_ev, b, g - 1, 4)
            for i in range(4):
                m = 4 * g + i
                to(87 + 6 * g + i)
                pe.wait_ge(s.wq_b[m % 2], (b * NWB + (ND + m) // 2 + 1) * 16)
                for d in range(ND):
                    ins = mm(pe, (Fb, A)[g % 2][:, i * P:i * P + P], wqb[m % 2][:, d, :], h1T[:, d, :], start=d == 0, stop=d == ND - 1)
                ins.then_inc(s.q_mm, 1)

        def scores(g):
            to(91 + 6 * g)
            w(pe, s.q_ev, b, g + 1, 4)
            if g < 2:
                w(pe, s.hy_ok, b, 2, 2)
            else:
                w(pe, s.sc_ev, b, g - 1, 4)
            for i in range(4):
                ins = mm(pe, (B, Cb)[g % 2][:, i * P:i * P + P], qT[g % 2][:, i, :], k.keys[:, 4 * g + i, :])
            ins.then_inc(s.sc_mm, 1)
        for g in range(4):
            queries(g)
            scores(g)

    def pe_value(pe, b, g):
        pe.wait_ge(s.v_in[g % NV], (b * (P // NV) + g // NV + 1) * 16)
        pe.wait_ge(s.diag_ok, b * P + g + 1)
        if g == 0:
            w(pe, s.fy_ok, b, 0)
        for j in range(2):
            ins = mm(pe, F[j][:, :], diag[g % ND4][:, :], vr[g % NV][:, 512 * j:512 * j + 512], start=g == 0, stop=g == P - 1)
        ins.then_inc(s.v_done, 1)

    def gather_u(pool, b, g):
        pool.wait_ge(s.u_done, b * P + g + 1)
        alone(pool)
        pool.indirect_dma_start(ur[g % NU], None, dram.u, bass.IndirectOffsetOnAxis(idc[:, g:g + 1], 0)).then_inc(s.u_in[g % NU], 16)

    def gather_v(pool, b, g):
        pool.wait_ge(s.v_done, b * P + g + 1)
        if g == P - LATE:
            w(pool, s.kept_ok, b, 2, 4)
        alone(pool)
        i = idc[:, g:g + 1] if g < P - LATE else idl[:, g - P + LATE:g - P + LATE + 1]
        pool.indirect_dma_start(vr[g % NV][:, :], None, dram.v, bass.IndirectOffsetOnAxis(i, 0)).then_inc(s.v_in[g % NV], 16)

    def pe_project(pe, x):
        for m in range(x * 2 * NCH * ND // P, (x + 1) * 2 * NCH * ND // P):
            n, d = m // ND, m % ND
            c, part = n // 2, n % 2
            if d == 0 and part == 0:
                pe.wait_ge(s.w_rest[c % 3], (c // 3 + 1) * 16)
            if d == 0 and n >= 2:
                pe.wait_ge(s.proj_ev, NCH + n - 1)
            col = BT + part * REST
            ins = mm(pe, F[part][:, 0:REST], wip[c % 3][:, d, :], hT[:, d, col:col + REST], start=d == 0, stop=d == ND - 1)
            if d == ND - 1:
                ins.then_inc(s.proj_mm, 1)

    def act_project(act, x):
        for n in range(2 * NCH):
            if (n + 1) * ND * P // (2 * NCH * ND) + 1 == x:
                act.wait_ge(s.proj_mm, NCH + n + 1)
                if n >= 3:
                    act.wait_ge(s.p_rest[n % 3], n // 3 * 16)
                act.activation(pst[n % 3], F[n % 2][:, 0:REST], ACT.Copy).then_inc(s.proj_ev, 1)

    def pool_project(pool):
        def load(c, j):
            pool.dma_start(wip[j], dram.w_in[bass.ds(c, 1)].rearrange("o p d c -> (o p) d c")).then_inc(s.w_rest[j], 16)

        def results(i, more):
            for n in range(6):
                pool.wait_ge(s.proj_ev, NCH + 6 * i + n + 1)
                col = PADC + BT + (n % 2) * REST
                pool.dma_start(dram.p[bass.ds(3 * i + n // 2, 1), :, col:col + REST].rearrange("o p t -> (o p) t"), pst[n % 3]).then_inc(s.p_rest[n % 3], 16)
                if more and n % 2 == 1:
                    load(3 * i + n // 2 + 3, n // 2)
        for j in range(3):
            load(j, j)
        with pool.Fori(0, NRND - 1) as i:
            results(i, True)
        results(NRND - 1, False)
        for j in range(3):
            pool.wait_ge(s.p_rest[j], NRND * 2 * 16)

    def idle(x):
        pass

    def stream(step):
        done = [0]

        def to(x):
            while done[0] < x:
                step(done[0])
                done[0] += 1
        return to

    @block.sync
    def _(sp):
        sp_projections(sp, 0)
        sp_weights(sp, 0)
        for j in range(3):
            sp.wait_ge(s.p_rest[j], NRND * 2 * 16)
        sp_projections(sp, 1)
        sp_weights(sp, 1)
        with sp.Fori(1, LAST) as b:
            sp_projections(sp, b + 1)
            sp_output(sp, b - 1)
            sp_weights(sp, b + 1)
        sp_output(sp, LAST - 1)
        sp_output(sp, LAST)

    @block.scalar
    def _(act):
        def mixer(b, to):
            act_gates(act, b, to)
            act_inverse(act, b, to)
            act_chunks(act, b, to)
            act_gla(act, b, to)
            act_queries(act, b, to)
            act_softmax(act, b, to)

        def steps(b, prev):
            to = stream(lambda x: act_expert(act, b, x, prev))
            if b is not LAST:
                mixer(b + 1, to)
            to(P)

        w(act, s.consts_ok, 0, NINIT)
        to = stream(lambda x: act_project(act, x))
        mixer(0, to)
        to(P + 2)
        steps(0, False)
        with act.Fori(1, LAST) as b:
            steps(b, True)
        steps(LAST, True)
        for x in range(P, P + X0):
            act_diag(act, LAST, x - X0)
            if x == P + 2:
                act_gelu(act, LAST, PH - 1)
        act_final(act, LAST)

    @block.vector
    def _(dve):
        def mixer(b, to):
            dve_gates(dve, b, to)
            dve_decays(dve, b, to)
            dve_inverse(dve, b, to)
            dve_chunks(dve, b, to)
            dve_gla_parts(dve, b, to)
            dve_group_norm(dve, b, to)
            dve_gla(dve, b, to)
            dve_residual(dve, b, to)
            for h in range(PH):
                dve_top(dve, b, h, to)
            dve_ids(dve, b, to)

        def steps(b, prev):
            to = stream(lambda x: dve_expert(dve, b, x, prev))
            if b is not LAST:
                mixer(b + 1, to)
            to(P)

        dve.memset(S[:, :, :], 0.0).then_inc(s.consts_ok, 1)
        dve.memset(Sg[:, :, :], 0.0).then_inc(s.consts_ok, 1)
        dve.memset(RK[:, :, :, :, :], 0.0)
        dve.memset(qI[:, :, :, :], 0.0)
        dve.memset(qi[:, :, :, :], 0.0)
        dve.memset(At[:, :, :], 0.0)
        dve.memset(egp[:, :, :, 0:1], 1.0).then_inc(s.consts_ok, 1)
        dve.memset(k.ones[:, :], 1.0).then_inc(s.consts_ok, 1)
        dve.tensor_scalar(k.omka[:, :], vec[:, VKA:VKA + 4], -1.0, 1.0, ALU.mult, ALU.add).then_inc(s.consts_ok, 1)
        dve.memset(stt[:, 0:1], 0.0).then_inc(s.u_done, NU)
        dve.memset(stt[:, 1:2], 0.0).then_inc(s.v_done, NV)
        w(dve, s.consts_ok, 0, NINIT)
        mixer(0, idle)
        steps(0, False)
        with dve.Fori(1, LAST) as b:
            steps(b, True)
        steps(LAST, True)
        dve_act(dve, LAST, PH - 1)
        dve_sum(dve, LAST, h1c)
        dve_last_norm(dve, LAST)

    @block.tensor
    def _(pe):
        def mixer(b, to):
            pe_gates(pe, b, to)
            pe_inverse(pe, b, to)
            pe_chunks(pe, b, to)
            pe_gla(pe, b, to)
            pe_out(pe, b, to)
            pe_queries(pe, b, to)

        def expert(b, x, prev):
            if x >= X0:
                pe_value(pe, b, x - X0)
            elif prev:
                pe_value(pe, b - 1, x - X0 + P)

        def steps(b, prev):
            to = stream(lambda x: expert(b, x, prev))
            if b is not LAST:
                mixer(b + 1, to)
            to(P)

        to = stream(lambda x: pe_project(pe, x))
        to(3)
        w(pe, s.consts_ok, 0, NINIT)
        mixer(0, to)
        to(P)
        pe.wait_ge(s.proj_ev, 3 * NCH)
        steps(0, False)
        with pe.Fori(1, LAST) as b:
            steps(b, True)
        steps(LAST, True)
        for g in range(P - X0, P):
            pe_value(pe, LAST, g)

    @block.gpsimd
    def _(pool):
        lag = VLAG + TOPK

        def steps(b, prev):
            w(pool, s.cur_ok, b, 3, 3)
            for x in range(P):
                gather_u(pool, b, x)
                if x >= lag:
                    gather_v(pool, b, x - lag)
                elif prev:
                    gather_v(pool, b - 1, x - lag + P)

        pool_project(pool)
        steps(0, False)
        with pool.Fori(1, LAST) as b:
            steps(b, True)
        steps(LAST, True)
        for g in range(P - lag, P):
            gather_v(pool, LAST, g)

_INS = ['x', 'w_in', 'vec', 'cst', 'w2a2', 'g2', 'gkw2', 'lnrows', 'w_out', 'wq', 'keys', 'u', 'v']


def _constants():
    import numpy as np
    c = np.zeros((P, NCST), np.float32)
    p = np.arange(P)
    q = p % C
    col = np.arange(C)
    c[:, CID:CID + P] = np.eye(P)
    c[:, CBO:CBO + P] = (p[:, None] // C == p[None, :] // C)
    c[:, CMG:CMG + C] = q[:, None] < col[None, :]
    c[:, CMG + C:CMG + 2 * C] = q[:, None] <= col[None, :]
    for l in range(6):
        s = 1 << l
        t, j = q[:, None], col[None, :]
        m = (t // (2 * s) == j // (2 * s)) & (t % (2 * s) >= s) & (j % (2 * s) < s)
        c[:, CML + l * C:CML + (l + 1) * C] = m
        if l == 0:
            c[:, CM0T:CM0T + C] = (j // 2 == t // 2) & (j % 2 == 1) & (t % 2 == 0)
    c[:, CI64:CI64 + C] = q[:, None] == col[None, :]
    c[:, CRS:CRS + 512] = (np.arange(512) % C != 0)[None, :]
    c[:, CIO:CIO + TOPK] = np.arange(TOPK)[None, :]
    return c


def kernel(**inputs):
    import numpy as np
    import concourse.bacc as bacc
    from concourse.bass_utils import run_bass_kernel_spmd

    a = {n: np.asarray(v) for n, v in inputs.items()}
    cols = lambda v: v.reshape(-1, P).T
    wi = a['w_in'][0]
    gk0 = CGK * P
    wi = np.concatenate([wi[:, :gk0 + P], wi[:, gk0 + 16:]], axis=1)
    vec = np.concatenate([cols(a['a_mu'][0]), cols(a['a_w0'][0]), cols(a['a_a0'][0]), cols(a['a_k_k'][0]), cols(a['a_k_a'][0]),
                          cols(a['a_r_k'][0].reshape(-1)), cols(a['a_gn_g'][0]), cols(a['a_gn_b'][0]),
                          cols(a['b_conv'][0].reshape(-1)), cols(a['b_gk_b'][0]), cols(a['b_norm_g'][0])], axis=1)
    arrays = {
        'x': a['x'][0],
        'w_in': wi.reshape(ND, P, NCH, P).transpose(2, 1, 0, 3),
        'vec': vec,
        'cst': _constants(),
        'w2a2': np.concatenate([a['a_w2'][0], a['a_a2'][0]], axis=0),
        'g2': a['a_g2'][0],
        'gkw2': a['b_gk_w2'][0],
        'lnrows': np.stack([a['ln_in_g'], a['ln_in_b'], a['ln1_g'][0], a['ln1_b'][0], a['ln2_g'][0], a['ln2_b'][0]]),
        'w_out': a['w_out'][0].reshape(ND, P, ND, P).transpose(2, 1, 0, 3),
        'wq': a['p_wq'][0].reshape(ND, P, 2 * PH, P).transpose(2, 1, 0, 3),
        'keys': a['p_keys'][0].reshape(2 * PH, NKEY, P).transpose(2, 0, 1),
        'u': a['p_u'][0],
        'v': a['p_v'][0],
    }
    nc = bacc.Bacc("TRN2", target_bir_lowering=False, num_devices=1)
    ins, args = {}, []
    for name in _INS:
        arr = np.ascontiguousarray(arrays[name])
        ins[f"in_{name}_dram"] = arr
        args.append(nc.dram_tensor(f"in_{name}_dram", arr.shape, mybir.dt.from_np(arr.dtype), kind="ExternalInput").ap())
    out = nc.dram_tensor("out_0_dram", (T, D), F32, kind="ExternalOutput").ap()
    hybrid_layer(nc, *args, out)
    r = run_bass_kernel_spmd(nc, [ins], core_ids=[0])
    return r.results[0]["out_0_dram"].reshape(1, T, D)
```
